# Optimizing a Trainium2 kernel written in Bass

```python
import jax, jax.numpy as jnp
from jax import lax
import numpy as np

D_MODEL = 1024
BATCH = 1
SEQ = 512
DEPTH = 1

EPS = 1e-6
SSM_EXPAND = 2
D_INNER = SSM_EXPAND * D_MODEL
SSM_HEAD_DIM = 64
N_SSM_HEADS = D_INNER // SSM_HEAD_DIM
N_SSM_GROUPS = 4
D_STATE = 128
SSM_CONV = 4
SSM_CHUNK = 128
CONV_DIM = D_INNER + 2 * N_SSM_GROUPS * D_STATE
D_SC = D_MODEL
SC_CONV = 3
N_ATT_HEADS = 16
ATT_HEAD_DIM = 64
ATT_V_DIM = 64
Q_LORA = 384
KV_LORA = 256
N_IDX_HEADS = 8
D_IDX = 64
TOPK_MAX = 256
Q_BLOCK = 128
ATT_SCALE = ATT_HEAD_DIM ** -0.5
IDX_SCALE = (N_IDX_HEADS * D_IDX) ** -0.5
N_EXPERT_GROUPS = 4
EXPERTS_PER_GROUP = 4
N_EXPERTS = N_EXPERT_GROUPS * EXPERTS_PER_GROUP
D_EXPERT = 512
TOP_K_EXPERTS = 2
SPLIT_SIZES = (D_INNER, CONV_DIM, N_SSM_HEADS,
               D_SC, D_SC, D_SC,
               Q_LORA, KV_LORA, D_IDX, N_IDX_HEADS,
               D_MODEL, D_MODEL, D_MODEL)
SPLIT_POINTS = tuple(int(v) for v in np.cumsum(SPLIT_SIZES)[:-1])
N_IN = int(sum(SPLIT_SIZES))

kernel_name = "hybrid_ssd_shortconv_dsa_hmoe"

F32 = jnp.float32

def rms_norm(x, g):
    xf = x.astype(F32)
    y = xf * lax.rsqrt(jnp.mean(xf * xf, axis=-1, keepdims=True) + EPS)
    return (y * g.astype(F32)).astype(x.dtype)

def causal_depthwise_conv(x, w):
    width, c = w.shape
    return lax.conv_general_dilated(
        x, w[:, None, :].astype(x.dtype), window_strides=(1,), padding=[(width - 1, 0)],
        dimension_numbers=("NWC", "WIO", "NWC"), feature_group_count=c)

def ssd_chunked(xh, dt, a, bm, cm):
    b, s, h, p = xh.shape
    g, n = bm.shape[2], bm.shape[3]
    r = h // g
    nc = s // SSM_CHUNK
    q = SSM_CHUNK
    xdt = (xh * dt[..., None]).reshape(b, nc, q, g, r, p)
    da = (dt * a).reshape(b, nc, q, g, r)
    bc = bm.reshape(b, nc, q, g, n)
    cc = cm.reshape(b, nc, q, g, n)
    da_cs = jnp.cumsum(da, axis=2)
    causal = jnp.tril(jnp.ones((q, q), dtype=bool))[:, :, None, None]
    seg = da_cs[:, :, :, None] - da_cs[:, :, None, :]
    decay = jnp.exp(jnp.where(causal, seg, -jnp.inf))
    cb = jnp.einsum("bclgn,bcsgn->bclsg", cc, bc)
    y_diag = jnp.einsum("bclsgr,bcsgrp->bclgrp", cb[..., None] * decay, xdt)
    decay_to_end = jnp.exp(da_cs[:, :, -1:] - da_cs)
    chunk_states = jnp.einsum("bclgn,bclgrp->bcgrpn", bc, xdt * decay_to_end[..., None])
    chunk_decay = jnp.exp(da_cs[:, :, -1])

    def carry_state(state, inp):
        new_c, dec_c = inp
        return dec_c[..., None, None] * state + new_c, state

    init = jnp.zeros((b, g, r, p, n), F32)
    _, entering = lax.scan(carry_state, init,
                           (jnp.moveaxis(chunk_states, 1, 0), jnp.moveaxis(chunk_decay, 1, 0)))
    entering = jnp.moveaxis(entering, 0, 1)
    y_off = jnp.einsum("bclgn,bcgrpn->bclgrp", cc, entering) * jnp.exp(da_cs)[..., None]
    return (y_diag + y_off).reshape(b, s, h, p)

def ssd_branch(z, xbc, dt_raw, conv_w, conv_b, dt_bias, a_log, d_skip, norm_g, w_out):
    b, s, _ = z.shape
    xbc = jax.nn.silu(causal_depthwise_conv(xbc, conv_w) + conv_b.astype(xbc.dtype))
    xs, bm, cm = jnp.split(xbc, [D_INNER, D_INNER + N_SSM_GROUPS * D_STATE], axis=-1)
    xh = xs.reshape(b, s, N_SSM_HEADS, SSM_HEAD_DIM).astype(F32)
    dt = jax.nn.softplus(dt_raw.astype(F32) + dt_bias.astype(F32))
    a = -jnp.exp(a_log.astype(F32))
    y = ssd_chunked(xh, dt, a,
                    bm.reshape(b, s, N_SSM_GROUPS, D_STATE).astype(F32),
                    cm.reshape(b, s, N_SSM_GROUPS, D_STATE).astype(F32))
    y = (y + d_skip.astype(F32)[:, None] * xh).reshape(b, s, D_INNER)
    yg = (y * jax.nn.silu(z.astype(F32))).reshape(b, s, N_SSM_GROUPS, D_INNER // N_SSM_GROUPS)
    yg = yg * lax.rsqrt(jnp.mean(yg * yg, axis=-1, keepdims=True) + EPS)
    yg = (yg.reshape(b, s, D_INNER) * norm_g.astype(F32)).astype(z.dtype)
    return yg @ w_out

def short_conv_branch(gate_b, gate_c, xin, conv_w, w_out):
    v = causal_depthwise_conv(gate_c * xin, conv_w)
    return (gate_b * v) @ w_out

def dsa_branch(c_q, c_kv, k_idx, w_idx, q_norm_g, kv_norm_g, k_norm_g,
               w_uq, w_qidx, w_uk, w_uv, w_out):
    b, s, _ = c_q.shape
    topk = min(TOPK_MAX, s // 4)
    c_q = rms_norm(c_q, q_norm_g)
    c_kv = rms_norm(c_kv, kv_norm_g)
    k_idx = rms_norm(k_idx, k_norm_g)
    key_pos = jnp.arange(s)

    def attend_block(blk):
        q0 = blk * Q_BLOCK
        cq = lax.dynamic_slice_in_dim(c_q, q0, Q_BLOCK, axis=1)
        wh = lax.dynamic_slice_in_dim(w_idx, q0, Q_BLOCK, axis=1).astype(F32) * IDX_SCALE
        q_pos = q0 + jnp.arange(Q_BLOCK)
        visible = key_pos[None, :] <= q_pos[:, None]
        qi = jnp.einsum("bqc,chd->bqhd", cq, w_qidx)
        dots = jnp.einsum("bqhd,bsd->bqhs", qi, k_idx).astype(F32)
        score = jnp.einsum("bqhs,bqh->bqs", jax.nn.relu(dots), wh)
        score = jnp.where(visible[None], score, -jnp.inf)
        _, sel = lax.top_k(score, topk)
        valid = sel <= q_pos[None, :, None]
        kv = jax.vmap(lambda lat, idx: lat[idx])(c_kv, sel)
        q = jnp.einsum("bqc,chd->bqhd", cq, w_uq)
        q_lat = jnp.einsum("bqhd,hdr->bqhr", q, w_uk)
        logits = jnp.einsum("bqhr,bqkr->bqhk", q_lat, kv).astype(F32) * ATT_SCALE
        logits = jnp.where(valid[:, :, None, :], logits, -jnp.inf)
        probs = jax.nn.softmax(logits, axis=-1).astype(kv.dtype)
        o_lat = jnp.einsum("bqhk,bqkr->bqhr", probs, kv)
        o = jnp.einsum("bqhr,hrv->bqhv", o_lat, w_uv)
        return o.reshape(b, Q_BLOCK, N_ATT_HEADS * ATT_V_DIM)

    out = lax.map(attend_block, jnp.arange(s // Q_BLOCK))
    out = jnp.moveaxis(out, 0, 1).reshape(b, s, N_ATT_HEADS * ATT_V_DIM)
    return out @ w_out

def hybrid_mixer(h, w_in, ssm_conv_w, ssm_conv_b, ssm_dt_bias, ssm_a_log, ssm_d, ssm_norm_g, ssm_w_out,
                 sc_conv_w, sc_w_out, att_q_norm_g, att_kv_norm_g, idx_k_norm_g, att_w_uq, idx_w_q,
                 att_w_uk, att_w_uv, att_w_out, mix_w_out):
    (z, xbc, dt_raw, sc_b, sc_c, sc_x, c_q, c_kv, k_idx, w_idx,
     g_a, g_b, g_c) = jnp.split(h @ w_in, SPLIT_POINTS, axis=-1)
    y_a = ssd_branch(z, xbc, dt_raw, ssm_conv_w, ssm_conv_b, ssm_dt_bias, ssm_a_log, ssm_d,
                     ssm_norm_g, ssm_w_out)
    y_b = short_conv_branch(sc_b, sc_c, sc_x, sc_conv_w, sc_w_out)
    y_c = dsa_branch(c_q, c_kv, k_idx, w_idx, att_q_norm_g, att_kv_norm_g, idx_k_norm_g,
                     att_w_uq, idx_w_q, att_w_uk, att_w_uv, att_w_out)
    merged = jax.nn.sigmoid(g_a) * y_a + jax.nn.sigmoid(g_b) * y_b + jax.nn.sigmoid(g_c) * y_c
    return merged @ mix_w_out

def hier_moe(h, w_group, b_group, w_expert, b_expert, w_gate, w_up, w_down):
    b, s, _ = h.shape
    group_probs = jax.nn.softmax((h @ w_group + b_group).astype(F32), axis=-1)
    p_group, g_sel = lax.top_k(group_probs, 1)
    exp_logits = (h @ w_expert + b_expert).astype(F32).reshape(b, s, N_EXPERT_GROUPS, EXPERTS_PER_GROUP)
    in_group = jnp.take_along_axis(exp_logits, g_sel[..., None], axis=2)[:, :, 0]
    p_in, e_sel = lax.top_k(jax.nn.softmax(in_group, axis=-1), TOP_K_EXPERTS)
    p_in = p_in / jnp.sum(p_in, axis=-1, keepdims=True)
    gate = p_group * p_in
    expert_id = g_sel * EXPERTS_PER_GROUP + e_sel
    combine = jnp.einsum("bsk,bske->bse", gate,
                         jax.nn.one_hot(expert_id, N_EXPERTS, dtype=F32)).astype(h.dtype)
    out = jnp.zeros_like(h)
    for e in range(N_EXPERTS):
        hid = jax.nn.silu(h @ w_gate[e]) * (h @ w_up[e])
        out = out + combine[..., e:e + 1] * (hid @ w_down[e])
    return out

def setup_inputs(seed: int = 0) -> dict:
    key = jax.random.key(seed)
    ks = jax.random.split(key, 30)

    def nrm(k, shape, scale):
        return jax.random.normal(k, shape, F32) * scale

    def gain(k, shape):
        return 1.0 + 0.05 * jax.random.normal(k, shape, F32)

    L = DEPTH
    dt0 = jnp.exp(jax.random.uniform(ks[5], (L, N_SSM_HEADS), F32) * (np.log(0.1) - np.log(0.001))
                  + np.log(0.001))
    return {
        "x": nrm(ks[0], (BATCH, SEQ, D_MODEL), 1.0),
        "norm1_g": gain(ks[1], (L, D_MODEL)),
        "w_in": nrm(ks[2], (L, D_MODEL, N_IN), D_MODEL ** -0.5),
        "ssm_conv_w": nrm(ks[3], (L, SSM_CONV, CONV_DIM), SSM_CONV ** -0.5),
        "ssm_conv_b": nrm(ks[4], (L, CONV_DIM), 0.02),
        "ssm_dt_bias": dt0 + jnp.log(-jnp.expm1(-dt0)),
        "ssm_a_log": jnp.log(jax.random.uniform(ks[6], (L, N_SSM_HEADS), F32, 1.0, 16.0)),
        "ssm_d": gain(ks[7], (L, N_SSM_HEADS)),
        "ssm_norm_g": gain(ks[8], (L, D_INNER)),
        "ssm_w_out": nrm(ks[9], (L, D_INNER, D_MODEL), D_INNER ** -0.5),
        "sc_conv_w": nrm(ks[10], (L, SC_CONV, D_SC), SC_CONV ** -0.5),
        "sc_w_out": nrm(ks[11], (L, D_SC, D_MODEL), D_SC ** -0.5),
        "att_q_norm_g": gain(ks[12], (L, Q_LORA)),
        "att_kv_norm_g": gain(ks[13], (L, KV_LORA)),
        "idx_k_norm_g": gain(ks[14], (L, D_IDX)),
        "att_w_uq": nrm(ks[15], (L, Q_LORA, N_ATT_HEADS, ATT_HEAD_DIM), Q_LORA ** -0.5),
        "idx_w_q": nrm(ks[16], (L, Q_LORA, N_IDX_HEADS, D_IDX), Q_LORA ** -0.5),
        "att_w_uk": nrm(ks[17], (L, N_ATT_HEADS, ATT_HEAD_DIM, KV_LORA), KV_LORA ** -0.5),
        "att_w_uv": nrm(ks[18], (L, N_ATT_HEADS, KV_LORA, ATT_V_DIM), KV_LORA ** -0.5),
        "att_w_out": nrm(ks[19], (L, N_ATT_HEADS * ATT_V_DIM, D_MODEL), (N_ATT_HEADS * ATT_V_DIM) ** -0.5),
        "mix_w_out": nrm(ks[20], (L, D_MODEL, D_MODEL), D_MODEL ** -0.5),
        "norm2_g": gain(ks[21], (L, D_MODEL)),
        "moe_w_group": nrm(ks[22], (L, D_MODEL, N_EXPERT_GROUPS), D_MODEL ** -0.5),
        "moe_b_group": nrm(ks[23], (L, N_EXPERT_GROUPS), 0.01),
        "moe_w_expert": nrm(ks[24], (L, D_MODEL, N_EXPERTS), D_MODEL ** -0.5),
        "moe_b_expert": nrm(ks[25], (L, N_EXPERTS), 0.01),
        "moe_w_gate": nrm(ks[26], (L, N_EXPERTS, D_MODEL, D_EXPERT), D_MODEL ** -0.5),
        "moe_w_up": nrm(ks[27], (L, N_EXPERTS, D_MODEL, D_EXPERT), D_MODEL ** -0.5),
        "moe_w_down": nrm(ks[28], (L, N_EXPERTS, D_EXPERT, D_MODEL), D_EXPERT ** -0.5),
        "final_norm_g": gain(ks[29], (D_MODEL,)),
    }

def reference(x, norm1_g, w_in, ssm_conv_w, ssm_conv_b, ssm_dt_bias, ssm_a_log, ssm_d, ssm_norm_g,
              ssm_w_out, sc_conv_w, sc_w_out, att_q_norm_g, att_kv_norm_g, idx_k_norm_g, att_w_uq,
              idx_w_q, att_w_uk, att_w_uv, att_w_out, mix_w_out, norm2_g, moe_w_group, moe_b_group,
              moe_w_expert, moe_b_expert, moe_w_gate, moe_w_up, moe_w_down, final_norm_g):
    for layer in range(DEPTH):
        h = rms_norm(x, norm1_g[layer])
        x = x + hybrid_mixer(h, w_in[layer], ssm_conv_w[layer], ssm_conv_b[layer], ssm_dt_bias[layer],
                             ssm_a_log[layer], ssm_d[layer], ssm_norm_g[layer], ssm_w_out[layer],
                             sc_conv_w[layer], sc_w_out[layer], att_q_norm_g[layer], att_kv_norm_g[layer],
                             idx_k_norm_g[layer], att_w_uq[layer], idx_w_q[layer], att_w_uk[layer],
                             att_w_uv[layer], att_w_out[layer], mix_w_out[layer])
        h = rms_norm(x, norm2_g[layer])
        x = x + hier_moe(h, moe_w_group[layer], moe_b_group[layer], moe_w_expert[layer],
                         moe_b_expert[layer], moe_w_gate[layer], moe_w_up[layer], moe_w_down[layer])
    return rms_norm(x, final_norm_g)


_drawn_inputs = setup_inputs


def setup_inputs(seed=0):
    import zlib

    import numpy as np

    out = dict(_drawn_inputs(seed))
    spreads = {}
    factors = {'ssm_conv_b': 8.316,
     'att_q_norm_g': 3.614,
     'att_kv_norm_g': 4.453,
     'idx_k_norm_g': 3.663,
     'moe_b_group': 23.921,
     'moe_b_expert': 25.271,
     'ssm_d': 7.168,
     'ssm_norm_g': 4.416,
     'norm2_g': 2.739}
    for name, (base, spread) in spreads.items():
        noise = np.random.default_rng([zlib.crc32(name.encode()), seed]).standard_normal(out[name].shape)
        drawn = base * np.exp(spread * noise) if base else spread * noise
        out[name] = __import__('jax').numpy.asarray(drawn.astype(out[name].dtype))
    for name, factor in factors.items():
        out[name] = (out[name] * factor).astype(out[name].dtype)
    return out
```

```python
from contextlib import ExitStack

import numpy as np

import concourse.bass as bass
from concourse import mybir

F32 = mybir.dt.float32
ALU = mybir.AluOpType
ACT = mybir.ActivationFunctionType
AX_X = mybir.AxisListType.X

P = 128
D = 1024
S = 512
KT = D // P
TT = S // P
EPS = 1e-6
D_INNER = 2048
SSM_HEADS = 32
HEAD = 64
GROUPS = 4
GH = SSM_HEADS // GROUPS
TAPS = 4
SC_TAPS = 3
Q_LORA = 384
QT = Q_LORA // P
KV_LORA = 256
RT = KV_LORA // P
D_IDX = 64
IDX_HEADS = 8
KVC = KV_LORA + D_IDX + IDX_HEADS
IDX_SCALE = (IDX_HEADS * D_IDX) ** -0.5
ATT_SCALE = 64 ** -0.5
HQ = 4
TOPK = 128
BIG = 1e30
UNSEEN = -1e38
TAKEN = -3e38
EXPERTS = 16
EG = 4
F_EXP = 512
FT = F_EXP // P

C_G1 = 0
C_QG = C_G1 + KT
C_KG = C_QG + QT
C_SC = C_KG + 1
C_CONV = C_SC + KT * SC_TAPS
C_NG = C_CONV + GROUPS * 6 * (TAPS + 1)
C_G2 = C_NG + D_INNER // P
NCOL = C_G2 + KT
R_KVG = 0
R_DTB = R_KVG + KV_LORA
R_ALOG = R_DTB + SSM_HEADS
R_D = R_ALOG + SSM_HEADS
R_RB = R_D + SSM_HEADS
NROW = R_RB + EG + EXPERTS


class Marks:

    def __init__(self, eng, sem):
        self.eng, self.sem, self.n, self.base = eng, sem, 0, 0

    def mark(self, ins):
        ins.then_inc(self.sem, 1)
        self.n += 1

    def settle(self):
        self.eng.wait_ge(self.sem, self.base + self.n)

    def loop(self, i, per):
        self.before, self.per = self.n, per
        self.base, self.n = i * per + self.n, 0

    def end(self, reps):
        assert self.n == self.per, (self.n, self.per)
        self.base, self.n = 0, self.before + reps * self.per


def build(nc, t, debug=None):
    with ExitStack() as ctx:
        def sb(name, shape):
            return ctx.enter_context(nc.sbuf_tensor(name, shape, F32))

        sems = {}

        def sem(name):
            if name not in sems:
                sems[name] = ctx.enter_context(nc.semaphore(name))
            return sems[name]

        hT = sb("hT", [P, KT, S])
        gatedT = sb("gatedT", [P, KT, S])
        oT = sb("oT", [P, KT, S])
        WA = sb("WA", [P, 4096])
        WB = sb("WB", [P, 4096])
        WC = sb("WC", [P, 4096])
        WD = sb("WD", [P, 4096])
        arena = sb("arena", [P, 21504])
        cols = sb("cols", [P, NCOL])
        rows = sb("rows", [P, NROW])
        ident = sb("ident", [P, P])
        tri_le = sb("tri_le", [P, P])
        tri_gt = sb("tri_gt", [P, P])
        ones = sb("ones", [P, P])
        small = sb("small", [P, 256])
        dt_sb = sb("dt_sb", [P, TT, SSM_HEADS])
        da_sb = sb("da_sb", [P, TT, SSM_HEADS])
        ex_sb = sb("ex_sb", [P, 3, TT, SSM_HEADS])
        psum = [ctx.enter_context(nc.psum_tensor(f"bank{b}", [P, 512], F32)) for b in range(8)]

        def part(at, *shape):
            n = int(np.prod(shape))
            ap = arena[:, at:at + n]
            if len(shape) == 2:
                ap = ap.rearrange("p (a b) -> p a b", a=shape[0])
            if len(shape) == 3:
                ap = ap.rearrange("p (a b c) -> p a b c", a=shape[0], b=shape[1])
            return ap, at + n

        cqT, at = part(0, QT, S)
        kvn, at = part(at, TT, KV_LORA)
        kvnT, at = part(at, RT, S)
        kidxT, at = part(at, S)
        bias, at_att = part(at, P * (1 + 2 + 3 + 4))
        BIAS_AT = [0, P, 3 * P, 6 * P]
        x_sb, at = part(at_att, TT, D)
        kvraw, at = part(at, TT, KVC)
        qraw, at = part(at, TT, Q_LORA)
        kdup, at = part(at, TT, 2 * D_IDX)
        qiT, at = part(at, 4, S)
        relu, at = part(at, 2, S)
        sc_u, at = part(at, S + SC_TAPS - 1)
        sc_v, at = part(at, S)
        sc_w, at = part(at, S)
        assert at <= 21504
        qlatT, at = part(at_att, HQ * RT, S)
        probs, at = part(at, 4, S)
        PT, at = part(at, 2, TT, HQ * P)
        assert at <= 21504
        qT = WD[:, 0:1024].rearrange("p (j s) -> p j s", j=2)
        olT = WD[:, 1024:2048].rearrange("p (j s) -> p j s", j=2)
        w_uq = WC[:, 0:768].rearrange("p (k n) -> p k n", k=QT)
        w_uk = WC[:, 768:1280].rearrange("p (j n) -> p j n", j=2)
        w_uv = WC[:, 1280:1792].rearrange("p (h r v) -> p h r v", h=HQ, r=RT)
        ynT, at_local = part(0, D_INNER // P, S)
        xsT, at = part(at_local, 6, S)
        conv, at = part(at, 2, S)
        xdt, at = part(at, TT, S)
        xend, at = part(at, 2, S)
        y, at = part(at, TT, S)
        decay, at = part(at, 2, 4, P)
        da_tri, at = part(at, 2, 4, P)
        mix_m, at = part(at, 4, 4, P)
        assert at <= 21504
        sz = WD[:, 0:2048].rearrange("p (c n) -> p c n", c=TT)
        state = WD[:, 2048:2560]
        tmp = WD[:, 2560:3072]
        b_tok = WD[:, 3072:3584]
        cb = WD[:, 3584:4096].rearrange("p (c l) -> p c l", c=TT)
        w_ssm_x = WA[:].rearrange("p (k n) -> p k n", k=KT)
        w_ssm_bc = WB[:, 0:2048].rearrange("p (k n) -> p k n", k=KT)
        w_z = WC[:].rearrange("p (k n) -> p k n", k=KT)
        mergedT, at = part(at_local, KT, S)
        sig, at = part(at, 3, S)
        branch, at = part(at, 2, S)
        x2, at_moe = part(at, TT, D)
        w_merge = WA[:].rearrange("p (k n) -> p k n", k=32)
        w_gates = WB[:, 0:3072].rearrange("p (k j n) -> p k j n", k=KT, j=3)
        w_mix = [w[:].rearrange("p (k n) -> p k n", k=KT) for w in (WC, WD)]
        h2, at = part(0, TT, D)
        h2T = hT
        hidT, at = part(at, FT, S)
        sg, at = part(at, 2, S)
        assert at <= at_local
        w_router = WD[:, 0:KT * (EG + EXPERTS)].rearrange("p (k n) -> p k n", k=KT)
        final_g = WD[:, 1024:1024 + D]
        w_gate = WA[:].rearrange("p (k n) -> p k n", k=KT)
        w_up = WB[:].rearrange("p (k n) -> p k n", k=KT)
        w_down = WC[:].rearrange("p (k n) -> p k n", k=FT)
        NR = EG + EXPERTS
        rt = at_moe
        logits, rt = part(rt, TT, NR)
        rsc, rt = part(rt, 24, TT * EXPERTS)
        assert rt <= 21504

        sc_in = oT[:].rearrange("p k s -> p (k s)")[:, 0:6 * S].rearrange("p (a b c) -> p a b c", a=2, b=3)
        sq = WD[:, 3072:4096]

        wa_kv = WA[:, 0:KT * KVC].rearrange("p (k n) -> p k n", k=KT)
        wb_q = WB[:, 0:KT * Q_LORA].rearrange("p (k n) -> p k n", k=KT)
        wc_dt = WC[:, 0:KT * SSM_HEADS].rearrange("p (k n) -> p k n", k=KT)
        wd_idx = WD[:, 0:QT * 512].rearrange("p (k n) -> p k n", k=QT)
        w_sc = [w[:, 0:KT * 3 * P].rearrange("p (k j n) -> p k j n", k=KT, j=3) for w in (WA, WB)]

        ms = small[:, 0:4]
        rstd = small[:, 4:8]
        ms2 = small[:, 8:20]
        rstd2 = small[:, 20:32]
        m8 = small[:, 32:40]
        widx = small[:, 40:72].rearrange("p (t h) -> p t h", t=TT)
        powm = small[:, 72:84]
        pmax = small[:, 84:88]
        nmax = small[:, 88:92]
        psums = small[:, 92:96]
        pinv = small[:, 96:100]
        m16 = small[:, 100:104]
        r16 = small[:, 104:108]
        waited = small[:, 108:109]

        block = ctx.enter_context(nc.Block())

        @block.sync
        def _(sp):
            sp.dma_start(x_sb, t["x"].rearrange("t p d -> p t d")).then_inc(sem("x_loaded"), 16)
            sp.dma_start(cols[:], t["cols"]).then_inc(sem("params_loaded"), 16)
            sp.dma_start(rows[:], t["rows"].broadcast_to([P, NROW])).then_inc(sem("params_loaded"), 16)
            sp.dma_start(WA[:, 0:KT * KVC], t["w_kv"]).then_inc(sem("w_kv_loaded"), 16)
            sp.dma_start(WB[:, 0:KT * Q_LORA], t["w_q"]).then_inc(sem("w_q_loaded"), 16)
            sp.dma_start(WC[:, 0:KT * SSM_HEADS], t["w_dt"]).then_inc(sem("w_dt_loaded"), 16)
            sp.dma_start(WD[:, 0:QT * 512], t["w_idx"]).then_inc(sem("w_idx_loaded"), 16)
            for u in range(2):
                sp.wait_ge(sem("kq_projected"), TT * (u + 1))
                sp.dma_start([WA, WB][u][:, 0:KT * 3 * P], t["w_sc"][u]).then_inc(sem(f"w_sc{u}_loaded"), 16)
            with sp.Fori(1, KT // 2) as i:
                for u in range(2):
                    sp.wait_ge(sem("sc_projected"), i * 6 - 6 + 3 * (u + 1))
                    sp.dma_start([WA, WB][u][:, 0:KT * 3 * P], t["w_sc"][2 * i + u]).then_inc(sem(f"w_sc{u}_loaded"), 16)
            def load_heads(hg, first=False):
                if not first:
                    sp.wait_ge(sem("head_done"), hg * 14 - 4)
                sp.dma_start(WC[:, 0:1280], t["w_qk"][hg]).then_inc(sem("w_qk_loaded"), 16)
                if not first:
                    sp.wait_ge(sem("head_done"), hg * 14)
                sp.dma_start(WC[:, 1280:1792], t["w_uv"][hg]).then_inc(sem("w_uv_loaded"), 16)
            sp.wait_ge(sem("kq_projected"), 3 * TT)
            load_heads(0, first=True)
            with sp.Fori(1, TT) as hg:
                load_heads(hg)
            def load_group(g, first=False):
                if not first:
                    sp.wait_ge(sem("conv_in"), g * 6 - 2)
                sp.dma_start(WA[:], t["w_ssm_x"][g]).then_inc(sem("w_ssm_x_loaded"), 16)
                if not first:
                    sp.wait_ge(sem("conv_in"), g * 6)
                sp.dma_start(WB[:, 0:2048], t["w_ssm_bc"][g]).then_inc(sem("w_ssm_bc_loaded"), 16)
                if first:
                    sp.wait_ge(sem("head_done"), 14 * TT)
                else:
                    sp.wait_ge(sem("pair_done"), g * 12 - 8)
                sp.dma_start(WC[:], t["w_z"][g]).then_inc(sem("w_z_loaded"), 16)
            sp.wait_ge(sem("sc_projected"), 3 * KT)
            load_group(0, first=True)
            with sp.Fori(1, GROUPS) as g:
                load_group(g)
            sp.wait_ge(sem("conv_in"), 6 * GROUPS)
            sp.dma_start(WA[:], t["w_merge"][0]).then_inc(sem("w_merge_loaded"), 16)
            sp.dma_start(WB[:, 0:3072], t["w_gates"][0]).then_inc(sem("w_gates_loaded"), 16)
            sp.wait_ge(sem("pair_done"), 12 * GROUPS - 8)
            sp.dma_start(WC[:], t["w_mix"][0]).then_inc(sem("w_mix_loaded"), 16)
            sp.wait_ge(sem("y_taken"), 4 * GROUPS + 4)
            sp.dma_start(WD[:], t["w_mix"][1]).then_inc(sem("w_mix_loaded"), 16)
            sp.dma_start(x2, t["x"].rearrange("t p d -> p t d")).then_inc(sem("x2_loaded"), 16)
            with sp.Fori(1, KT) as n:
                sp.wait_ge(sem("branch_done"), n * 3)
                sp.dma_start(WA[:], t["w_merge"][n]).then_inc(sem("w_merge_loaded"), 16)
                sp.wait_ge(sem("gate_done"), n * 3)
                sp.dma_start(WB[:, 0:3072], t["w_gates"][n]).then_inc(sem("w_gates_loaded"), 16)
            sp.wait_ge(sem("branch_done"), KT * 3)
            sp.dma_start(WA[:], t["w_gate"][0]).then_inc(sem("w_gate_loaded"), 16)
            sp.wait_ge(sem("gate_done"), KT * 3)
            sp.dma_start(WB[:], t["w_up"][0]).then_inc(sem("w_up_loaded"), 16)
            sp.wait_ge(sem("mix_done"), 8)
            sp.dma_start(WC[:], t["w_down"][0]).then_inc(sem("w_down_loaded"), 16)
            sp.dma_start(WD[:, 0:KT * (EG + EXPERTS)], t["w_router"]).then_inc(sem("w_router_loaded"), 16)
            sp.dma_start(WD[:, 1024:1024 + D], t["final_g"].broadcast_to([P, D])).then_inc(sem("final_g_loaded"), 16)
            with sp.Fori(1, EXPERTS) as e:
                sp.wait_ge(sem("gate_up_done"), e * 8 - 1)
                sp.dma_start(WA[:], t["w_gate"][e]).then_inc(sem("w_gate_loaded"), 16)
                sp.wait_ge(sem("gate_up_done"), e * 8)
                sp.dma_start(WB[:], t["w_up"][e]).then_inc(sem("w_up_loaded"), 16)
                sp.wait_ge(sem("down_done"), e * 8)
                sp.dma_start(WC[:], t["w_down"][e]).then_inc(sem("w_down_loaded"), 16)
            for c in range(TT):
                sp.wait_ge(sem("out_ready"), c + 1)
                sp.dma_start(t["out"][c], x2[:, c, :]).then_inc(sem("out_stored"), 16)
            sp.wait_ge(sem("out_stored"), 16 * TT)
            if debug:
                debug(sp, sem, dict(oT=oT, ynT=ynT, x2=x2, hT=hT, cqT=cqT, kvn=kvn, kvnT=kvnT, kidxT=kidxT, bias=bias, gatedT=gatedT, dt_sb=dt_sb, ex_sb=ex_sb))

        @block.gpsimd
        def _(pool):
            def tri(ap, op, base, mult, step):
                pool.affine_select(out=ap, in_=ones[:], compare_op=op, fill=0.0, base=base,
                                   pattern=[[step, P]], channel_multiplier=mult).then_inc(sem("consts_ready"), 1)
            pool.memset(ones[:], 1.0).then_inc(sem("ones_ready"), 1)
            pool.memset(powm, -0.5).then_inc(sem("ones_ready"), 1)
            pool.memset(sc_u, 0.0).then_inc(sem("ones_ready"), 1)
            pool.wait_ge(sem("ones_ready"), 3)
            tri(ident[:], ALU.is_equal, 0, 1, -1)
            tri(tri_le[:], ALU.is_ge, 0, -1, 1)
            tri(tri_gt[:], ALU.is_gt, 0, 1, -1)
            pool.memset(bias[:, 0:P], 0.0).then_inc(sem("bias_zero"), 1)
            pool.wait_ge(sem("bias_zero"), 1)
            pool.affine_select(out=bias[:, 0:P], in_=bias[:, 0:P], compare_op=ALU.is_ge, fill=-BIG, base=0,
                               pattern=[[-1, P]], channel_multiplier=1).then_inc(sem("consts_ready"), 1)
            pool.wait_ge(sem("ms_ready"), 1)
            pool.tensor_tensor(rstd, ms, powm[:, 0:4], ALU.pow).then_inc(sem("rstd_ready"), 1)
            pool.wait_ge(sem("ms2_ready"), 1)
            pool.tensor_tensor(rstd2, ms2, powm[:, 0:12], ALU.pow).then_inc(sem("rstd2_ready"), 1)
            for b in range(1, TT):
                pool.wait_ge(sem("score_ready"), b)
                dg = bias[:, BIAS_AT[b] + b * P:BIAS_AT[b] + (b + 1) * P]
                pool.affine_select(out=dg, in_=dg, compare_op=ALU.is_ge, fill=UNSEEN, base=0,
                                   pattern=[[-1, P]], channel_multiplier=1).then_inc(sem("score_hidden"), 1)
            own = Marks(pool, sem("pool_sc"))
            for u in range(2):
                pool.sem_inc(sem(f"sc_gated{u}"), 1)
            with pool.Fori(0, KT // 2) as i:
                own.loop(i, 2 * 7)
                for u in range(2):
                    b, c, x = (sc_in[:, u, j, :] for j in range(3))
                    w = [cols[:, bass.ds(C_SC + (2 * i + u) * SC_TAPS + k, 1)].to_broadcast([P, S]) for k in range(SC_TAPS)]
                    pool.wait_ge(sem(f"sc_in{u}"), i * 3 + 6)
                    own.mark(pool.tensor_tensor(sc_u[:, SC_TAPS - 1:], c, x, ALU.mult))
                    own.settle()
                    own.mark(pool.tensor_tensor(sc_v, sc_u[:, 2:2 + S], w[2], ALU.mult))
                    own.mark(pool.tensor_tensor(sc_w, sc_u[:, 1:1 + S], w[1], ALU.mult))
                    own.settle()
                    own.mark(pool.tensor_tensor(sc_v, sc_v, sc_w, ALU.add))
                    own.settle()
                    own.mark(pool.tensor_tensor(sc_w, sc_u[:, 0:S], w[0], ALU.mult))
                    own.settle()
                    own.mark(pool.tensor_tensor(sc_v, sc_v, sc_w, ALU.add))
                    own.settle()
                    own.mark(pool.tensor_tensor(sc_w, sc_v, b, ALU.mult))
                    own.settle()
                    pool.tensor_copy(gatedT[:, 2 * i + u, :], sc_w).then_inc(sem(f"sc_gated{u}"), 1)
                own.end(KT // 2)
            with pool.Fori(0, GROUPS) as g:
                def triangle(k):
                    pool.wait_ge(sem("pair_done"), g * 12 + k + 3)
                    da = da_sb[:, k // 2, bass.ds(g * GH + 4 * (k % 2), 4)].unsqueeze(2).to_broadcast([P, 4, P])
                    tri = tri_le[:].unsqueeze(1).to_broadcast([P, 4, P])
                    pool.tensor_tensor(da_tri[:, k % 2], tri, da, ALU.mult).then_inc(sem("tri_ready"), 1)
                triangle(0)
                triangle(1)
                for c in range(TT):
                    if c < TT - 1:
                        pool.wait_ge(sem("xdt_ready"), g * TT + c + 1)
                        if c == 2:
                            pool.wait_ge(sem("state_done"), g * 3 + 1)
                        ex = ex_sb[:, 1, c, bass.ds(g * GH, GH)].unsqueeze(2).to_broadcast([P, GH, HEAD])
                        pool.tensor_tensor(heads(xend[:, c % 2]), heads(xdt[:, c]), ex, ALU.mult).then_inc(sem("xend_ready"), 1)
                        triangle(2 * c + 2)
                        triangle(2 * c + 3)
                pool.wait_ge(sem("yms_ready"), g + 1)
                pool.tensor_tensor(r16, m16, powm[:, 0:4], ALU.pow).then_inc(sem("yrstd_ready"), 1)
            pool.wait_ge(sem("ms3_ready"), 1)
            pool.tensor_tensor(rstd, ms, powm[:, 0:4], ALU.pow).then_inc(sem("rstd3_ready"), 1)
            pool.wait_ge(sem("ms4_ready"), 1)
            pool.tensor_tensor(rstd, ms, powm[:, 0:4], ALU.pow).then_inc(sem("rstd4_ready"), 1)

        @block.tensor
        def _(pe):
            pe.wait_ge(sem("consts_ready"), 3)
            for k in range(KT):
                if k == 0:
                    pe.wait_ge(sem("xn_ready"), TT)
                for c in range(TT):
                    ins = pe.transpose(psum[k][:, c * P:(c + 1) * P], x_sb[:, c, k * P:(k + 1) * P], ident[:])
                ins.then_inc(sem("x_turned"), 1)
            for n, (w, cn, ready) in enumerate((
                    (wa_kv, KVC, "w_kv_loaded"), (wb_q, Q_LORA, "w_q_loaded"), (wc_dt, SSM_HEADS, "w_dt_loaded"))):
                pe.wait_ge(sem(ready), 16)
                if n == 0:
                    pe.wait_ge(sem("hT_ready"), KT)
                for c in range(TT):
                    b = (n * TT + c) % 8
                    if n == 2:
                        pe.wait_ge(sem("kv_taken"), c + 1)
                    for k in range(KT):
                        ins = pe.matmul(psum[b][:, 0:cn], hT[:, k, c * P:(c + 1) * P], w[:, k, :],
                                        start=k == 0, stop=k == KT - 1)
                    ins.then_inc(sem("kq_projected"), 1)
            pe.wait_ge(sem("latents_scaled"), 3)
            pe.wait_ge(sem("q_taken"), TT)
            for j in range(QT + RT + 1):
                b = 4 + j % 4
                if j >= 4:
                    pe.wait_ge(sem("latents_taken"), j - 3)
                for c in range(TT):
                    src = (qraw[:, c, j * P:(j + 1) * P] if j < QT else
                           kvn[:, c, (j - QT) * P:(j - QT + 1) * P] if j < QT + RT else kdup[:, c, :])
                    ins = pe.transpose(psum[b][:, c * P:(c + 1) * P], src, ident[:])
                ins.then_inc(sem("latents_turned"), 1)
            pe.wait_ge(sem("da_ready"), 1)
            for c in range(TT):
                for j, m in enumerate((tri_le, tri_gt, ones)):
                    ins = pe.matmul(psum[0][:, (j * TT + c) * SSM_HEADS:(j * TT + c + 1) * SSM_HEADS], m[:], da_sb[:, c, :],
                                    start=True, stop=True)
            ins.then_inc(sem("sums_ready"), 1)
            pe.wait_ge(sem("w_idx_loaded"), 16)
            pe.wait_ge(sem("latents_taken"), QT + RT + 1)
            for j in range(IDX_HEADS // 2):
                for k in range(QT):
                    ins = pe.matmul(psum[4 + j][:], wd_idx[:, k, j * P:(j + 1) * P], cqT[:, k, :], start=k == 0, stop=k == QT - 1)
                ins.then_inc(sem("qi_projected"), 1)
            pe.wait_ge(sem("qi_ready"), IDX_HEADS // 2)
            n = 0
            for b in range(1, TT):
                for h in range(IDX_HEADS):
                    if n >= 2:
                        pe.wait_ge(sem("dots_taken"), n - 1)
                    half = slice(64 * (h % 2), 64 * (h % 2) + 64)
                    pe.matmul(psum[6 + n % 2][:, 0:(b + 1) * P], qiT[half, h // 2, b * P:(b + 1) * P],
                              kidxT[half, 0:(b + 1) * P], start=True, stop=True).then_inc(sem("dots_ready"), 1)
                    n += 1
            pe.wait_ge(sem("sums_taken"), 1)
            with pe.Fori(0, KT // 2) as i:
                for u in range(2):
                    pe.wait_ge(sem(f"w_sc{u}_loaded"), i * 16 + 16)
                    for j in range(3):
                        pe.wait_ge(sem(f"sc_in{u}"), i * 3 + j + 1)
                        for k in range(KT):
                            ins = pe.matmul(psum[3 * u + j][:], w_sc[u][:, k, j, :], hT[:, k, :], start=k == 0, stop=k == KT - 1)
                        ins.then_inc(sem("sc_projected"), 1)
            for u in range(2):
                pe.wait_ge(sem(f"sc_in{u}"), 3 + 3 * KT // 2)
            with pe.Fori(0, TT) as hg:
                def head(k):
                    pe.wait_ge(sem("head_taken"), hg * 14 + k + 1)
                    return psum[k % 2]

                def half(h):
                    return slice(64 * (h % 2), 64 * (h % 2) + 64)

                def score(s):
                    b, h = s // HQ, s % HQ
                    pe.wait_ge(sem("logits_taken"), hg * 16 + s + 1)
                    for r in range(RT):
                        ins = pe.matmul(psum[2 + s % 2][:, 0:(b + 1) * P], qlatT[:, h * RT + r, b * P:(b + 1) * P],
                                        kvnT[:, r, 0:(b + 1) * P], start=r == 0, stop=r == RT - 1)
                    ins.then_inc(sem("logits_done"), 1)

                def out_heads(b):
                    pe.wait_ge(sem("olat_taken"), hg * 8 + 2 * b + 4)
                    if b == 0:
                        pe.wait_ge(sem("w_uv_loaded"), hg * 16 + 16)
                    bank = head(10 + b)
                    for h in range(HQ):
                        for r in range(RT):
                            ins = pe.matmul(bank[half(h), (h // 2) * P:(h // 2 + 1) * P], w_uv[:, h, r, :],
                                            olT[:, r, h * P:(h + 1) * P], start=r == 0, stop=r == RT - 1)
                    ins.then_inc(sem("head_done"), 1)

                pe.wait_ge(sem("w_qk_loaded"), hg * 16 + 16)
                for j in range(2):
                    bank = head(j)
                    for k in range(QT):
                        ins = pe.matmul(bank[:], w_uq[:, k, j * P:(j + 1) * P], cqT[:, k, :], start=k == 0, stop=k == QT - 1)
                    ins.then_inc(sem("head_done"), 1)
                pe.wait_ge(sem("head_taken"), hg * 14 + 2 + 2)
                for h in range(HQ):
                    for r in range(RT):
                        bank = head(2 + h * RT + r)
                        pe.matmul(bank[:], w_uk[half(h), h // 2, r * P:(r + 1) * P], qT[half(h), h // 2, :],
                                  start=True, stop=True).then_inc(sem("head_done"), 1)
                pe.wait_ge(sem("head_taken"), hg * 14 + 10 + 2)
                score(0)
                score(1)
                for s in range(16):
                    b, h = s // HQ, s % HQ
                    if s + 2 < 16:
                        score(s + 2)
                    pe.wait_ge(sem("probs_ready"), hg * 16 + s + 1)
                    pe.wait_ge(sem("turned_taken"), hg * 16 + s + 1)
                    for kb in range(b + 1):
                        ins = pe.transpose(psum[4 + s % 2][:, kb * P:(kb + 1) * P], probs[:, s % 4, kb * P:(kb + 1) * P], ident[:])
                    ins.then_inc(sem("turned"), 1)
                    if s % 4 == 1 and s > 4:
                        out_heads(s // 4 - 1)
                    if h == HQ - 1:
                        pe.wait_ge(sem("turned_taken"), hg * 16 + s + 1 + 2)
                        for r in range(RT):
                            pe.wait_ge(sem("olat_taken"), hg * 8 + 2 * b + r + 1)
                            for kb in range(b + 1):
                                ins = pe.matmul(psum[6 + r][:], kvn[:, kb, r * P:(r + 1) * P], PT[:, b % 2, kb, :],
                                                start=kb == 0, stop=kb == b)
                            ins.then_inc(sem("olat_done"), 1)
                out_heads(TT - 1)
            pe.wait_ge(sem("head_taken"), 14 * TT + 2)
            pe.wait_ge(sem("olat_taken"), 8 * TT + 2)
            with pe.Fori(0, GROUPS) as g:
                for j in range(6):
                    if j in (0, 4):
                        pe.wait_ge(sem(("w_ssm_x_loaded", "w_ssm_bc_loaded")[j // 4]), g * 16 + 16)
                    if j < 4:
                        pe.wait_ge(sem("y_taken"), g * 4 + j + 1)
                    else:
                        pe.wait_ge(sem(("btok_ready", "cb_ready")[j - 4]), g + 1)
                        if j == 4:
                            pe.wait_ge(sem("off_taken"), g * 3 + 1)
                    for k in range(KT):
                        w = w_ssm_x[:, k, j * P:(j + 1) * P] if j < 4 else w_ssm_bc[:, k, (j - 4) * P:(j - 3) * P]
                        ins = pe.matmul(psum[j][:], w, hT[:, k, :], start=k == 0, stop=k == KT - 1)
                    ins.then_inc(sem("conv_in"), 1)
                pe.wait_ge(sem("w_z_loaded"), g * 16 + 16)
                for c in range(TT):
                    pe.wait_ge(sem("pair_taken"), g * 12 + c + 1)
                    for k in range(KT):
                        ins = pe.matmul(psum[6 + c % 2][:], hT[:, k, c * P:(c + 1) * P], w_z[:, k, :], start=k == 0, stop=k == KT - 1)
                    ins.then_inc(sem("pair_done"), 1)

                def sums(k):
                    pe.wait_ge(sem("tri_ready"), g * 8 + k + 1)
                    pe.wait_ge(sem("pair_taken"), g * 12 + 4 + k + 1)
                    pe.matmul(psum[6 + k % 2][:], tri_gt[:], da_tri[:, k % 2].rearrange("p h l -> p (h l)"),
                              start=True, stop=True).then_inc(sem("pair_done"), 1)
                pe.wait_ge(sem("conv_ready"), g * 6 + 6 + 2)
                for c in range(TT):
                    for j in range(4):
                        ins = pe.transpose(psum[c][:, j * P:(j + 1) * P], xsT[:, j, c * P:(c + 1) * P], ident[:])
                    ins.then_inc(sem("x_ready"), 1)
                for c in range(TT):
                    ins = pe.transpose(psum[4][:, c * P:(c + 1) * P], xsT[:, 4, c * P:(c + 1) * P], ident[:])
                ins.then_inc(sem("b_turned"), 1)
                for c in range(TT):
                    ins = pe.matmul(psum[5][:, c * P:(c + 1) * P], xsT[:, 4, c * P:(c + 1) * P], xsT[:, 5, c * P:(c + 1) * P],
                                    start=True, stop=True)
                ins.then_inc(sem("cb_done"), 1)
                sums(0)
                sums(1)
                for c in range(TT):
                    if c < TT - 1:
                        pe.wait_ge(sem("xend_ready"), g * 3 + c + 1)
                        if c == 0:
                            pe.wait_ge(sem("btok_ready"), g + 2)
                            pe.wait_ge(sem("cb_ready"), g + 2)
                        else:
                            pe.wait_ge(sem("state_ready"), g * 3 + c)
                        sums(2 * c + 2)
                        sums(2 * c + 3)
                    if c > 0:
                        pe.wait_ge(sem("state_ready"), g * 3 + c)
                        pe.wait_ge(sem("off_taken"), g * 3 + c)
                        pe.matmul(psum[4][:], xsT[:, 5, c * P:(c + 1) * P], state, start=True, stop=True).then_inc(sem("off_done"), 1)
                    if c < TT - 1:
                        pe.matmul(psum[5][:], b_tok[:, c * P:(c + 1) * P], xend[:, c % 2], start=True, stop=True).then_inc(sem("state_done"), 1)
                    pe.wait_ge(sem("m_ready"), g * 8 + 2 * c + 2 + 2)
                    pe.wait_ge(sem("xdt_ready"), g * 4 + c + 1)
                    for h in range(GH):
                        ins = pe.matmul(psum[c][:, h * HEAD:(h + 1) * HEAD], mix_m[:, (2 * c + h // 4) % 4, h % 4, :],
                                        xdt[:, c, h * HEAD:(h + 1) * HEAD], start=True, stop=True)
                    ins.then_inc(sem("diag_done"), 1)
                pe.wait_ge(sem("yn_ready"), g * 4 + 4)
                for j in range(4):
                    for c in range(TT):
                        ins = pe.transpose(psum[j][:, c * P:(c + 1) * P], y[:, c, j * P:(j + 1) * P], ident[:])
                    ins.then_inc(sem("y_turned"), 1)
            pe.wait_ge(sem("y_taken"), 4 * GROUPS + 4)
            for u in range(2):
                pe.wait_ge(sem(f"sc_gated{u}"), KT // 2 + 1)
            with pe.Fori(0, KT) as n:
                pe.wait_ge(sem("w_merge_loaded"), n * 16 + 16)
                for j, (at_k, kn, src) in enumerate(((0, 16, ynT), (16, KT, gatedT), (24, KT, oT))):
                    pe.wait_ge(sem("branch_taken"), n * 3 + j + 1)
                    for k in range(kn):
                        ins = pe.matmul(psum[j][:], w_merge[:, at_k + k, :], src[:, k, :], start=k == 0, stop=k == kn - 1)
                    ins.then_inc(sem("branch_done"), 1)
                pe.wait_ge(sem("w_gates_loaded"), n * 16 + 16)
                for j in range(3):
                    pe.wait_ge(sem("gate_taken"), n * 3 + j + 1)
                    for k in range(KT):
                        ins = pe.matmul(psum[3 + j][:], w_gates[:, k, j, :], hT[:, k, :], start=k == 0, stop=k == KT - 1)
                    ins.then_inc(sem("gate_done"), 1)
            pe.wait_ge(sem("w_mix_loaded"), 32)
            pe.wait_ge(sem("merged"), KT + 1)
            for b in range(8):
                c, half = b // 2, b % 2
                for k in range(KT):
                    ins = pe.matmul(psum[b][:], mergedT[:, k, c * P:(c + 1) * P], w_mix[half][:, k, :], start=k == 0, stop=k == KT - 1)
                ins.then_inc(sem("mix_done"), 1)
            pe.wait_ge(sem("h2_ready"), TT)
            for k in range(KT):
                for c in range(TT):
                    ins = pe.transpose(psum[k][:, c * P:(c + 1) * P], h2[:, c, k * P:(k + 1) * P], ident[:])
                ins.then_inc(sem("h2_turned"), 1)
            pe.wait_ge(sem("h2T_ready"), KT)
            pe.wait_ge(sem("w_router_loaded"), 16)
            for c in range(TT):
                for k in range(KT):
                    ins = pe.matmul(psum[7][:, c * NR:(c + 1) * NR], h2T[:, k, c * P:(c + 1) * P], w_router[:, k, :],
                                    start=k == 0, stop=k == KT - 1)
            ins.then_inc(sem("routed"), 1)
            pe.wait_ge(sem("logits_out"), 1)
            with pe.Fori(0, EXPERTS) as e:
                for f in range(FT):
                    for j, (w, ready) in enumerate(((w_gate, "w_gate_loaded"), (w_up, "w_up_loaded"))):
                        if f == 0:
                            pe.wait_ge(sem(ready), e * 16 + 16)
                        pe.wait_ge(sem("hid_ready"), e * 4 + f + 1)
                        for k in range(KT):
                            ins = pe.matmul(psum[2 * j + f % 2][:], w[:, k, f * P:(f + 1) * P], h2T[:, k, :], start=k == 0, stop=k == KT - 1)
                        ins.then_inc(sem("gate_up_done"), 1)
                pe.wait_ge(sem("w_down_loaded"), e * 16 + 16)
                pe.wait_ge(sem("hid_ready"), e * 4 + 4 + 2)
                for b in range(8):
                    c, half = b // 2, b % 2
                    pe.wait_ge(sem("down_taken"), e * 8 + b + 1)
                    for f in range(FT):
                        ins = pe.matmul(psum[4 + b % 4][:], hidT[:, f, c * P:(c + 1) * P], w_down[:, f, half * 512:(half + 1) * 512],
                                        start=f == 0, stop=f == FT - 1)
                    ins.then_inc(sem("down_done"), 1)

        @block.scalar
        def _(act):
            act.wait_ge(sem("params_loaded"), 32)
            for k in range(KT):
                act.wait_ge(sem("x_turned"), k + 1)
                act.activation(hT[:, k, :], psum[k][:], ACT.Copy, scale=cols[:, C_G1 + k:C_G1 + k + 1]).then_inc(sem("hT_ready"), 1)
            for c in range(TT):
                act.wait_ge(sem("kq_projected"), c + 1)
                act.activation(kvraw[:, c, :], psum[c][:, 0:KVC], ACT.Copy).then_inc(sem("kv_taken"), 1)
            for c in range(TT):
                act.wait_ge(sem("kq_projected"), TT + c + 1)
                act.activation(qraw[:, c, :], psum[4 + c][:, 0:Q_LORA], ACT.Copy).then_inc(sem("q_taken"), 1)
            act.wait_ge(sem("dtabs_ready"), 1)
            act.activation(da_sb[:], da_sb[:], ACT.Exp, scale=-1.0).then_inc(sem("dtexp_ready"), 1)
            act.activation(rows[:, R_ALOG:R_ALOG + SSM_HEADS], rows[:, R_ALOG:R_ALOG + SSM_HEADS], ACT.Exp).then_inc(sem("dtexp_ready"), 1)
            for j in range(QT + RT + 1):
                act.wait_ge(sem("latents_turned"), j + 1)
                src = psum[4 + j % 4][:]
                if j < QT:
                    ins = act.activation(cqT[:, j, :], src, ACT.Copy, scale=cols[:, C_QG + j:C_QG + j + 1])
                elif j < QT + RT:
                    ins = act.activation(kvnT[:, j - QT, :], src, ACT.Copy)
                else:
                    ins = act.activation(kidxT, src, ACT.Copy, scale=cols[:, C_KG:C_KG + 1])
                ins.then_inc(sem("latents_taken"), 1)
            act.wait_ge(sem("sums_ready"), 1)
            act.activation(ex_sb[:].rearrange("p a c h -> p (a c h)"), psum[0][:, 0:3 * TT * SSM_HEADS], ACT.Exp).then_inc(sem("sums_taken"), 1)
            for j in range(IDX_HEADS // 2):
                act.wait_ge(sem("qi_projected"), j + 1)
                act.activation(qiT[:, j, :], psum[4 + j][:], ACT.Copy).then_inc(sem("qi_ready"), 1)
            n = 0
            for b in range(1, TT):
                for h in range(IDX_HEADS):
                    act.wait_ge(sem("dots_ready"), n + 1)
                    if n >= 2:
                        act.wait_ge(sem("score_added"), n - 1)
                    act.activation(relu[:, n % 2, 0:(b + 1) * P], psum[6 + n % 2][:, 0:(b + 1) * P], ACT.Relu).then_inc(sem("dots_taken"), 1)
                    n += 1
            for u in range(2):
                act.sem_inc(sem(f"sc_in{u}"), 3)
            with act.Fori(0, KT // 2) as i:
                for u in range(2):
                    act.wait_ge(sem(f"sc_gated{u}"), i + 1)
                    for j in range(3):
                        act.wait_ge(sem("sc_projected"), i * 6 + 3 * u + j + 1)
                        act.activation(sc_in[:, u, j, :], psum[3 * u + j][:], ACT.Copy).then_inc(sem(f"sc_in{u}"), 1)
            act.wait_ge(sem("bias_ready"), TT - 1)
            for u in range(2):
                act.wait_ge(sem(f"sc_gated{u}"), KT // 2 + 1)
            act.sem_inc(sem("head_taken"), 2)
            act.sem_inc(sem("turned_taken"), 2)
            with act.Fori(0, TT) as hg:
                def take_head(k):
                    act.wait_ge(sem("head_done"), hg * 14 + k + 1)
                    if k < 2:
                        ins = act.activation(qT[:, k, :], psum[k][:], ACT.Copy)
                    elif k < 10:
                        ins = act.activation(qlatT[:, k - 2, :], psum[k % 2][:], ACT.Copy)
                    else:
                        b = k - 10
                        ins = act.activation(oT[:, bass.ds(hg * 2, 2), b * P:(b + 1) * P],
                                             psum[k % 2][:, 0:2 * P].rearrange("p (j q) -> p j q", j=2), ACT.Copy)
                    ins.then_inc(sem("head_taken"), 1)

                def take_turned(s):
                    b, h = s // HQ, s % HQ
                    act.wait_ge(sem("turned"), hg * 16 + s + 1)
                    act.activation(PT[:, b % 2, 0:b + 1, h * P:(h + 1) * P],
                                   psum[4 + s % 2][:, 0:(b + 1) * P].rearrange("p (k q) -> p k q", k=b + 1), ACT.Copy
                                   ).then_inc(sem("turned_taken"), 1)
                for k in range(10):
                    take_head(k)
                for s in range(16):
                    b = s // HQ
                    act.wait_ge(sem("max_ready"), hg * 16 + s + 1)
                    pr = probs[:, s % 4, 0:(b + 1) * P]
                    act.activation(pr, pr, ACT.Exp, bias=nmax[:, s % 4:s % 4 + 1], scale=ATT_SCALE,
                                   accum_out=psums[:, s % 4:s % 4 + 1]).then_inc(sem("exp_done"), 1)
                    if s >= 1:
                        take_turned(s - 1)
                    if s >= 6 and s % 4 == 2:
                        take_head(10 + (s - 6) // 4)
                take_turned(15)
                take_head(13)
            act.sem_inc(sem("y_taken"), 4)
            act.sem_inc(sem("btok_ready"), 1)
            act.sem_inc(sem("pair_taken"), 2)
            act.sem_inc(sem("conv_ready"), 2)
            act.wait_ge(sem("olat_taken"), 8 * TT + 2)
            with act.Fori(0, GROUPS) as g:
                for j in range(6):
                    act.wait_ge(sem("conv_out"), g * 6 + j + 1)
                    act.activation(xsT[:, j, :], conv[:, j % 2], ACT.Silu,
                                   bias=cols[:, bass.ds(C_CONV + TAPS + g * 30 + j * 5, 1)]).then_inc(sem("conv_ready"), 1)
                for c in range(TT):
                    act.wait_ge(sem("pair_done"), g * 12 + c + 1)
                    act.activation(sz[:, c, :], psum[6 + c % 2][:], ACT.Silu).then_inc(sem("pair_taken"), 1)
                act.wait_ge(sem("b_turned"), g + 1)
                act.activation(b_tok, psum[4][:], ACT.Copy).then_inc(sem("btok_ready"), 1)
                for k in range(8):
                    act.wait_ge(sem("pair_done"), g * 12 + 4 + k + 1)
                    act.wait_ge(sem("m_ready"), g * 8 + k + 1)
                    act.activation(decay[:, k % 2].rearrange("p h l -> p (h l)"), psum[6 + k % 2][:], ACT.Exp).then_inc(sem("pair_taken"), 1)
                for j in range(4):
                    act.wait_ge(sem("y_turned"), g * 4 + j + 1)
                    act.activation(ynT[:, bass.ds(g * 4 + j, 1), :].rearrange("p o s -> p (o s)"), psum[j][:], ACT.Copy,
                                   scale=cols[:, bass.ds(C_NG + g * 4 + j, 1)]).then_inc(sem("y_taken"), 1)
            act.sem_inc(sem("gate_taken"), 3)
            with act.Fori(0, KT) as n:
                for j in range(3):
                    act.wait_ge(sem("gate_done"), n * 3 + j + 1)
                    act.wait_ge(sem("branch_taken"), n * 3 + j + 1)
                    act.activation(sig[:, j, :], psum[3 + j][:], ACT.Sigmoid).then_inc(sem("gate_taken"), 1)
            for k in range(KT):
                act.wait_ge(sem("h2_turned"), k + 1)
                act.activation(h2T[:, k, :], psum[k][:], ACT.Copy, scale=cols[:, C_G2 + k:C_G2 + k + 1]).then_inc(sem("h2T_ready"), 1)
            act.wait_ge(sem("rt_in"), 1)
            act.activation(rsc[:, 2, 0:16], rsc[:, 1, 0:16], ACT.Exp).then_inc(sem("rt_exp"), 1)
            act.wait_ge(sem("rt_in"), 2)
            act.activation(rsc[:, 10, 0:4], rsc[:, 10, 0:4], ACT.Exp).then_inc(sem("rt_exp"), 1)
            with act.Fori(0, EXPERTS) as e:
                for f in range(FT):
                    act.wait_ge(sem("gate_up_done"), e * 8 + 2 * f + 1)
                    act.wait_ge(sem("hid_ready"), e * 4 + f + 1)
                    act.activation(sg[:, f % 2, :], psum[f % 2][:], ACT.Silu).then_inc(sem("sg_ready"), 1)

        @block.vector
        def _(dve):
            own = Marks(dve, sem("dve_pre"))
            dve.wait_ge(sem("x_loaded"), 16)
            for c in range(TT):
                own.mark(dve.tensor_tensor_reduce(sq, x_sb[:, c, :], x_sb[:, c, :], 1.0, 0.0, ALU.mult, ALU.add, ms[:, c:c + 1]))
                own.settle()
            dve.tensor_scalar(ms, ms, 1.0 / D, EPS, ALU.mult, ALU.add).then_inc(sem("ms_ready"), 1)
            dve.wait_ge(sem("rstd_ready"), 1)
            for c in range(TT):
                dve.tensor_scalar(x_sb[:, c, :], x_sb[:, c, :], rstd[:, c:c + 1], None, ALU.mult).then_inc(sem("xn_ready"), 1)
            dve.wait_ge(sem("kv_taken"), TT)
            dve.wait_ge(sem("params_loaded"), 32)
            for c in range(TT):
                a = kvraw[:, c, 0:KV_LORA]
                own.mark(dve.tensor_tensor_reduce(sq[:, 0:KV_LORA], a, a, 1.0, 0.0, ALU.mult, ALU.add, ms2[:, 4 + c:5 + c]))
                a = kvraw[:, c, KV_LORA:KV_LORA + D_IDX]
                own.mark(dve.tensor_tensor_reduce(sq[:, 256:256 + D_IDX], a, a, 1.0, 0.0, ALU.mult, ALU.add, ms2[:, 8 + c:9 + c]))
                own.settle()
            dve.wait_ge(sem("q_taken"), TT)
            for c in range(TT):
                own.mark(dve.tensor_tensor_reduce(sq[:, 0:Q_LORA], qraw[:, c, :], qraw[:, c, :], 1.0, 0.0, ALU.mult, ALU.add, ms2[:, c:c + 1]))
                own.settle()
            own.mark(dve.tensor_scalar(ms2[:, 0:4], ms2[:, 0:4], 1.0 / Q_LORA, EPS, ALU.mult, ALU.add))
            own.mark(dve.tensor_scalar(ms2[:, 4:8], ms2[:, 4:8], 1.0 / KV_LORA, EPS, ALU.mult, ALU.add))
            dve.tensor_scalar(ms2[:, 8:12], ms2[:, 8:12], 1.0 / D_IDX, EPS, ALU.mult, ALU.add).then_inc(sem("ms2_ready"), 1)
            own.settle()
            dtb = rows[:, R_DTB:R_DTB + SSM_HEADS]
            for c in range(TT):
                dve.wait_ge(sem("kq_projected"), 2 * TT + c + 1)
                own.mark(dve.tensor_tensor(dt_sb[:, c, :], psum[c][:, 0:SSM_HEADS], dtb, ALU.add))
            own.settle()
            own.mark(dve.tensor_scalar(da_sb[:], dt_sb[:], -1.0, None, ALU.mult))
            own.settle()
            dve.tensor_tensor(da_sb[:], da_sb[:], dt_sb[:], ALU.max).then_inc(sem("dtabs_ready"), 1)
            dve.wait_ge(sem("rstd2_ready"), 1)
            for c in range(TT):
                own.mark(dve.tensor_scalar(qraw[:, c, :], qraw[:, c, :], rstd2[:, c:c + 1], None, ALU.mult))
                own.mark(dve.scalar_tensor_tensor(out=kvn[:, c, :], in0=kvraw[:, c, 0:KV_LORA], scalar=rstd2[:, 4 + c:5 + c],
                                                  in1=rows[:, R_KVG:R_KVG + KV_LORA], op0=ALU.mult, op1=ALU.mult))
                for u in range(2):
                    own.mark(dve.tensor_scalar(kdup[:, c, u * D_IDX:(u + 1) * D_IDX], kvraw[:, c, KV_LORA:KV_LORA + D_IDX],
                                               rstd2[:, 8 + c:9 + c], None, ALU.mult))
            own.settle()
            dve.tensor_scalar(widx, kvraw[:, :, KV_LORA + D_IDX:KVC], IDX_SCALE, None, ALU.mult).then_inc(sem("latents_scaled"), 3)
            dve.wait_ge(sem("dtexp_ready"), 2)
            lu, ls, lp = da_sb[:], relu_tmp(relu, 0), relu_tmp(relu, 1)
            ls2 = relu_tmp(relu, 2)
            own.mark(dve.tensor_scalar(ls, lu, 2.0, None, ALU.add))
            own.settle()
            own.mark(dve.reciprocal(ls, ls))
            own.settle()
            own.mark(dve.tensor_tensor(ls, lu, ls, ALU.mult))
            own.settle()
            own.mark(dve.tensor_tensor(ls2, ls, ls, ALU.mult))
            own.settle()
            own.mark(dve.tensor_scalar(lp, ls2, 1.0 / 15, 1.0 / 13, ALU.mult, ALU.add))
            own.settle()
            for d in (11, 9, 7, 5, 3, 1):
                own.mark(dve.tensor_tensor(lp, lp, ls2, ALU.mult))
                own.settle()
                own.mark(dve.tensor_scalar(lp, lp, 1.0 / d, None, ALU.add))
                own.settle()
            own.mark(dve.scalar_tensor_tensor(out=lp, in0=lp, scalar=2.0, in1=ls, op0=ALU.mult, op1=ALU.mult))
            own.settle()
            own.mark(dve.scalar_tensor_tensor(out=dt_sb[:], in0=dt_sb[:], scalar=0.0, in1=lp, op0=ALU.max, op1=ALU.add))
            own.settle()
            ea = rows[:, R_ALOG:R_ALOG + SSM_HEADS].unsqueeze(1).to_broadcast([P, TT, SSM_HEADS])
            dve.scalar_tensor_tensor(out=da_sb[:], in0=dt_sb[:], scalar=-1.0, in1=ea, op0=ALU.mult, op1=ALU.mult).then_inc(sem("da_ready"), 1)
            n = 0
            for b in range(1, TT):
                sc = bias[:, BIAS_AT[b]:BIAS_AT[b] + (b + 1) * P]
                for h in range(IDX_HEADS):
                    dve.wait_ge(sem("dots_taken"), n + 1)
                    r = relu[:, n % 2, 0:(b + 1) * P]
                    if h == 0:
                        ins = dve.tensor_scalar(sc, r, widx[:, b, h:h + 1], None, ALU.mult)
                    else:
                        dve.wait_ge(sem("score_added"), n)
                        ins = dve.scalar_tensor_tensor(out=sc, in0=r, scalar=widx[:, b, h:h + 1], in1=sc, op0=ALU.mult, op1=ALU.add)
                    ins.then_inc(sem("score_added"), 1)
                    n += 1
                dve.wait_ge(sem("score_added"), n)
                dve.engine_nop().then_inc(sem("score_ready"), 1)
            for b in range(1, TT):
                sc = bias[:, BIAS_AT[b]:BIAS_AT[b] + (b + 1) * P]
                dve.wait_ge(sem("score_hidden"), b)
                for r in range(TOPK // 8):
                    own.mark(dve.max(m8, sc))
                    own.settle()
                    own.mark(dve.match_replace(sc, m8, sc, TAKEN))
                    own.settle()
                dve.tensor_scalar(sc, sc, 0.5 * (UNSEEN + TAKEN), -BIG, ALU.is_gt, ALU.mult).then_inc(sem("bias_ready"), 1)
            for u in range(2):
                dve.wait_ge(sem(f"sc_gated{u}"), KT // 2 + 1)
            dve.wait_ge(sem("consts_ready"), 4)
            dve.sem_inc(sem("logits_taken"), 2)
            dve.sem_inc(sem("olat_taken"), 2)
            with dve.Fori(0, TT) as hg:
                def largest(s):
                    b = s // HQ
                    n = (b + 1) * P
                    dve.wait_ge(sem("logits_done"), hg * 16 + s + 1)
                    dve.memset(waited, 0.0)
                    dve.tensor_tensor_reduce(probs[:, s % 4, 0:n], psum[2 + s % 2][:, 0:n], bias[:, BIAS_AT[b]:BIAS_AT[b] + n],
                                             1.0, TAKEN, ALU.add, ALU.max, pmax[:, s % 4:s % 4 + 1]).then_inc(sem("logits_taken"), 1)
                    dve.wait_ge(sem("logits_taken"), hg * 16 + s + 1 + 2)
                    dve.tensor_scalar(nmax[:, s % 4:s % 4 + 1], pmax[:, s % 4:s % 4 + 1], -ATT_SCALE, None, ALU.mult).then_inc(sem("max_ready"), 1)

                def divide(s):
                    n = (s // HQ + 1) * P
                    dve.wait_ge(sem("exp_done"), hg * 16 + s + 1)
                    dve.reciprocal(pinv[:, s % 4:s % 4 + 1], psums[:, s % 4:s % 4 + 1]).then_inc(sem("pinv_ready"), 1)
                    dve.wait_ge(sem("pinv_ready"), hg * 16 + s + 1)
                    pr = probs[:, s % 4, 0:n]
                    dve.tensor_scalar(pr, pr, pinv[:, s % 4:s % 4 + 1], None, ALU.mult).then_inc(sem("probs_ready"), 1)

                def take_olat(b):
                    for r in range(RT):
                        dve.wait_ge(sem("olat_done"), hg * 8 + 2 * b + r + 1)
                        dve.tensor_copy(olT[:, r, :], psum[6 + r][:]).then_inc(sem("olat_taken"), 1)
                for s in range(17):
                    if s < 16:
                        largest(s)
                    if s >= 1:
                        divide(s - 1)
                    if s % 4 == 1 and s > 4:
                        take_olat(s // 4 - 1)
                take_olat(TT - 1)
            dve.wait_ge(sem("head_done"), 14 * TT)
            dve.sem_inc(sem("cb_ready"), 1)
            dve.sem_inc(sem("m_ready"), 2)
            dve.sem_inc(sem("off_taken"), 1)
            own = Marks(dve, sem("dve_ssd"))
            with dve.Fori(0, GROUPS) as g:
                own.loop(i=g, per=6 * 3 + 3 * TT + 3 + 2)
                for j in range(6):
                    w = [cols[:, bass.ds(C_CONV + k + g * 30 + j * 5, 1)] for k in range(TAPS)]
                    a, src = conv[:, j % 2], psum[j][:]
                    dve.wait_ge(sem("conv_in"), g * 6 + j + 1)
                    dve.wait_ge(sem("conv_ready"), g * 6 + j + 1)
                    own.mark(dve.tensor_scalar(a, src, w[3], None, ALU.mult))
                    for d in (1, 2, 3):
                        own.settle()
                        ins = dve.scalar_tensor_tensor(out=a[:, d:], in0=src[:, 0:S - d], scalar=w[3 - d], in1=a[:, d:], op0=ALU.mult, op1=ALU.add)
                        if d < 3:
                            own.mark(ins)
                    ins.then_inc(sem("conv_out"), 1)
                hs = bass.ds(g * GH, GH)
                dskip = rows[:, bass.ds(R_D + g * GH, GH)].unsqueeze(2).to_broadcast([P, GH, HEAD])
                dve.wait_ge(sem("x_ready"), g * 4 + 4)
                for c in range(TT):
                    dve.tensor_tensor(heads(y[:, c]), heads(psum[c][:]), dskip, ALU.mult)
                    dve.tensor_tensor(heads(xdt[:, c]), heads(psum[c][:]), dt_sb[:, c, hs].unsqueeze(2).to_broadcast([P, GH, HEAD]),
                                      ALU.mult).then_inc(sem("xdt_ready"), 1)
                dve.wait_ge(sem("cb_done"), g + 1)
                dve.tensor_tensor(cb, psum[5][:].rearrange("p (c l) -> p c l", c=TT), tri_le[:].unsqueeze(1).to_broadcast([P, TT, P]),
                                  ALU.mult).then_inc(sem("cb_ready"), 1)
                dve.wait_ge(sem("cb_ready"), g + 2)
                dve.wait_ge(sem("xdt_ready"), g * 4 + 4)
                for c in range(TT):
                    for k in (2 * c, 2 * c + 1):
                        dve.wait_ge(sem("pair_taken"), g * 12 + 4 + k + 1 + 2)
                        dve.tensor_tensor(mix_m[:, k % 4], decay[:, k % 2], cb[:, c, :].unsqueeze(1).to_broadcast([P, 4, P]),
                                          ALU.mult).then_inc(sem("m_ready"), 1)
                    if c < TT - 1:
                        dve.wait_ge(sem("state_done"), g * 3 + c + 1)
                        if c == 0:
                            dve.tensor_copy(state, psum[5][:]).then_inc(sem("state_ready"), 1)
                        else:
                            dve.wait_ge(sem("off_done"), g * 3 + c)
                            cd = ex_sb[:, 2, c, hs].unsqueeze(2).to_broadcast([P, GH, HEAD])
                            own.mark(dve.tensor_tensor(heads(state), heads(state), cd, ALU.mult))
                            own.settle()
                            dve.tensor_tensor(state, state, psum[5][:], ALU.add).then_inc(sem("state_ready"), 1)
                    dve.wait_ge(sem("diag_done"), g * 4 + c + 1)
                    own.mark(dve.tensor_tensor(y[:, c], y[:, c], psum[c][:], ALU.add))
                    if c > 0:
                        dve.wait_ge(sem("off_done"), g * 3 + c)
                        ec = ex_sb[:, 0, c, hs].unsqueeze(2).to_broadcast([P, GH, HEAD])
                        dve.tensor_tensor(heads(tmp), heads(psum[4][:]), ec, ALU.mult).then_inc(sem("off_taken"), 1)
                        own.settle()
                        dve.wait_ge(sem("off_taken"), g * 3 + c + 1)
                        own.mark(dve.tensor_tensor(y[:, c], y[:, c], tmp, ALU.add))
                    own.settle()
                    own.mark(dve.tensor_tensor(y[:, c], y[:, c], sz[:, c, :], ALU.mult))
                    own.settle()
                    own.mark(dve.tensor_tensor_reduce(tmp, y[:, c], y[:, c], 1.0, 0.0, ALU.mult, ALU.add, m16[:, c:c + 1]))
                    own.settle()
                dve.tensor_scalar(m16, m16, 1.0 / 512, EPS, ALU.mult, ALU.add).then_inc(sem("yms_ready"), 1)
                dve.wait_ge(sem("yrstd_ready"), g + 1)
                for c in range(TT):
                    dve.tensor_scalar(y[:, c], y[:, c], r16[:, c:c + 1], None, ALU.mult).then_inc(sem("yn_ready"), 1)
                own.end(GROUPS)
            dve.wait_ge(sem("y_taken"), 4 * GROUPS + 4)
            dve.sem_inc(sem("branch_taken"), 3)
            dve.sem_inc(sem("merged"), 1)
            own = Marks(dve, sem("dve_merge"))
            with dve.Fori(0, KT) as n:
                own.loop(n, 1)
                dve.wait_ge(sem("merged"), n + 1)
                for j in range(3):
                    dve.wait_ge(sem("branch_done"), n * 3 + j + 1)
                    dve.wait_ge(sem("gate_taken"), n * 3 + j + 1 + 3)
                    dve.tensor_tensor(branch[:, min(j, 1)], psum[j][:], sig[:, j, :], ALU.mult).then_inc(sem("branch_taken"), 1)
                    dve.wait_ge(sem("branch_taken"), n * 3 + j + 1 + 3)
                    if j == 1:
                        own.mark(dve.tensor_tensor(branch[:, 0], branch[:, 0], branch[:, 1], ALU.add))
                        own.settle()
                    if j == 2:
                        dve.tensor_tensor(mergedT[:, bass.ds(n, 1), :].rearrange("p o s -> p (o s)"), branch[:, 0], branch[:, 1],
                                          ALU.add).then_inc(sem("merged"), 1)
                own.end(KT)
            own = Marks(dve, sem("dve_post"))
            dve.wait_ge(sem("x2_loaded"), 16)
            for b in range(8):
                c, half = b // 2, b % 2
                dve.wait_ge(sem("mix_done"), b + 1)
                a = x2[:, c, half * 512:(half + 1) * 512]
                own.mark(dve.tensor_tensor(a, a, psum[b][:], ALU.add))
            own.settle()

            def mean_squares(name):
                for c in range(TT):
                    own.mark(dve.tensor_tensor_reduce(h2[:, c, :], x2[:, c, :], x2[:, c, :], 1.0, 0.0, ALU.mult, ALU.add, ms[:, c:c + 1]))
                own.settle()
                dve.tensor_scalar(ms, ms, 1.0 / D, EPS, ALU.mult, ALU.add).then_inc(sem(name), 1)
            mean_squares("ms3_ready")
            dve.wait_ge(sem("rstd3_ready"), 1)
            for c in range(TT):
                dve.tensor_scalar(h2[:, c, :], x2[:, c, :], rstd[:, c:c + 1], None, ALU.mult).then_inc(sem("h2_ready"), 1)
            def do(ins):
                own.mark(ins)
                own.settle()

            def b4(ap, inner):
                return ap.unsqueeze(len(ap.shape)).to_broadcast(list(ap.shape) + [inner])

            def first_of(out, val, largest, tmp4):
                do(dve.tensor_tensor(tmp4, val, b4(largest, 4), ALU.is_equal))
                for j in range(4):
                    do(dve.tensor_scalar(tmp4[:, :, j], tmp4[:, :, j], float(4 - j), None, ALU.mult))
                do(dve.tensor_reduce(r1, tmp4, AX_X, ALU.max))
                do(dve.tensor_tensor(out, tmp4, b4(r1, 4), ALU.is_equal))

            def r4(j):
                return rsc[:, j, 0:TT * 4].rearrange("p (c g) -> p c g", c=TT)
            r1, gmax, l1, l2, pg, g1, g2 = (rsc[:, 11 + j, 0:TT] for j in range(7))
            glog, ohg, t4, ing, oh1, oh2, gx, t4b = (r4(j) for j in (0, 3, 4, 5, 6, 7, 1, 8))
            big16 = rsc[:, 18, :].rearrange("p (c j g) -> p c j g", c=TT, j=4)
            comb = rsc[:, 19, :].rearrange("p (c e) -> p c e", c=TT)
            dve.wait_ge(sem("routed"), 1)
            dve.tensor_tensor(logits, psum[7][:, 0:TT * NR].rearrange("p (c n) -> p c n", c=TT),
                              rows[:, R_RB:R_RB + NR].unsqueeze(1).to_broadcast([P, TT, NR]), ALU.add).then_inc(sem("logits_out"), 1)
            dve.wait_ge(sem("logits_out"), 1)
            do(dve.tensor_copy(glog, logits[:, :, 0:EG]))
            do(dve.tensor_reduce(gmax, glog, AX_X, ALU.max))
            dve.tensor_tensor(gx, glog, b4(gmax, 4), ALU.subtract).then_inc(sem("rt_in"), 1)
            first_of(ohg, glog, gmax, t4)
            for j in range(4):
                do(dve.tensor_tensor(big16[:, :, j, :], logits[:, :, EG:].rearrange("p c (g j) -> p c j g", j=4)[:, :, j, :], ohg, ALU.mult))
            do(dve.tensor_reduce(ing, big16, AX_X, ALU.add))
            do(dve.tensor_reduce(l1, ing, AX_X, ALU.max))
            first_of(oh1, ing, l1, t4)
            do(dve.scalar_tensor_tensor(out=t4b, in0=oh1, scalar=-BIG, in1=ing, op0=ALU.mult, op1=ALU.add))
            do(dve.tensor_reduce(l2, t4b, AX_X, ALU.max))
            first_of(oh2, t4b, l2, t4)
            dve.tensor_tensor(rsc[:, 10, 0:TT], l2, l1, ALU.subtract).then_inc(sem("rt_in"), 1)
            dve.wait_ge(sem("rt_exp"), 2)
            do(dve.tensor_reduce(pg, r4(2), AX_X, ALU.add))
            do(dve.tensor_scalar(g1, rsc[:, 10, 0:TT], 1.0, None, ALU.add))
            do(dve.tensor_tensor(g1, g1, pg, ALU.mult))
            do(dve.reciprocal(g1, g1))
            do(dve.tensor_tensor(g2, g1, rsc[:, 10, 0:TT], ALU.mult))
            do(dve.tensor_tensor(oh1, oh1, b4(g1, 4), ALU.mult))
            do(dve.tensor_tensor(oh2, oh2, b4(g2, 4), ALU.mult))
            do(dve.tensor_tensor(oh1, oh1, oh2, ALU.add))
            for j in range(4):
                do(dve.tensor_tensor(comb[:, :, 4 * j:4 * j + 4], oh1, b4(ohg[:, :, j], 4), ALU.mult))
            dve.sem_inc(sem("hid_ready"), 2)
            dve.sem_inc(sem("down_taken"), 4)
            with dve.Fori(0, EXPERTS) as e:
                for f in range(FT):
                    dve.wait_ge(sem("gate_up_done"), e * 8 + 2 * f + 2)
                    dve.wait_ge(sem("sg_ready"), e * 4 + f + 1)
                    dve.tensor_tensor(hidT[:, f, :], sg[:, f % 2, :], psum[2 + f % 2][:], ALU.mult).then_inc(sem("hid_ready"), 1)
                for b in range(8):
                    c, half = b // 2, b % 2
                    a = x2[:, c, half * 512:(half + 1) * 512]
                    dve.wait_ge(sem("down_done"), e * 8 + b + 1)
                    dve.scalar_tensor_tensor(out=a, in0=psum[4 + b % 4][:], scalar=comb[:, c, bass.ds(e, 1)], in1=a,
                                             op0=ALU.mult, op1=ALU.add).then_inc(sem("down_taken"), 1)
            dve.wait_ge(sem("down_taken"), 8 * EXPERTS + 4)
            mean_squares("ms4_ready")
            dve.wait_ge(sem("rstd4_ready"), 1)
            dve.wait_ge(sem("final_g_loaded"), 16)
            for c in range(TT):
                dve.scalar_tensor_tensor(out=x2[:, c, :], in0=x2[:, c, :], scalar=rstd[:, c:c + 1], in1=final_g,
                                         op0=ALU.mult, op1=ALU.mult).then_inc(sem("out_ready"), 1)


def heads(ap):
    return ap.rearrange("p (h d) -> p h d", d=HEAD)


def relu_tmp(relu, j):
    return relu[:, 0, j * 128:(j + 1) * 128].rearrange("p (t h) -> p t h", t=TT)


def tile_k(w, n=None):
    k, n = w.shape
    return np.ascontiguousarray(w.reshape(k // P, P, n).transpose(1, 0, 2).reshape(P, -1))


def layout(i):
    g = {k: np.asarray(v)[0] for k, v in i.items() if k not in ("x", "final_norm_g")}
    w_in = g["w_in"]
    sizes = [2048, 3072, 32, 1024, 1024, 1024, 384, 256, 64, 8, 1024, 1024, 1024]
    at = np.cumsum([0] + sizes)
    z, xbc, dt, sb_, sc_, sx_, cq, ckv, kix, wix, ga, gb, gc = (w_in[:, at[j]:at[j + 1]] for j in range(len(sizes)))

    def pair3(ws):
        return np.stack([np.stack([w[:, j * P:(j + 1) * P] for w in ws], 1).reshape(KT, P, 3, P).transpose(1, 0, 2, 3).reshape(P, -1)
                         for j in range(KT)])

    a = {}
    a["x"] = np.asarray(i["x"]).reshape(TT, P, D)
    a["w_kv"] = tile_k(w_in[:, at[7]:at[10]])
    a["w_q"] = tile_k(cq)
    a["w_dt"] = tile_k(dt)
    a["w_idx"] = tile_k(g["idx_w_q"].reshape(Q_LORA, -1))
    a["w_sc"] = pair3([sb_, sc_, sx_])
    uq = g["att_w_uq"].reshape(Q_LORA, -1)
    uk = g["att_w_uk"].reshape(4, 2, 2, HEAD, KV_LORA).transpose(0, 2, 3, 1, 4).reshape(4, P, -1)
    a["w_qk"] = np.stack([np.concatenate([tile_k(uq[:, j * 256:(j + 1) * 256]), uk[j]], 1) for j in range(4)])
    a["w_uv"] = g["att_w_uv"].reshape(4, HQ, RT, P, HEAD).transpose(0, 3, 1, 2, 4).reshape(4, P, -1)
    xs_, b_, c_ = xbc[:, :2048], xbc[:, 2048:2560], xbc[:, 2560:]
    a["w_ssm_x"] = np.stack([tile_k(xs_[:, 512 * q:512 * q + 512]) for q in range(GROUPS)])
    a["w_ssm_bc"] = np.stack([tile_k(np.concatenate([b_[:, P * q:P * q + P], c_[:, P * q:P * q + P]], 1)) for q in range(GROUPS)])
    a["w_z"] = np.stack([tile_k(z[:, 512 * q:512 * q + 512]) for q in range(GROUPS)])
    outs = np.concatenate([g["ssm_w_out"], g["sc_w_out"], g["att_w_out"]], 0)
    a["w_merge"] = np.stack([tile_k(outs[:, P * j:P * j + P]) for j in range(KT)])
    a["w_gates"] = pair3([ga, gb, gc])
    a["w_mix"] = np.stack([tile_k(g["mix_w_out"][:, 512 * j:512 * j + 512]) for j in range(2)])
    a["w_router"] = tile_k(np.concatenate([g["moe_w_group"], g["moe_w_expert"]], 1))
    for n in ("gate", "up"):
        a["w_" + n] = g["moe_w_" + n].reshape(EXPERTS, KT, P, F_EXP).transpose(0, 2, 1, 3).reshape(EXPERTS, P, -1)
    a["w_down"] = g["moe_w_down"].reshape(EXPERTS, FT, P, D).transpose(0, 2, 1, 3).reshape(EXPERTS, P, -1)
    a["final_g"] = np.asarray(i["final_norm_g"])[None]
    conv = np.concatenate([g["ssm_conv_w"], g["ssm_conv_b"][None]], 0)
    ct = conv.reshape(5, 24, P).transpose(2, 1, 0)
    order = [j for q in range(GROUPS) for j in (4 * q, 4 * q + 1, 4 * q + 2, 4 * q + 3, 16 + q, 20 + q)]

    def col(v):
        return v.reshape(-1, P).T
    a["cols"] = np.concatenate([
        col(g["norm1_g"]), col(g["att_q_norm_g"]), np.tile(g["idx_k_norm_g"], 2)[:, None],
        g["sc_conv_w"].reshape(SC_TAPS, KT, P).transpose(2, 1, 0).reshape(P, -1),
        ct[:, order, :].reshape(P, -1), col(g["ssm_norm_g"]), col(g["norm2_g"])], 1)
    a["rows"] = np.concatenate([g["att_kv_norm_g"], g["ssm_dt_bias"], g["ssm_a_log"], g["ssm_d"],
                                g["moe_b_group"], g["moe_b_expert"]])[None]
    assert a["cols"].shape == (P, NCOL) and a["rows"].shape == (1, NROW)
    return {k: np.ascontiguousarray(v) for k, v in a.items()}


def kernel(**inputs):
    import concourse.bacc as bacc
    from concourse.bass_utils import run_bass_kernel_spmd

    nc = bacc.Bacc("TRN2", target_bir_lowering=False, num_devices=1)
    arrays = {"in_" + k: v for k, v in layout(inputs).items()}
    t = {k[3:]: nc.dram_tensor(k, v.shape, mybir.dt.from_np(v.dtype), kind="ExternalInput").ap() for k, v in arrays.items()}
    t["out"] = nc.dram_tensor("out_dram", (TT, P, D), F32, kind="ExternalOutput").ap()
    build(nc, t)
    r = run_bass_kernel_spmd(nc, [arrays], core_ids=[0])
    return r.results[0]["out_dram"].reshape(1, S, D)
```

```python
from contextlib import ExitStack

import numpy as np

import concourse.bass as bass
from concourse import mybir

F32 = mybir.dt.float32
U32 = mybir.dt.uint32
I32 = mybir.dt.int32
ALU = mybir.AluOpType
ACT = mybir.ActivationFunctionType
AX_X = mybir.AxisListType.X

P = 128
D = 1024
S = 512
KT = D // P
TT = S // P
EPS = 1e-6
D_INNER = 2048
SSM_HEADS = 32
HEAD = 64
GROUPS = 4
GH = SSM_HEADS // GROUPS
TAPS = 4
SC_TAPS = 3
Q_LORA = 384
QT = Q_LORA // P
KV_LORA = 256
RT = KV_LORA // P
D_IDX = 64
IDX_HEADS = 8
KVC = KV_LORA + D_IDX + IDX_HEADS
IDX_SCALE = (IDX_HEADS * D_IDX) ** -0.5
ATT_SCALE = 64 ** -0.5
HQ = 4
TOPK = 128
BIG = 1e30
UNSEEN = -1e38
TAKEN = -3e38
EXPERTS = 16
EG = 4
F_EXP = 512
FT = F_EXP // P
EXTRA = 7
TILES = EXPERTS + EXTRA

C_G1 = 0
C_QG = C_G1 + KT
C_KG = C_QG + QT
C_SC = C_KG + 1
C_CONV = C_SC + KT * SC_TAPS
C_NG = C_CONV + GROUPS * 6 * (TAPS + 1)
C_G2 = C_NG + D_INNER // P
NCOL = C_G2 + KT
R_KVG = 0
R_DTB = R_KVG + KV_LORA
R_ALOG = R_DTB + SSM_HEADS
R_D = R_ALOG + SSM_HEADS
R_RB = R_D + SSM_HEADS
NROW = R_RB + EG + EXPERTS


class Marks:

    def __init__(self, eng, sem):
        self.eng, self.sem, self.n, self.base = eng, sem, 0, 0

    def mark(self, ins):
        ins.then_inc(self.sem, 1)
        self.n += 1

    def settle(self):
        self.eng.wait_ge(self.sem, self.base + self.n)

    def loop(self, i, per):
        self.before, self.per = self.n, per
        self.base, self.n = i * per + self.n, 0

    def end(self, reps):
        assert self.n == self.per, (self.n, self.per)
        self.base, self.n = 0, self.before + reps * self.per


def build(nc, t, debug=None):
    with ExitStack() as ctx:
        def sb(name, shape):
            return ctx.enter_context(nc.sbuf_tensor(name, shape, F32))

        sems = {}

        def sem(name):
            if name not in sems:
                sems[name] = ctx.enter_context(nc.semaphore(name))
            return sems[name]

        hT = sb("hT", [P, KT, S])
        gatedT = sb("gatedT", [P, KT, S])
        oT = sb("oT", [P, KT, S])
        WA = sb("WA", [P, 4096])
        WB = sb("WB", [P, 4096])
        WC = sb("WC", [P, 4096])
        WD = sb("WD", [P, 4096])
        arena = sb("arena", [P, 21504])
        cols = sb("cols", [P, NCOL])
        rows = sb("rows", [P, NROW])
        ident = sb("ident", [P, P])
        tri_le = sb("tri_le", [P, P])
        tri_gt = sb("tri_gt", [P, P])
        ones = sb("ones", [P, P])
        small = sb("small", [P, 256])
        dt_sb = sb("dt_sb", [P, TT, SSM_HEADS])
        da_sb = sb("da_sb", [P, TT, SSM_HEADS])
        ex_sb = sb("ex_sb", [P, 3, TT, SSM_HEADS])
        psum = [ctx.enter_context(nc.psum_tensor(f"bank{b}", [P, 512], F32)) for b in range(8)]

        h2_dram = nc.dram_tensor("h2_dram", (S, D), F32, kind="Internal").ap()
        y_dram = nc.dram_tensor("y_dram", (TILES * P, D), F32, kind="Internal").ap()
        token_of = ctx.enter_context(nc.sbuf_tensor("token_of", [P, 24], U32))
        slot_of = ctx.enter_context(nc.sbuf_tensor("slot_of", [P, 2, TT], U32))
        extra_of = ctx.enter_context(nc.sbuf_tensor("extra_of", [P, 8], I32))
        place_now = ctx.enter_context(nc.sbuf_tensor("place_now", [P, 1], U32))
        iota_i = ctx.enter_context(nc.sbuf_tensor("iota_i", [P, P + TT], I32))

        def part(at, *shape):
            n = int(np.prod(shape))
            ap = arena[:, at:at + n]
            if len(shape) == 2:
                ap = ap.rearrange("p (a b) -> p a b", a=shape[0])
            if len(shape) == 3:
                ap = ap.rearrange("p (a b c) -> p a b c", a=shape[0], b=shape[1])
            return ap, at + n

        cqT, at = part(0, QT, S)
        kvn, at = part(at, TT, KV_LORA)
        kvnT, at = part(at, RT, S)
        kidxT, at = part(at, S)
        bias, at_att = part(at, P * (1 + 2 + 3 + 4))
        BIAS_AT = [0, P, 3 * P, 6 * P]
        x_sb, at = part(at_att, TT, D)
        kvraw, at = part(at, TT, KVC)
        qraw, at = part(at, TT, Q_LORA)
        kdup, at = part(at, TT, 2 * D_IDX)
        qiT, at = part(at, 4, S)
        relu, at = part(at, 2, S)
        sc_u, at = part(at, S + SC_TAPS - 1)
        sc_v, at = part(at, S)
        sc_w, at = part(at, S)
        assert at <= 21504
        qlatT, at = part(at_att, HQ * RT, S)
        probs, at = part(at, 4, S)
        PT, at = part(at, 2, TT, HQ * P)
        assert at <= 21504
        qT = WD[:, 0:1024].rearrange("p (j s) -> p j s", j=2)
        olT = WD[:, 1024:2048].rearrange("p (j s) -> p j s", j=2)
        w_uq = WC[:, 0:768].rearrange("p (k n) -> p k n", k=QT)
        w_uk = WC[:, 768:1280].rearrange("p (j n) -> p j n", j=2)
        w_uv = WC[:, 1280:1792].rearrange("p (h r v) -> p h r v", h=HQ, r=RT)
        ynT, at_local = part(0, D_INNER // P, S)
        xsT, at = part(at_local, 6, S)
        conv, at = part(at, 2, S)
        xdt, at = part(at, TT, S)
        xend, at = part(at, 2, S)
        y, at = part(at, TT, S)
        decay, at = part(at, 2, 4, P)
        da_tri, at = part(at, 2, 4, P)
        mix_m, at = part(at, 4, 4, P)
        assert at <= 21504
        sz = WD[:, 0:2048].rearrange("p (c n) -> p c n", c=TT)
        state = WD[:, 2048:2560]
        tmp = WD[:, 2560:3072]
        b_tok = WD[:, 3072:3584]
        cb = WD[:, 3584:4096].rearrange("p (c l) -> p c l", c=TT)
        w_ssm_x = WA[:].rearrange("p (k n) -> p k n", k=KT)
        w_ssm_bc = WB[:, 0:2048].rearrange("p (k n) -> p k n", k=KT)
        w_z = WC[:].rearrange("p (k n) -> p k n", k=KT)
        mergedT, at = part(at_local, KT, S)
        sig, at = part(at, 3, S)
        branch, at = part(at, 2, S)
        x2, at_moe = part(at, TT, D)
        w_merge = WA[:].rearrange("p (k n) -> p k n", k=32)
        w_gates = WB[:, 0:3072].rearrange("p (k j n) -> p k j n", k=KT, j=3)
        w_mix = [w[:].rearrange("p (k n) -> p k n", k=KT) for w in (WC, WD)]
        h2, at = part(0, TT, D)
        h2T = hT
        f_flat, o_flat = (b[:].rearrange("p k s -> p (k s)") for b in (gatedT, oT))
        w_exp = [[w.rearrange("p (k n) -> p k n", k=k) for w, k in zip(ws, (KT, KT, FT))]
                 for ws in ((WA[:], WB[:], WC[:]), (f_flat, o_flat, arena[:, 4096:8192]))]
        gath, at = part(at_local, 2, D)
        hgT, at = part(at, 2, KT, P)
        sg, at = part(at, F_EXP)
        hid, at = part(at, F_EXP)
        hidT, at = part(at, FT, P)
        yt, at = part(at, D)
        assert at <= at_moe - TT * D
        pick = arena[:, at_local:at_local + 4 * D].rearrange("p (u m d) -> p u m d", u=2, m=2)
        w_router = WD[:, 0:KT * (EG + EXPERTS)].rearrange("p (k n) -> p k n", k=KT)
        final_g = WD[:, 1024:1024 + D]
        NR = EG + EXPERTS
        rt = at_moe
        logits, rt = part(rt, TT, NR)
        rsc, rt = part(rt, 22, TT * EXPERTS)
        first, second, chosen, place, ahead, beyond, big = (rsc[:, j, :].rearrange("p (c e) -> p c e", c=TT) for j in (1, 2, 19, 20, 21, 8, 9))
        count, extras, upto = (rsc[:, 18, 16 * j:16 * j + 16] for j in range(3))
        tile_at, place_at = (rsc[:, 4, 8 * j:8 * j + 8].rearrange("p (m c) -> p m c", m=2) for j in range(2))
        extra_at = rsc[:, 4, 16:24]
        iota_row, rt = part(rt, P)
        one_extra, rt = part(rt, EXTRA, EXPERTS)
        token_id, rt = part(rt, TT)
        at_one = 2048
        one_hot = WD[:, at_one:at_one + 8 * P].rearrange("p (a j) -> p a j", a=8)
        tile_hot = WD[:, at_one + 8 * P:at_one + 8 * P + 8 * 24].rearrange("p (a j) -> p a j", a=8)
        assert rt <= 21504

        sc_in = oT[:].rearrange("p k s -> p (k s)")[:, 0:6 * S].rearrange("p (a b c) -> p a b c", a=2, b=3)
        sq = WD[:, 3072:4096]

        wa_kv = WA[:, 0:KT * KVC].rearrange("p (k n) -> p k n", k=KT)
        wb_q = WB[:, 0:KT * Q_LORA].rearrange("p (k n) -> p k n", k=KT)
        wc_dt = WC[:, 0:KT * SSM_HEADS].rearrange("p (k n) -> p k n", k=KT)
        wd_idx = WD[:, 0:QT * 512].rearrange("p (k n) -> p k n", k=QT)
        w_sc = [w[:, 0:KT * 3 * P].rearrange("p (k j n) -> p k j n", k=KT, j=3) for w in (WA, WB)]

        ms = small[:, 0:4]
        rstd = small[:, 4:8]
        ms2 = small[:, 8:20]
        rstd2 = small[:, 20:32]
        m8 = small[:, 32:40]
        widx = small[:, 40:72].rearrange("p (t h) -> p t h", t=TT)
        powm = small[:, 72:84]
        pmax = small[:, 84:88]
        nmax = small[:, 88:92]
        psums = small[:, 92:96]
        pinv = small[:, 96:100]
        m16 = small[:, 100:104]
        r16 = small[:, 104:108]
        waited = small[:, 108:109]

        block = ctx.enter_context(nc.Block())

        @block.sync
        def _(sp):
            sp.dma_start(x_sb, t["x"].rearrange("t p d -> p t d")).then_inc(sem("x_loaded"), 16)
            sp.dma_start(cols[:], t["cols"]).then_inc(sem("params_loaded"), 16)
            sp.dma_start(rows[:], t["rows"].broadcast_to([P, NROW])).then_inc(sem("params_loaded"), 16)
            sp.dma_start(WA[:, 0:KT * KVC], t["w_kv"]).then_inc(sem("w_kv_loaded"), 16)
            sp.dma_start(WB[:, 0:KT * Q_LORA], t["w_q"]).then_inc(sem("w_q_loaded"), 16)
            sp.dma_start(WC[:, 0:KT * SSM_HEADS], t["w_dt"]).then_inc(sem("w_dt_loaded"), 16)
            sp.dma_start(WD[:, 0:QT * 512], t["w_idx"]).then_inc(sem("w_idx_loaded"), 16)
            for u in range(2):
                sp.wait_ge(sem("kq_projected"), TT * (u + 1))
                sp.dma_start([WA, WB][u][:, 0:KT * 3 * P], t["w_sc"][u]).then_inc(sem(f"w_sc{u}_loaded"), 16)
            with sp.Fori(1, KT // 2) as i:
                for u in range(2):
                    sp.wait_ge(sem("sc_projected"), i * 6 - 6 + 3 * (u + 1))
                    sp.dma_start([WA, WB][u][:, 0:KT * 3 * P], t["w_sc"][2 * i + u]).then_inc(sem(f"w_sc{u}_loaded"), 16)
            def load_heads(hg, first=False):
                if not first:
                    sp.wait_ge(sem("head_done"), hg * 14 - 4)
                sp.dma_start(WC[:, 0:1280], t["w_qk"][hg]).then_inc(sem("w_qk_loaded"), 16)
                if not first:
                    sp.wait_ge(sem("head_done"), hg * 14)
                sp.dma_start(WC[:, 1280:1792], t["w_uv"][hg]).then_inc(sem("w_uv_loaded"), 16)
            sp.wait_ge(sem("kq_projected"), 3 * TT)
            load_heads(0, first=True)
            with sp.Fori(1, TT) as hg:
                load_heads(hg)
            def load_group(g, first=False):
                if not first:
                    sp.wait_ge(sem("conv_in"), g * 6 - 2)
                sp.dma_start(WA[:], t["w_ssm_x"][g]).then_inc(sem("w_ssm_x_loaded"), 16)
                if not first:
                    sp.wait_ge(sem("conv_in"), g * 6)
                sp.dma_start(WB[:, 0:2048], t["w_ssm_bc"][g]).then_inc(sem("w_ssm_bc_loaded"), 16)
                if first:
                    sp.wait_ge(sem("head_done"), 14 * TT)
                else:
                    sp.wait_ge(sem("pair_done"), g * 12 - 8)
                sp.dma_start(WC[:], t["w_z"][g]).then_inc(sem("w_z_loaded"), 16)
            sp.wait_ge(sem("sc_projected"), 3 * KT)
            load_group(0, first=True)
            with sp.Fori(1, GROUPS) as g:
                load_group(g)
            sp.wait_ge(sem("conv_in"), 6 * GROUPS)
            sp.dma_start(WA[:], t["w_merge"][0]).then_inc(sem("w_merge_loaded"), 16)
            sp.dma_start(WB[:, 0:3072], t["w_gates"][0]).then_inc(sem("w_gates_loaded"), 16)
            sp.wait_ge(sem("pair_done"), 12 * GROUPS - 8)
            sp.dma_start(WC[:], t["w_mix"][0]).then_inc(sem("w_mix_loaded"), 16)
            sp.wait_ge(sem("y_taken"), 4 * GROUPS + 4)
            sp.dma_start(WD[:], t["w_mix"][1]).then_inc(sem("w_mix_loaded"), 16)
            sp.dma_start(x2, t["x"].rearrange("t p d -> p t d")).then_inc(sem("x_loaded"), 16)
            with sp.Fori(1, KT) as n:
                sp.wait_ge(sem("branch_done"), n * 3)
                sp.dma_start(WA[:], t["w_merge"][n]).then_inc(sem("w_merge_loaded"), 16)
                sp.wait_ge(sem("gate_done"), n * 3)
                sp.dma_start(WB[:, 0:3072], t["w_gates"][n]).then_inc(sem("w_gates_loaded"), 16)
            def flat(ap):
                return ap.rearrange("p k n -> p (k n)")
            sp.wait_ge(sem("branch_done"), KT * 3)
            sp.dma_start(WA[:], t["w_gate"][0]).then_inc(sem("w_gate0_loaded"), 16)
            sp.dma_start(flat(w_exp[1][0]), t["w_gate"][1]).then_inc(sem("w_gate1_loaded"), 16)
            sp.wait_ge(sem("gate_done"), KT * 3)
            sp.dma_start(WB[:], t["w_up"][0]).then_inc(sem("w_up0_loaded"), 16)
            sp.dma_start(flat(w_exp[1][1]), t["w_up"][1]).then_inc(sem("w_up1_loaded"), 16)
            sp.dma_start(flat(w_exp[1][2]), t["w_down"][1]).then_inc(sem("w_down1_loaded"), 16)
            sp.wait_ge(sem("mix_done"), 8)
            sp.dma_start(WC[:], t["w_down"][0]).then_inc(sem("w_down0_loaded"), 16)
            sp.dma_start(WD[:, 0:KT * (EG + EXPERTS)], t["w_router"]).then_inc(sem("w_router_loaded"), 16)
            sp.dma_start(final_g, t["final_g"].broadcast_to([P, D])).then_inc(sem("final_g_loaded"), 16)
            sp.wait_ge(sem("h2_ready"), TT)
            sp.dma_start(h2_dram.rearrange("(c p) d -> p c d", p=P), h2).then_inc(sem("h2_stored"), 16)
            for at_row, n in ((EXPERTS, TT), (EXPERTS + TT, EXTRA - TT)):
                sp.dma_start(y_dram[at_row * P:(at_row + n) * P, :].rearrange("(c p) d -> p c d", p=P), h2[:, 0:n, :]).then_inc(sem("rows_filled"), 16)
            sp.wait_ge(sem("rows_filled"), 32)
            sp.sem_inc(sem("e_y_stored"), 16)
            sp.sem_inc(sem("x_y_stored"), 16)

            def reload(T, u):
                sp.wait_ge(sem("e_gate_done"), T + 1)
                sp.dma_start(flat(w_exp[u][0]), t["w_gate"][T + 2]).then_inc(sem(f"w_gate{u}_loaded"), 16)
                sp.wait_ge(sem("e_up_done"), T + 1)
                sp.dma_start(flat(w_exp[u][1]), t["w_up"][T + 2]).then_inc(sem(f"w_up{u}_loaded"), 16)
                sp.wait_ge(sem("e_down_done"), 2 * T + 2)
                sp.dma_start(flat(w_exp[u][2]), t["w_down"][T + 2]).then_inc(sem(f"w_down{u}_loaded"), 16)

            def store_rows(T, slot, pre):
                sp.wait_ge(sem(pre + "y_taken"), 2 * T + 2 + 2)
                sp.dma_start(y_dram[bass.ds(slot * P, P), :], yt).then_inc(sem(pre + "y_stored"), 16)
            with sp.Fori(0, EXPERTS // 2 - 1) as i:
                for u in range(2):
                    reload(2 * i + u, u)
                    store_rows(2 * i + u, 2 * i + u, "e_")
            for T in (EXPERTS - 2, EXPERTS - 1):
                store_rows(T, T, "e_")
            sp.wait_ge(sem("planned"), 1)
            n_extra = sp.value_load(extra_of[0:1, 7:8], min_val=0, max_val=EXTRA)
            with sp.Fori(0, EXTRA) as x:
                with sp.If(x < n_extra):
                    e = sp.value_load(extra_of[0:1, bass.ds(x, 1)], min_val=0, max_val=EXPERTS - 1)
                    sp.wait_ge(sem("x_y_stored"), x * 16 + 16)
                    for w, b in zip(("w_gate", "w_up", "w_down"), w_exp[0]):
                        sp.dma_start(flat(b), t[w][bass.ds(e, 1)].rearrange("o p n -> p (o n)")).then_inc(sem("x_w_loaded"), 16)
                    store_rows(x, x + EXPERTS, "x_")
            sp.wait_ge(sem("e_y_stored"), EXPERTS * 16 + 16)
            sp.wait_ge(sem("x_y_stored"), n_extra * 16 + 16)
            sp.sem_inc(sem("rows_stored"), 1)
            for c in range(TT):
                sp.wait_ge(sem("out_ready"), c + 1)
                sp.dma_start(t["out"][c], x2[:, c, :]).then_inc(sem("out_stored"), 16)
            sp.wait_ge(sem("out_stored"), 16 * TT)
            if debug:
                debug(sp, sem, dict(oT=oT, ynT=ynT, x2=x2, hT=hT, cqT=cqT, kvn=kvn, kvnT=kvnT, kidxT=kidxT, bias=bias, gatedT=gatedT, dt_sb=dt_sb, ex_sb=ex_sb))

        @block.gpsimd
        def _(pool):
            def tri(ap, op, base, mult, step):
                pool.affine_select(out=ap, in_=ones[:], compare_op=op, fill=0.0, base=base,
                                   pattern=[[step, P]], channel_multiplier=mult).then_inc(sem("consts_ready"), 1)
            pool.memset(ones[:], 1.0).then_inc(sem("ones_ready"), 1)
            pool.iota(iota_i[:, 0:P], pattern=[[1, P]], base=0, channel_multiplier=0).then_inc(sem("iota_ready"), 1)
            pool.iota(iota_i[:, P:], pattern=[[P, TT]], base=0, channel_multiplier=1).then_inc(sem("iota_ready"), 1)
            pool.memset(powm, -0.5).then_inc(sem("ones_ready"), 1)
            pool.memset(sc_u, 0.0).then_inc(sem("ones_ready"), 1)
            pool.wait_ge(sem("ones_ready"), 3)
            tri(ident[:], ALU.is_equal, 0, 1, -1)
            tri(tri_le[:], ALU.is_ge, 0, -1, 1)
            tri(tri_gt[:], ALU.is_gt, 0, 1, -1)
            pool.memset(bias[:, 0:P], 0.0).then_inc(sem("bias_zero"), 1)
            pool.wait_ge(sem("bias_zero"), 1)
            pool.affine_select(out=bias[:, 0:P], in_=bias[:, 0:P], compare_op=ALU.is_ge, fill=-BIG, base=0,
                               pattern=[[-1, P]], channel_multiplier=1).then_inc(sem("consts_ready"), 1)
            pool.wait_ge(sem("ms_ready"), 1)
            pool.tensor_tensor(rstd, ms, powm[:, 0:4], ALU.pow).then_inc(sem("rstd_ready"), 1)
            pool.wait_ge(sem("ms_ready"), 2)
            pool.tensor_tensor(rstd2, ms2, powm[:, 0:12], ALU.pow).then_inc(sem("rstd_ready"), 1)
            for b in range(1, TT):
                pool.wait_ge(sem("score_ready"), b)
                dg = bias[:, BIAS_AT[b] + b * P:BIAS_AT[b] + (b + 1) * P]
                pool.affine_select(out=dg, in_=dg, compare_op=ALU.is_ge, fill=UNSEEN, base=0,
                                   pattern=[[-1, P]], channel_multiplier=1).then_inc(sem("score_hidden"), 1)
            own = Marks(pool, sem("pool_sc"))
            for u in range(2):
                pool.sem_inc(sem(f"sc_gated{u}"), 1)
            with pool.Fori(0, KT // 2) as i:
                own.loop(i, 2 * 7)
                for u in range(2):
                    b, c, x = (sc_in[:, u, j, :] for j in range(3))
                    w = [cols[:, bass.ds(C_SC + (2 * i + u) * SC_TAPS + k, 1)].to_broadcast([P, S]) for k in range(SC_TAPS)]
                    pool.wait_ge(sem(f"sc_in{u}"), i * 3 + 6)
                    own.mark(pool.tensor_tensor(sc_u[:, SC_TAPS - 1:], c, x, ALU.mult))
                    own.settle()
                    own.mark(pool.tensor_tensor(sc_v, sc_u[:, 2:2 + S], w[2], ALU.mult))
                    own.mark(pool.tensor_tensor(sc_w, sc_u[:, 1:1 + S], w[1], ALU.mult))
                    own.settle()
                    own.mark(pool.tensor_tensor(sc_v, sc_v, sc_w, ALU.add))
                    own.settle()
                    own.mark(pool.tensor_tensor(sc_w, sc_u[:, 0:S], w[0], ALU.mult))
                    own.settle()
                    own.mark(pool.tensor_tensor(sc_v, sc_v, sc_w, ALU.add))
                    own.settle()
                    own.mark(pool.tensor_tensor(sc_w, sc_v, b, ALU.mult))
                    own.settle()
                    pool.tensor_copy(gatedT[:, 2 * i + u, :], sc_w).then_inc(sem(f"sc_gated{u}"), 1)
                own.end(KT // 2)
            with pool.Fori(0, GROUPS) as g:
                def triangle(k):
                    pool.wait_ge(sem("pair_done"), g * 12 + k + 3)
                    da = da_sb[:, k // 2, bass.ds(g * GH + 4 * (k % 2), 4)].unsqueeze(2).to_broadcast([P, 4, P])
                    tri = tri_le[:].unsqueeze(1).to_broadcast([P, 4, P])
                    pool.tensor_tensor(da_tri[:, k % 2], tri, da, ALU.mult).then_inc(sem("tri_ready"), 1)
                triangle(0)
                triangle(1)
                for c in range(TT):
                    if c < TT - 1:
                        pool.wait_ge(sem("xdt_ready"), g * TT + c + 1)
                        if c == 2:
                            pool.wait_ge(sem("state_done"), g * 3 + 1)
                        ex = ex_sb[:, 1, c, bass.ds(g * GH, GH)].unsqueeze(2).to_broadcast([P, GH, HEAD])
                        pool.tensor_tensor(heads(xend[:, c % 2]), heads(xdt[:, c]), ex, ALU.mult).then_inc(sem("xend_ready"), 1)
                        triangle(2 * c + 2)
                        triangle(2 * c + 3)
                pool.wait_ge(sem("yms_ready"), g + 1)
                pool.tensor_tensor(r16, m16, powm[:, 0:4], ALU.pow).then_inc(sem("yrstd_ready"), 1)
            pool.wait_ge(sem("ms_ready"), 3)
            pool.tensor_tensor(rstd, ms, powm[:, 0:4], ALU.pow).then_inc(sem("rstd_ready"), 1)
            pool.wait_ge(sem("planned"), 1)
            pool.wait_ge(sem("h2_stored"), 16)
            for T in range(EXPERTS + 1):
                if T >= 2:
                    pool.wait_ge(sem("e_hg_turned"), T - 1)
                pool.indirect_dma_start(out=gath[:, T % 2, :], out_offset=None, in_=h2_dram,
                                        in_offset=bass.IndirectOffsetOnAxis(ap=token_of[:, T:T + 1], axis=0)
                                        ).then_inc(sem(f"e_hg{T % 2}_loaded"), 16)
            pool.wait_ge(sem("e_hg_turned"), EXPERTS + 1)
            pool.sem_inc(sem("place_ready"), 1)
            n_extra = pool.value_load(extra_of[0:1, 7:8], min_val=0, max_val=EXTRA)
            with pool.Fori(0, EXTRA) as x:
                with pool.If(x < n_extra):
                    pool.wait_ge(sem("x_hg_turned"), x + 1)
                    pool.tensor_tensor(r16, r16, r16, ALU.add)
                    pool.tensor_copy(place_now[:], token_of[:, bass.ds(x + EXPERTS, 1)]).then_inc(sem("place_ready"), 1)
                    pool.wait_ge(sem("place_ready"), x + 2)
                    pool.tensor_tensor(m16, m16, m16, ALU.add)
                    pool.indirect_dma_start(out=gath[:, 0, :], out_offset=None, in_=h2_dram,
                                            in_offset=bass.IndirectOffsetOnAxis(ap=place_now[:, 0:1], axis=0)
                                            ).then_inc(sem("x_hg0_loaded"), 16)
            pool.wait_ge(sem("rows_stored"), 1)
            pool.wait_ge(sem("e_hgT_ready"), EXPERTS + 2)
            for c in range(TT):
                if c >= 2:
                    pool.wait_ge(sem("rows_added"), 2 * c - 2)
                for m in range(2):
                    pool.indirect_dma_start(out=pick[:, c % 2, m, :], out_offset=None, in_=y_dram,
                                            in_offset=bass.IndirectOffsetOnAxis(ap=slot_of[:, m, c:c + 1], axis=0)
                                            ).then_inc(sem(f"rows{c % 2}_loaded"), 16)
            pool.wait_ge(sem("ms_ready"), 4)
            pool.tensor_tensor(rstd, ms, powm[:, 0:4], ALU.pow).then_inc(sem("rstd_ready"), 1)

        @block.tensor
        def _(pe):
            pe.wait_ge(sem("consts_ready"), 3)
            for k in range(KT):
                if k == 0:
                    pe.wait_ge(sem("xn_ready"), TT)
                for c in range(TT):
                    ins = pe.transpose(psum[k][:, c * P:(c + 1) * P], x_sb[:, c, k * P:(k + 1) * P], ident[:])
                ins.then_inc(sem("x_turned"), 1)
            for n, (w, cn, ready) in enumerate((
                    (wa_kv, KVC, "w_kv_loaded"), (wb_q, Q_LORA, "w_q_loaded"), (wc_dt, SSM_HEADS, "w_dt_loaded"))):
                pe.wait_ge(sem(ready), 16)
                if n == 0:
                    pe.wait_ge(sem("hT_ready"), KT)
                for c in range(TT):
                    b = (n * TT + c) % 8
                    if n == 2:
                        pe.wait_ge(sem("kv_taken"), c + 1)
                    for k in range(KT):
                        ins = pe.matmul(psum[b][:, 0:cn], hT[:, k, c * P:(c + 1) * P], w[:, k, :],
                                        start=k == 0, stop=k == KT - 1)
                    ins.then_inc(sem("kq_projected"), 1)
            pe.wait_ge(sem("latents_scaled"), 3)
            pe.wait_ge(sem("q_taken"), TT)
            for j in range(QT + RT + 1):
                b = 4 + j % 4
                if j >= 4:
                    pe.wait_ge(sem("latents_taken"), j - 3)
                for c in range(TT):
                    src = (qraw[:, c, j * P:(j + 1) * P] if j < QT else
                           kvn[:, c, (j - QT) * P:(j - QT + 1) * P] if j < QT + RT else kdup[:, c, :])
                    ins = pe.transpose(psum[b][:, c * P:(c + 1) * P], src, ident[:])
                ins.then_inc(sem("latents_turned"), 1)
            pe.wait_ge(sem("da_ready"), 1)
            for c in range(TT):
                for j, m in enumerate((tri_le, tri_gt, ones)):
                    ins = pe.matmul(psum[0][:, (j * TT + c) * SSM_HEADS:(j * TT + c + 1) * SSM_HEADS], m[:], da_sb[:, c, :],
                                    start=True, stop=True)
            ins.then_inc(sem("sums_ready"), 1)
            pe.wait_ge(sem("w_idx_loaded"), 16)
            pe.wait_ge(sem("latents_taken"), QT + RT + 1)
            for j in range(IDX_HEADS // 2):
                for k in range(QT):
                    ins = pe.matmul(psum[4 + j][:], wd_idx[:, k, j * P:(j + 1) * P], cqT[:, k, :], start=k == 0, stop=k == QT - 1)
                ins.then_inc(sem("qi_projected"), 1)
            pe.wait_ge(sem("qi_ready"), IDX_HEADS // 2)
            n = 0
            for b in range(1, TT):
                for h in range(IDX_HEADS):
                    if n >= 2:
                        pe.wait_ge(sem("dots_taken"), n - 1)
                    half = slice(64 * (h % 2), 64 * (h % 2) + 64)
                    pe.matmul(psum[6 + n % 2][:, 0:(b + 1) * P], qiT[half, h // 2, b * P:(b + 1) * P],
                              kidxT[half, 0:(b + 1) * P], start=True, stop=True).then_inc(sem("dots_ready"), 1)
                    n += 1
            pe.wait_ge(sem("sums_taken"), 1)
            with pe.Fori(0, KT // 2) as i:
                for u in range(2):
                    pe.wait_ge(sem(f"w_sc{u}_loaded"), i * 16 + 16)
                    for j in range(3):
                        pe.wait_ge(sem(f"sc_in{u}"), i * 3 + j + 1)
                        for k in range(KT):
                            ins = pe.matmul(psum[3 * u + j][:], w_sc[u][:, k, j, :], hT[:, k, :], start=k == 0, stop=k == KT - 1)
                        ins.then_inc(sem("sc_projected"), 1)
            for u in range(2):
                pe.wait_ge(sem(f"sc_in{u}"), 3 + 3 * KT // 2)
            with pe.Fori(0, TT) as hg:
                def head(k):
                    pe.wait_ge(sem("head_taken"), hg * 14 + k + 1)
                    return psum[k % 2]

                def half(h):
                    return slice(64 * (h % 2), 64 * (h % 2) + 64)

                def score(s):
                    b, h = s // HQ, s % HQ
                    pe.wait_ge(sem("logits_taken"), hg * 16 + s + 1)
                    for r in range(RT):
                        ins = pe.matmul(psum[2 + s % 2][:, 0:(b + 1) * P], qlatT[:, h * RT + r, b * P:(b + 1) * P],
                                        kvnT[:, r, 0:(b + 1) * P], start=r == 0, stop=r == RT - 1)
                    ins.then_inc(sem("logits_done"), 1)

                def out_heads(b):
                    pe.wait_ge(sem("olat_taken"), hg * 8 + 2 * b + 4)
                    if b == 0:
                        pe.wait_ge(sem("w_uv_loaded"), hg * 16 + 16)
                    bank = head(10 + b)
                    for h in range(HQ):
                        for r in range(RT):
                            ins = pe.matmul(bank[half(h), (h // 2) * P:(h // 2 + 1) * P], w_uv[:, h, r, :],
                                            olT[:, r, h * P:(h + 1) * P], start=r == 0, stop=r == RT - 1)
                    ins.then_inc(sem("head_done"), 1)

                pe.wait_ge(sem("w_qk_loaded"), hg * 16 + 16)
                for j in range(2):
                    bank = head(j)
                    for k in range(QT):
                        ins = pe.matmul(bank[:], w_uq[:, k, j * P:(j + 1) * P], cqT[:, k, :], start=k == 0, stop=k == QT - 1)
                    ins.then_inc(sem("head_done"), 1)
                pe.wait_ge(sem("head_taken"), hg * 14 + 2 + 2)
                for h in range(HQ):
                    for r in range(RT):
                        bank = head(2 + h * RT + r)
                        pe.matmul(bank[:], w_uk[half(h), h // 2, r * P:(r + 1) * P], qT[half(h), h // 2, :],
                                  start=True, stop=True).then_inc(sem("head_done"), 1)
                pe.wait_ge(sem("head_taken"), hg * 14 + 10 + 2)
                score(0)
                score(1)
                for s in range(16):
                    b, h = s // HQ, s % HQ
                    if s + 2 < 16:
                        score(s + 2)
                    pe.wait_ge(sem("probs_ready"), hg * 16 + s + 1)
                    pe.wait_ge(sem("turned_taken"), hg * 16 + s + 1)
                    for kb in range(b + 1):
                        ins = pe.transpose(psum[4 + s % 2][:, kb * P:(kb + 1) * P], probs[:, s % 4, kb * P:(kb + 1) * P], ident[:])
                    ins.then_inc(sem("turned"), 1)
                    if s % 4 == 1 and s > 4:
                        out_heads(s // 4 - 1)
                    if h == HQ - 1:
                        pe.wait_ge(sem("turned_taken"), hg * 16 + s + 1 + 2)
                        for r in range(RT):
                            pe.wait_ge(sem("olat_taken"), hg * 8 + 2 * b + r + 1)
                            for kb in range(b + 1):
                                ins = pe.matmul(psum[6 + r][:], kvn[:, kb, r * P:(r + 1) * P], PT[:, b % 2, kb, :],
                                                start=kb == 0, stop=kb == b)
                            ins.then_inc(sem("olat_done"), 1)
                out_heads(TT - 1)
            pe.wait_ge(sem("head_taken"), 14 * TT + 2)
            pe.wait_ge(sem("olat_taken"), 8 * TT + 2)
            with pe.Fori(0, GROUPS) as g:
                for j in range(6):
                    if j in (0, 4):
                        pe.wait_ge(sem(("w_ssm_x_loaded", "w_ssm_bc_loaded")[j // 4]), g * 16 + 16)
                    if j < 4:
                        pe.wait_ge(sem("y_taken"), g * 4 + j + 1)
                    else:
                        pe.wait_ge(sem(("btok_ready", "cb_ready")[j - 4]), g + 1)
                        if j == 4:
                            pe.wait_ge(sem("off_taken"), g * 3 + 1)
                    for k in range(KT):
                        w = w_ssm_x[:, k, j * P:(j + 1) * P] if j < 4 else w_ssm_bc[:, k, (j - 4) * P:(j - 3) * P]
                        ins = pe.matmul(psum[j][:], w, hT[:, k, :], start=k == 0, stop=k == KT - 1)
                    ins.then_inc(sem("conv_in"), 1)
                pe.wait_ge(sem("w_z_loaded"), g * 16 + 16)
                for c in range(TT):
                    pe.wait_ge(sem("pair_taken"), g * 12 + c + 1)
                    for k in range(KT):
                        ins = pe.matmul(psum[6 + c % 2][:], hT[:, k, c * P:(c + 1) * P], w_z[:, k, :], start=k == 0, stop=k == KT - 1)
                    ins.then_inc(sem("pair_done"), 1)

                def sums(k):
                    pe.wait_ge(sem("tri_ready"), g * 8 + k + 1)
                    pe.wait_ge(sem("pair_taken"), g * 12 + 4 + k + 1)
                    pe.matmul(psum[6 + k % 2][:], tri_gt[:], da_tri[:, k % 2].rearrange("p h l -> p (h l)"),
                              start=True, stop=True).then_inc(sem("pair_done"), 1)
                pe.wait_ge(sem("conv_ready"), g * 6 + 6 + 2)
                for c in range(TT):
                    for j in range(4):
                        ins = pe.transpose(psum[c][:, j * P:(j + 1) * P], xsT[:, j, c * P:(c + 1) * P], ident[:])
                    ins.then_inc(sem("x_ready"), 1)
                for c in range(TT):
                    ins = pe.transpose(psum[4][:, c * P:(c + 1) * P], xsT[:, 4, c * P:(c + 1) * P], ident[:])
                ins.then_inc(sem("b_turned"), 1)
                for c in range(TT):
                    ins = pe.matmul(psum[5][:, c * P:(c + 1) * P], xsT[:, 4, c * P:(c + 1) * P], xsT[:, 5, c * P:(c + 1) * P],
                                    start=True, stop=True)
                ins.then_inc(sem("cb_done"), 1)
                sums(0)
                sums(1)
                for c in range(TT):
                    if c < TT - 1:
                        pe.wait_ge(sem("xend_ready"), g * 3 + c + 1)
                        if c == 0:
                            pe.wait_ge(sem("btok_ready"), g + 2)
                            pe.wait_ge(sem("cb_ready"), g + 2)
                        else:
                            pe.wait_ge(sem("state_ready"), g * 3 + c)
                        sums(2 * c + 2)
                        sums(2 * c + 3)
                    if c > 0:
                        pe.wait_ge(sem("state_ready"), g * 3 + c)
                        pe.wait_ge(sem("off_taken"), g * 3 + c)
                        pe.matmul(psum[4][:], xsT[:, 5, c * P:(c + 1) * P], state, start=True, stop=True).then_inc(sem("off_done"), 1)
                    if c < TT - 1:
                        pe.matmul(psum[5][:], b_tok[:, c * P:(c + 1) * P], xend[:, c % 2], start=True, stop=True).then_inc(sem("state_done"), 1)
                    pe.wait_ge(sem("m_ready"), g * 8 + 2 * c + 2 + 2)
                    pe.wait_ge(sem("xdt_ready"), g * 4 + c + 1)
                    for h in range(GH):
                        ins = pe.matmul(psum[c][:, h * HEAD:(h + 1) * HEAD], mix_m[:, (2 * c + h // 4) % 4, h % 4, :],
                                        xdt[:, c, h * HEAD:(h + 1) * HEAD], start=True, stop=True)
                    ins.then_inc(sem("diag_done"), 1)
                pe.wait_ge(sem("yn_ready"), g * 4 + 4)
                for j in range(4):
                    for c in range(TT):
                        ins = pe.transpose(psum[j][:, c * P:(c + 1) * P], y[:, c, j * P:(j + 1) * P], ident[:])
                    ins.then_inc(sem("y_turned"), 1)
            pe.wait_ge(sem("y_taken"), 4 * GROUPS + 4)
            for u in range(2):
                pe.wait_ge(sem(f"sc_gated{u}"), KT // 2 + 1)
            with pe.Fori(0, KT) as n:
                pe.wait_ge(sem("w_merge_loaded"), n * 16 + 16)
                for j, (at_k, kn, src) in enumerate(((0, 16, ynT), (16, KT, gatedT), (24, KT, oT))):
                    pe.wait_ge(sem("branch_taken"), n * 3 + j + 1)
                    for k in range(kn):
                        ins = pe.matmul(psum[j][:], w_merge[:, at_k + k, :], src[:, k, :], start=k == 0, stop=k == kn - 1)
                    ins.then_inc(sem("branch_done"), 1)
                pe.wait_ge(sem("w_gates_loaded"), n * 16 + 16)
                for j in range(3):
                    pe.wait_ge(sem("gate_taken"), n * 3 + j + 1)
                    for k in range(KT):
                        ins = pe.matmul(psum[3 + j][:], w_gates[:, k, j, :], hT[:, k, :], start=k == 0, stop=k == KT - 1)
                    ins.then_inc(sem("gate_done"), 1)
            pe.wait_ge(sem("w_mix_loaded"), 32)
            pe.wait_ge(sem("merged"), KT + 1)
            for b in range(8):
                c, half = b // 2, b % 2
                for k in range(KT):
                    ins = pe.matmul(psum[b][:], mergedT[:, k, c * P:(c + 1) * P], w_mix[half][:, k, :], start=k == 0, stop=k == KT - 1)
                ins.then_inc(sem("mix_done"), 1)
            pe.wait_ge(sem("h2_ready"), TT)
            for k in range(KT):
                for c in range(TT):
                    ins = pe.transpose(psum[k][:, c * P:(c + 1) * P], h2[:, c, k * P:(k + 1) * P], ident[:])
                ins.then_inc(sem("h2_turned"), 1)
            pe.wait_ge(sem("h2T_ready"), KT)
            pe.wait_ge(sem("w_router_loaded"), 16)
            for c in range(TT):
                for k in range(KT):
                    ins = pe.matmul(psum[7][:, c * NR:(c + 1) * NR], h2T[:, k, c * P:(c + 1) * P], w_router[:, k, :],
                                    start=k == 0, stop=k == KT - 1)
            ins.then_inc(sem("routed"), 1)
            pe.wait_ge(sem("chosen"), 1)
            for c in range(TT):
                for d in range(c + 1):
                    pe.matmul(psum[4][:, c * EXPERTS:(c + 1) * EXPERTS], (tri_le if d == c else ones)[:], chosen[:, d, :],
                              start=d == 0, stop=d == c)
            for c in range(TT):
                ins = pe.matmul(psum[4][:, TT * EXPERTS:(TT + 1) * EXPERTS], ones[:], chosen[:, c, :], start=c == 0, stop=c == TT - 1)
            ins.then_inc(sem("counted"), 1)
            pe.wait_ge(sem("one_hot_ready"), 8)
            for a in range(8):
                ins = pe.matmul(psum[5][:, 0:24], one_hot[:, a, :], tile_hot[:, a, :], start=a == 0, stop=a == 7)
            ins.then_inc(sem("placed"), 1)

            def turn_tokens(T, u, loaded, pre):
                pe.wait_ge(sem(f"{pre}hg{u}_loaded"), loaded)
                pe.wait_ge(sem(pre + "hgT_ready"), T + 1)
                for k in range(KT):
                    ins = pe.transpose(psum[2 + k // 4][:, k % 4 * P:(k % 4 + 1) * P], gath[:, u, k * P:(k + 1) * P], ident[:])
                ins.then_inc(sem(pre + "hg_turned"), 1)

            def expert_tile(T, u, pre, loads, between):
                pe.wait_ge(sem(pre + "hgT_ready"), T + 2)
                for j, name in enumerate(("gate", "up")):
                    pe.wait_ge(sem(loads[j][0]), loads[j][1])
                    pe.wait_ge(sem(pre + ("sg_ready", "hid_ready")[j]), T + 1)
                    for k in range(KT):
                        ins = pe.matmul(psum[j][:], hgT[:, u, k, :], w_exp[u][j][:, k, :], start=k == 0, stop=k == KT - 1)
                    ins.then_inc(sem(f"{pre}{name}_done"), 1)
                between()
                pe.wait_ge(sem(pre + "hid_ready"), T + 2)
                pe.wait_ge(sem(pre + "hidT_ready"), T + 1)
                for f in range(FT):
                    ins = pe.transpose(psum[4][:, f * P:(f + 1) * P], hid[:, f * P:(f + 1) * P], ident[:])
                ins.then_inc(sem(pre + "hid_turned"), 1)
                pe.wait_ge(sem(pre + "hidT_ready"), T + 2)
                pe.wait_ge(sem(loads[2][0]), loads[2][1])
                for half in range(2):
                    pe.wait_ge(sem(pre + "y_taken"), 2 * T + half + 1)
                    for f in range(FT):
                        ins = pe.matmul(psum[5 + half][:], hidT[:, f, :], w_exp[u][2][:, f, half * 512:(half + 1) * 512],
                                        start=f == 0, stop=f == FT - 1)
                    ins.then_inc(sem(pre + "down_done"), 1)
            pe.wait_ge(sem("planned"), 1)
            turn_tokens(0, 0, 16, "e_")
            with pe.Fori(0, EXPERTS // 2) as i:
                for u in range(2):
                    T = 2 * i + u
                    expert_tile(T, u, "e_", [(f"w_{w}{u}_loaded", i * 16 + 16) for w in ("gate", "up", "down")],
                                lambda: turn_tokens(T + 1, 1 - u, i * 16 + 16 + 16 * u, "e_"))
            n_extra = pe.value_load(extra_of[0:1, 7:8], min_val=0, max_val=EXTRA)
            with pe.Fori(0, EXTRA) as x:
                with pe.If(x < n_extra):
                    turn_tokens(x, 0, x * 16 + 16, "x_")
                    expert_tile(x, 0, "x_", [("x_w_loaded", x * 48 + 48)] * 3, lambda: None)

        @block.scalar
        def _(act):
            act.wait_ge(sem("params_loaded"), 32)
            for k in range(KT):
                act.wait_ge(sem("x_turned"), k + 1)
                act.activation(hT[:, k, :], psum[k][:], ACT.Copy, scale=cols[:, C_G1 + k:C_G1 + k + 1]).then_inc(sem("hT_ready"), 1)
            for c in range(TT):
                act.wait_ge(sem("kq_projected"), c + 1)
                act.activation(kvraw[:, c, :], psum[c][:, 0:KVC], ACT.Copy).then_inc(sem("kv_taken"), 1)
            for c in range(TT):
                act.wait_ge(sem("kq_projected"), TT + c + 1)
                act.activation(qraw[:, c, :], psum[4 + c][:, 0:Q_LORA], ACT.Copy).then_inc(sem("q_taken"), 1)
            act.wait_ge(sem("dtabs_ready"), 1)
            act.activation(da_sb[:], da_sb[:], ACT.Exp, scale=-1.0).then_inc(sem("dtexp_ready"), 1)
            act.activation(rows[:, R_ALOG:R_ALOG + SSM_HEADS], rows[:, R_ALOG:R_ALOG + SSM_HEADS], ACT.Exp).then_inc(sem("dtexp_ready"), 1)
            for j in range(QT + RT + 1):
                act.wait_ge(sem("latents_turned"), j + 1)
                src = psum[4 + j % 4][:]
                if j < QT:
                    ins = act.activation(cqT[:, j, :], src, ACT.Copy, scale=cols[:, C_QG + j:C_QG + j + 1])
                elif j < QT + RT:
                    ins = act.activation(kvnT[:, j - QT, :], src, ACT.Copy)
                else:
                    ins = act.activation(kidxT, src, ACT.Copy, scale=cols[:, C_KG:C_KG + 1])
                ins.then_inc(sem("latents_taken"), 1)
            act.wait_ge(sem("sums_ready"), 1)
            act.activation(ex_sb[:].rearrange("p a c h -> p (a c h)"), psum[0][:, 0:3 * TT * SSM_HEADS], ACT.Exp).then_inc(sem("sums_taken"), 1)
            for j in range(IDX_HEADS // 2):
                act.wait_ge(sem("qi_projected"), j + 1)
                act.activation(qiT[:, j, :], psum[4 + j][:], ACT.Copy).then_inc(sem("qi_ready"), 1)
            n = 0
            for b in range(1, TT):
                for h in range(IDX_HEADS):
                    act.wait_ge(sem("dots_ready"), n + 1)
                    if n >= 2:
                        act.wait_ge(sem("score_added"), n - 1)
                    act.activation(relu[:, n % 2, 0:(b + 1) * P], psum[6 + n % 2][:, 0:(b + 1) * P], ACT.Relu).then_inc(sem("dots_taken"), 1)
                    n += 1
            for u in range(2):
                act.sem_inc(sem(f"sc_in{u}"), 3)
            with act.Fori(0, KT // 2) as i:
                for u in range(2):
                    act.wait_ge(sem(f"sc_gated{u}"), i + 1)
                    for j in range(3):
                        act.wait_ge(sem("sc_projected"), i * 6 + 3 * u + j + 1)
                        act.activation(sc_in[:, u, j, :], psum[3 * u + j][:], ACT.Copy).then_inc(sem(f"sc_in{u}"), 1)
            act.wait_ge(sem("bias_ready"), TT - 1)
            for u in range(2):
                act.wait_ge(sem(f"sc_gated{u}"), KT // 2 + 1)
            act.sem_inc(sem("head_taken"), 2)
            act.sem_inc(sem("turned_taken"), 2)
            with act.Fori(0, TT) as hg:
                def take_head(k):
                    act.wait_ge(sem("head_done"), hg * 14 + k + 1)
                    if k < 2:
                        ins = act.activation(qT[:, k, :], psum[k][:], ACT.Copy)
                    elif k < 10:
                        ins = act.activation(qlatT[:, k - 2, :], psum[k % 2][:], ACT.Copy)
                    else:
                        b = k - 10
                        ins = act.activation(oT[:, bass.ds(hg * 2, 2), b * P:(b + 1) * P],
                                             psum[k % 2][:, 0:2 * P].rearrange("p (j q) -> p j q", j=2), ACT.Copy)
                    ins.then_inc(sem("head_taken"), 1)

                def take_turned(s):
                    b, h = s // HQ, s % HQ
                    act.wait_ge(sem("turned"), hg * 16 + s + 1)
                    act.activation(PT[:, b % 2, 0:b + 1, h * P:(h + 1) * P],
                                   psum[4 + s % 2][:, 0:(b + 1) * P].rearrange("p (k q) -> p k q", k=b + 1), ACT.Copy
                                   ).then_inc(sem("turned_taken"), 1)
                for k in range(10):
                    take_head(k)
                for s in range(16):
                    b = s // HQ
                    act.wait_ge(sem("max_ready"), hg * 16 + s + 1)
                    pr = probs[:, s % 4, 0:(b + 1) * P]
                    act.activation(pr, pr, ACT.Exp, bias=nmax[:, s % 4:s % 4 + 1], scale=ATT_SCALE,
                                   accum_out=psums[:, s % 4:s % 4 + 1]).then_inc(sem("exp_done"), 1)
                    if s >= 1:
                        take_turned(s - 1)
                    if s >= 6 and s % 4 == 2:
                        take_head(10 + (s - 6) // 4)
                take_turned(15)
                take_head(13)
            act.sem_inc(sem("y_taken"), 4)
            act.sem_inc(sem("btok_ready"), 1)
            act.sem_inc(sem("pair_taken"), 2)
            act.sem_inc(sem("conv_ready"), 2)
            act.wait_ge(sem("olat_taken"), 8 * TT + 2)
            with act.Fori(0, GROUPS) as g:
                for j in range(6):
                    act.wait_ge(sem("conv_out"), g * 6 + j + 1)
                    act.activation(xsT[:, j, :], conv[:, j % 2], ACT.Silu,
                                   bias=cols[:, bass.ds(C_CONV + TAPS + g * 30 + j * 5, 1)]).then_inc(sem("conv_ready"), 1)
                for c in range(TT):
                    act.wait_ge(sem("pair_done"), g * 12 + c + 1)
                    act.activation(sz[:, c, :], psum[6 + c % 2][:], ACT.Silu).then_inc(sem("pair_taken"), 1)
                act.wait_ge(sem("b_turned"), g + 1)
                act.activation(b_tok, psum[4][:], ACT.Copy).then_inc(sem("btok_ready"), 1)
                for k in range(8):
                    act.wait_ge(sem("pair_done"), g * 12 + 4 + k + 1)
                    act.wait_ge(sem("m_ready"), g * 8 + k + 1)
                    act.activation(decay[:, k % 2].rearrange("p h l -> p (h l)"), psum[6 + k % 2][:], ACT.Exp).then_inc(sem("pair_taken"), 1)
                for j in range(4):
                    act.wait_ge(sem("y_turned"), g * 4 + j + 1)
                    act.activation(ynT[:, bass.ds(g * 4 + j, 1), :].rearrange("p o s -> p (o s)"), psum[j][:], ACT.Copy,
                                   scale=cols[:, bass.ds(C_NG + g * 4 + j, 1)]).then_inc(sem("y_taken"), 1)
            act.sem_inc(sem("gate_taken"), 3)
            with act.Fori(0, KT) as n:
                for j in range(3):
                    act.wait_ge(sem("gate_done"), n * 3 + j + 1)
                    act.wait_ge(sem("branch_taken"), n * 3 + j + 1)
                    act.activation(sig[:, j, :], psum[3 + j][:], ACT.Sigmoid).then_inc(sem("gate_taken"), 1)
            for k in range(KT):
                act.wait_ge(sem("h2_turned"), k + 1)
                act.activation(h2T[:, k, :], psum[k][:], ACT.Copy, scale=cols[:, C_G2 + k:C_G2 + k + 1]).then_inc(sem("h2T_ready"), 1)
            act.wait_ge(sem("rt_in"), 1)
            act.activation(rsc[:, 2, 0:16], rsc[:, 1, 0:16], ACT.Exp).then_inc(sem("rt_exp"), 1)
            act.wait_ge(sem("rt_in"), 2)
            act.activation(rsc[:, 10, 0:4], rsc[:, 10, 0:4], ACT.Exp).then_inc(sem("rt_exp"), 1)
            def expert_tile(T, pre):
                act.wait_ge(sem(pre + "gate_done"), T + 1)
                act.wait_ge(sem(pre + "hid_ready"), T + 1)
                act.activation(sg, psum[0][:], ACT.Silu).then_inc(sem(pre + "sg_ready"), 1)
                act.wait_ge(sem(pre + "hid_turned"), T + 1)
                act.activation(hidT.rearrange("p f j -> p (f j)"), psum[4][:], ACT.Copy).then_inc(sem(pre + "hidT_ready"), 1)
                for half in range(2):
                    act.wait_ge(sem(pre + "down_done"), 2 * T + half + 1)
                    if half == 0:
                        act.wait_ge(sem(pre + "y_stored"), T * 16 + 16)
                    act.activation(yt[:, half * 512:(half + 1) * 512], psum[5 + half][:], ACT.Copy).then_inc(sem(pre + "y_taken"), 1)
            act.wait_ge(sem("planned"), 1)
            for pre in ("e_", "x_"):
                act.sem_inc(sem(pre + "sg_ready"), 1)
                act.sem_inc(sem(pre + "hidT_ready"), 1)
                act.sem_inc(sem(pre + "y_taken"), 2)
            with act.Fori(0, EXPERTS) as T:
                expert_tile(T, "e_")
            act.wait_ge(sem("e_y_stored"), EXPERTS * 16 + 16)
            n_extra = act.value_load(extra_of[0:1, 7:8], min_val=0, max_val=EXTRA)
            with act.Fori(0, EXTRA) as x:
                with act.If(x < n_extra):
                    expert_tile(x, "x_")

        @block.vector
        def _(dve):
            own = Marks(dve, sem("dve_own"))
            dve.wait_ge(sem("x_loaded"), 16)
            for c in range(TT):
                own.mark(dve.tensor_tensor_reduce(sq, x_sb[:, c, :], x_sb[:, c, :], 1.0, 0.0, ALU.mult, ALU.add, ms[:, c:c + 1]))
                own.settle()
            dve.tensor_scalar(ms, ms, 1.0 / D, EPS, ALU.mult, ALU.add).then_inc(sem("ms_ready"), 1)
            dve.wait_ge(sem("rstd_ready"), 1)
            for c in range(TT):
                dve.tensor_scalar(x_sb[:, c, :], x_sb[:, c, :], rstd[:, c:c + 1], None, ALU.mult).then_inc(sem("xn_ready"), 1)
            dve.wait_ge(sem("kv_taken"), TT)
            dve.wait_ge(sem("params_loaded"), 32)
            for c in range(TT):
                a = kvraw[:, c, 0:KV_LORA]
                own.mark(dve.tensor_tensor_reduce(sq[:, 0:KV_LORA], a, a, 1.0, 0.0, ALU.mult, ALU.add, ms2[:, 4 + c:5 + c]))
                a = kvraw[:, c, KV_LORA:KV_LORA + D_IDX]
                own.mark(dve.tensor_tensor_reduce(sq[:, 256:256 + D_IDX], a, a, 1.0, 0.0, ALU.mult, ALU.add, ms2[:, 8 + c:9 + c]))
                own.settle()
            dve.wait_ge(sem("q_taken"), TT)
            for c in range(TT):
                own.mark(dve.tensor_tensor_reduce(sq[:, 0:Q_LORA], qraw[:, c, :], qraw[:, c, :], 1.0, 0.0, ALU.mult, ALU.add, ms2[:, c:c + 1]))
                own.settle()
            own.mark(dve.tensor_scalar(ms2[:, 0:4], ms2[:, 0:4], 1.0 / Q_LORA, EPS, ALU.mult, ALU.add))
            own.mark(dve.tensor_scalar(ms2[:, 4:8], ms2[:, 4:8], 1.0 / KV_LORA, EPS, ALU.mult, ALU.add))
            dve.tensor_scalar(ms2[:, 8:12], ms2[:, 8:12], 1.0 / D_IDX, EPS, ALU.mult, ALU.add).then_inc(sem("ms_ready"), 1)
            own.settle()
            dtb = rows[:, R_DTB:R_DTB + SSM_HEADS]
            for c in range(TT):
                dve.wait_ge(sem("kq_projected"), 2 * TT + c + 1)
                own.mark(dve.tensor_tensor(dt_sb[:, c, :], psum[c][:, 0:SSM_HEADS], dtb, ALU.add))
            own.settle()
            own.mark(dve.tensor_scalar(da_sb[:], dt_sb[:], -1.0, None, ALU.mult))
            own.settle()
            dve.tensor_tensor(da_sb[:], da_sb[:], dt_sb[:], ALU.max).then_inc(sem("dtabs_ready"), 1)
            dve.wait_ge(sem("rstd_ready"), 2)
            for c in range(TT):
                own.mark(dve.tensor_scalar(qraw[:, c, :], qraw[:, c, :], rstd2[:, c:c + 1], None, ALU.mult))
                own.mark(dve.scalar_tensor_tensor(out=kvn[:, c, :], in0=kvraw[:, c, 0:KV_LORA], scalar=rstd2[:, 4 + c:5 + c],
                                                  in1=rows[:, R_KVG:R_KVG + KV_LORA], op0=ALU.mult, op1=ALU.mult))
                for u in range(2):
                    own.mark(dve.tensor_scalar(kdup[:, c, u * D_IDX:(u + 1) * D_IDX], kvraw[:, c, KV_LORA:KV_LORA + D_IDX],
                                               rstd2[:, 8 + c:9 + c], None, ALU.mult))
            own.settle()
            dve.tensor_scalar(widx, kvraw[:, :, KV_LORA + D_IDX:KVC], IDX_SCALE, None, ALU.mult).then_inc(sem("latents_scaled"), 3)
            dve.wait_ge(sem("dtexp_ready"), 2)
            lu, ls, lp = da_sb[:], relu_tmp(relu, 0), relu_tmp(relu, 1)
            ls2 = relu_tmp(relu, 2)
            own.mark(dve.tensor_scalar(ls, lu, 2.0, None, ALU.add))
            own.settle()
            own.mark(dve.reciprocal(ls, ls))
            own.settle()
            own.mark(dve.tensor_tensor(ls, lu, ls, ALU.mult))
            own.settle()
            own.mark(dve.tensor_tensor(ls2, ls, ls, ALU.mult))
            own.settle()
            own.mark(dve.tensor_scalar(lp, ls2, 1.0 / 15, 1.0 / 13, ALU.mult, ALU.add))
            own.settle()
            for d in (11, 9, 7, 5, 3, 1):
                own.mark(dve.tensor_tensor(lp, lp, ls2, ALU.mult))
                own.settle()
                own.mark(dve.tensor_scalar(lp, lp, 1.0 / d, None, ALU.add))
                own.settle()
            own.mark(dve.scalar_tensor_tensor(out=lp, in0=lp, scalar=2.0, in1=ls, op0=ALU.mult, op1=ALU.mult))
            own.settle()
            own.mark(dve.scalar_tensor_tensor(out=dt_sb[:], in0=dt_sb[:], scalar=0.0, in1=lp, op0=ALU.max, op1=ALU.add))
            own.settle()
            ea = rows[:, R_ALOG:R_ALOG + SSM_HEADS].unsqueeze(1).to_broadcast([P, TT, SSM_HEADS])
            dve.scalar_tensor_tensor(out=da_sb[:], in0=dt_sb[:], scalar=-1.0, in1=ea, op0=ALU.mult, op1=ALU.mult).then_inc(sem("da_ready"), 1)
            n = 0
            for b in range(1, TT):
                sc = bias[:, BIAS_AT[b]:BIAS_AT[b] + (b + 1) * P]
                for h in range(IDX_HEADS):
                    dve.wait_ge(sem("dots_taken"), n + 1)
                    r = relu[:, n % 2, 0:(b + 1) * P]
                    if h == 0:
                        ins = dve.tensor_scalar(sc, r, widx[:, b, h:h + 1], None, ALU.mult)
                    else:
                        dve.wait_ge(sem("score_added"), n)
                        ins = dve.scalar_tensor_tensor(out=sc, in0=r, scalar=widx[:, b, h:h + 1], in1=sc, op0=ALU.mult, op1=ALU.add)
                    ins.then_inc(sem("score_added"), 1)
                    n += 1
                dve.wait_ge(sem("score_added"), n)
                dve.engine_nop().then_inc(sem("score_ready"), 1)
            for b in range(1, TT):
                sc = bias[:, BIAS_AT[b]:BIAS_AT[b] + (b + 1) * P]
                dve.wait_ge(sem("score_hidden"), b)
                for r in range(TOPK // 8):
                    own.mark(dve.max(m8, sc))
                    own.settle()
                    own.mark(dve.match_replace(sc, m8, sc, TAKEN))
                    own.settle()
                dve.tensor_scalar(sc, sc, 0.5 * (UNSEEN + TAKEN), -BIG, ALU.is_gt, ALU.mult).then_inc(sem("bias_ready"), 1)
            for u in range(2):
                dve.wait_ge(sem(f"sc_gated{u}"), KT // 2 + 1)
            dve.wait_ge(sem("consts_ready"), 4)
            dve.sem_inc(sem("logits_taken"), 2)
            dve.sem_inc(sem("olat_taken"), 2)
            with dve.Fori(0, TT) as hg:
                def largest(s):
                    b = s // HQ
                    n = (b + 1) * P
                    dve.wait_ge(sem("logits_done"), hg * 16 + s + 1)
                    dve.memset(waited, 0.0)
                    dve.tensor_tensor_reduce(probs[:, s % 4, 0:n], psum[2 + s % 2][:, 0:n], bias[:, BIAS_AT[b]:BIAS_AT[b] + n],
                                             1.0, TAKEN, ALU.add, ALU.max, pmax[:, s % 4:s % 4 + 1]).then_inc(sem("logits_taken"), 1)
                    dve.wait_ge(sem("logits_taken"), hg * 16 + s + 1 + 2)
                    dve.tensor_scalar(nmax[:, s % 4:s % 4 + 1], pmax[:, s % 4:s % 4 + 1], -ATT_SCALE, None, ALU.mult).then_inc(sem("max_ready"), 1)

                def divide(s):
                    n = (s // HQ + 1) * P
                    dve.wait_ge(sem("exp_done"), hg * 16 + s + 1)
                    dve.reciprocal(pinv[:, s % 4:s % 4 + 1], psums[:, s % 4:s % 4 + 1]).then_inc(sem("pinv_ready"), 1)
                    dve.wait_ge(sem("pinv_ready"), hg * 16 + s + 1)
                    pr = probs[:, s % 4, 0:n]
                    dve.tensor_scalar(pr, pr, pinv[:, s % 4:s % 4 + 1], None, ALU.mult).then_inc(sem("probs_ready"), 1)

                def take_olat(b):
                    for r in range(RT):
                        dve.wait_ge(sem("olat_done"), hg * 8 + 2 * b + r + 1)
                        dve.tensor_copy(olT[:, r, :], psum[6 + r][:]).then_inc(sem("olat_taken"), 1)
                for s in range(17):
                    if s < 16:
                        largest(s)
                    if s >= 1:
                        divide(s - 1)
                    if s % 4 == 1 and s > 4:
                        take_olat(s // 4 - 1)
                take_olat(TT - 1)
            dve.wait_ge(sem("head_done"), 14 * TT)
            dve.sem_inc(sem("cb_ready"), 1)
            dve.sem_inc(sem("m_ready"), 2)
            dve.sem_inc(sem("off_taken"), 1)
            with dve.Fori(0, GROUPS) as g:
                own.loop(i=g, per=6 * 3 + 3 * TT + 3 + 2)
                for j in range(6):
                    w = [cols[:, bass.ds(C_CONV + k + g * 30 + j * 5, 1)] for k in range(TAPS)]
                    a, src = conv[:, j % 2], psum[j][:]
                    dve.wait_ge(sem("conv_in"), g * 6 + j + 1)
                    dve.wait_ge(sem("conv_ready"), g * 6 + j + 1)
                    own.mark(dve.tensor_scalar(a, src, w[3], None, ALU.mult))
                    for d in (1, 2, 3):
                        own.settle()
                        ins = dve.scalar_tensor_tensor(out=a[:, d:], in0=src[:, 0:S - d], scalar=w[3 - d], in1=a[:, d:], op0=ALU.mult, op1=ALU.add)
                        if d < 3:
                            own.mark(ins)
                    ins.then_inc(sem("conv_out"), 1)
                hs = bass.ds(g * GH, GH)
                dskip = rows[:, bass.ds(R_D + g * GH, GH)].unsqueeze(2).to_broadcast([P, GH, HEAD])
                dve.wait_ge(sem("x_ready"), g * 4 + 4)
                for c in range(TT):
                    dve.tensor_tensor(heads(y[:, c]), heads(psum[c][:]), dskip, ALU.mult)
                    dve.tensor_tensor(heads(xdt[:, c]), heads(psum[c][:]), dt_sb[:, c, hs].unsqueeze(2).to_broadcast([P, GH, HEAD]),
                                      ALU.mult).then_inc(sem("xdt_ready"), 1)
                dve.wait_ge(sem("cb_done"), g + 1)
                dve.tensor_tensor(cb, psum[5][:].rearrange("p (c l) -> p c l", c=TT), tri_le[:].unsqueeze(1).to_broadcast([P, TT, P]),
                                  ALU.mult).then_inc(sem("cb_ready"), 1)
                dve.wait_ge(sem("cb_ready"), g + 2)
                dve.wait_ge(sem("xdt_ready"), g * 4 + 4)
                for c in range(TT):
                    for k in (2 * c, 2 * c + 1):
                        dve.wait_ge(sem("pair_taken"), g * 12 + 4 + k + 1 + 2)
                        dve.tensor_tensor(mix_m[:, k % 4], decay[:, k % 2], cb[:, c, :].unsqueeze(1).to_broadcast([P, 4, P]),
                                          ALU.mult).then_inc(sem("m_ready"), 1)
                    if c < TT - 1:
                        dve.wait_ge(sem("state_done"), g * 3 + c + 1)
                        if c == 0:
                            dve.tensor_copy(state, psum[5][:]).then_inc(sem("state_ready"), 1)
                        else:
                            dve.wait_ge(sem("off_done"), g * 3 + c)
                            cd = ex_sb[:, 2, c, hs].unsqueeze(2).to_broadcast([P, GH, HEAD])
                            own.mark(dve.tensor_tensor(heads(state), heads(state), cd, ALU.mult))
                            own.settle()
                            dve.tensor_tensor(state, state, psum[5][:], ALU.add).then_inc(sem("state_ready"), 1)
                    dve.wait_ge(sem("diag_done"), g * 4 + c + 1)
                    own.mark(dve.tensor_tensor(y[:, c], y[:, c], psum[c][:], ALU.add))
                    if c > 0:
                        dve.wait_ge(sem("off_done"), g * 3 + c)
                        ec = ex_sb[:, 0, c, hs].unsqueeze(2).to_broadcast([P, GH, HEAD])
                        dve.tensor_tensor(heads(tmp), heads(psum[4][:]), ec, ALU.mult).then_inc(sem("off_taken"), 1)
                        own.settle()
                        dve.wait_ge(sem("off_taken"), g * 3 + c + 1)
                        own.mark(dve.tensor_tensor(y[:, c], y[:, c], tmp, ALU.add))
                    own.settle()
                    own.mark(dve.tensor_tensor(y[:, c], y[:, c], sz[:, c, :], ALU.mult))
                    own.settle()
                    own.mark(dve.tensor_tensor_reduce(tmp, y[:, c], y[:, c], 1.0, 0.0, ALU.mult, ALU.add, m16[:, c:c + 1]))
                    own.settle()
                dve.tensor_scalar(m16, m16, 1.0 / 512, EPS, ALU.mult, ALU.add).then_inc(sem("yms_ready"), 1)
                dve.wait_ge(sem("yrstd_ready"), g + 1)
                for c in range(TT):
                    dve.tensor_scalar(y[:, c], y[:, c], r16[:, c:c + 1], None, ALU.mult).then_inc(sem("yn_ready"), 1)
                own.end(GROUPS)
            dve.wait_ge(sem("y_taken"), 4 * GROUPS + 4)
            dve.sem_inc(sem("branch_taken"), 3)
            dve.sem_inc(sem("merged"), 1)
            with dve.Fori(0, KT) as n:
                own.loop(n, 1)
                dve.wait_ge(sem("merged"), n + 1)
                for j in range(3):
                    dve.wait_ge(sem("branch_done"), n * 3 + j + 1)
                    dve.wait_ge(sem("gate_taken"), n * 3 + j + 1 + 3)
                    dve.tensor_tensor(branch[:, min(j, 1)], psum[j][:], sig[:, j, :], ALU.mult).then_inc(sem("branch_taken"), 1)
                    dve.wait_ge(sem("branch_taken"), n * 3 + j + 1 + 3)
                    if j == 1:
                        own.mark(dve.tensor_tensor(branch[:, 0], branch[:, 0], branch[:, 1], ALU.add))
                        own.settle()
                    if j == 2:
                        dve.tensor_tensor(mergedT[:, bass.ds(n, 1), :].rearrange("p o s -> p (o s)"), branch[:, 0], branch[:, 1],
                                          ALU.add).then_inc(sem("merged"), 1)
                own.end(KT)
            dve.wait_ge(sem("x_loaded"), 32)
            for b in range(8):
                c, half = b // 2, b % 2
                dve.wait_ge(sem("mix_done"), b + 1)
                a = x2[:, c, half * 512:(half + 1) * 512]
                own.mark(dve.tensor_tensor(a, a, psum[b][:], ALU.add))
            own.settle()

            def mean_squares(name):
                for c in range(TT):
                    own.mark(dve.tensor_tensor_reduce(h2[:, c, :], x2[:, c, :], x2[:, c, :], 1.0, 0.0, ALU.mult, ALU.add, ms[:, c:c + 1]))
                own.settle()
                dve.tensor_scalar(ms, ms, 1.0 / D, EPS, ALU.mult, ALU.add).then_inc(sem(name), 1)
            mean_squares("ms_ready")
            dve.wait_ge(sem("rstd_ready"), 3)
            for c in range(TT):
                dve.tensor_scalar(h2[:, c, :], x2[:, c, :], rstd[:, c:c + 1], None, ALU.mult).then_inc(sem("h2_ready"), 1)
            def do(ins):
                own.mark(ins)
                own.settle()

            def b4(ap, inner):
                return ap.unsqueeze(len(ap.shape)).to_broadcast(list(ap.shape) + [inner])

            def first_of(out, val, largest, tmp4):
                do(dve.tensor_tensor(tmp4, val, b4(largest, 4), ALU.is_equal))
                for j in range(4):
                    do(dve.tensor_scalar(tmp4[:, :, j], tmp4[:, :, j], float(4 - j), None, ALU.mult))
                do(dve.tensor_reduce(r1, tmp4, AX_X, ALU.max))
                do(dve.tensor_tensor(out, tmp4, b4(r1, 4), ALU.is_equal))

            def r4(j):
                return rsc[:, j, 0:TT * 4].rearrange("p (c g) -> p c g", c=TT)
            r1, gmax, l1, l2, pg, g1, g2 = (rsc[:, 11 + j, 0:TT] for j in range(7))
            glog, ohg, t4, ing, oh1, oh2, gx, t4b = (r4(j) for j in (0, 3, 4, 5, 6, 7, 1, 8))
            big16 = rsc[:, 18, :].rearrange("p (c j g) -> p c j g", c=TT, j=4)
            dve.wait_ge(sem("routed"), 1)
            dve.tensor_tensor(logits, psum[7][:, 0:TT * NR].rearrange("p (c n) -> p c n", c=TT),
                              rows[:, R_RB:R_RB + NR].unsqueeze(1).to_broadcast([P, TT, NR]), ALU.add).then_inc(sem("logits_out"), 1)
            dve.wait_ge(sem("logits_out"), 1)
            do(dve.tensor_copy(glog, logits[:, :, 0:EG]))
            do(dve.tensor_reduce(gmax, glog, AX_X, ALU.max))
            dve.tensor_tensor(gx, glog, b4(gmax, 4), ALU.subtract).then_inc(sem("rt_in"), 1)
            first_of(ohg, glog, gmax, t4)
            for j in range(4):
                do(dve.tensor_tensor(big16[:, :, j, :], logits[:, :, EG:].rearrange("p c (g j) -> p c j g", j=4)[:, :, j, :], ohg, ALU.mult))
            do(dve.tensor_reduce(ing, big16, AX_X, ALU.add))
            do(dve.tensor_reduce(l1, ing, AX_X, ALU.max))
            first_of(oh1, ing, l1, t4)
            do(dve.scalar_tensor_tensor(out=t4b, in0=oh1, scalar=-BIG, in1=ing, op0=ALU.mult, op1=ALU.add))
            do(dve.tensor_reduce(l2, t4b, AX_X, ALU.max))
            first_of(oh2, t4b, l2, t4)
            dve.tensor_tensor(rsc[:, 10, 0:TT], l2, l1, ALU.subtract).then_inc(sem("rt_in"), 1)
            dve.wait_ge(sem("rt_exp"), 2)
            do(dve.tensor_reduce(pg, r4(2), AX_X, ALU.add))
            do(dve.tensor_scalar(g1, rsc[:, 10, 0:TT], 1.0, None, ALU.add))
            do(dve.tensor_tensor(g1, g1, pg, ALU.mult))
            do(dve.reciprocal(g1, g1))
            do(dve.tensor_tensor(g2, g1, rsc[:, 10, 0:TT], ALU.mult))
            for m, oh in ((first, oh1), (second, oh2)):
                for j in range(4):
                    own.mark(dve.tensor_tensor(m[:, :, 4 * j:4 * j + 4], oh, b4(ohg[:, :, j], 4), ALU.mult))
            own.settle()
            dve.tensor_tensor(chosen, first, second, ALU.add).then_inc(sem("chosen"), 1)
            dve.wait_ge(sem("iota_ready"), 2)
            own.mark(dve.tensor_copy(iota_row, iota_i[:, 0:P]))
            own.mark(dve.tensor_copy(token_id, iota_i[:, P:]))
            own.settle()
            dve.wait_ge(sem("counted"), 1)
            own.mark(dve.tensor_scalar(place, psum[4][:, 0:TT * EXPERTS].rearrange("p (c e) -> p c e", c=TT), -1.0, None, ALU.add))
            do(dve.tensor_copy(count, psum[4][:, TT * EXPERTS:(TT + 1) * EXPERTS]))
            own.mark(dve.tensor_scalar(ahead, place, float(P), None, ALU.is_ge))
            do(dve.tensor_scalar(extras, count, float(P), None, ALU.is_gt))
            own.mark(dve.tensor_scalar(beyond, ahead, 1.0, None, ALU.mult))
            for j in (2, 3):
                own.mark(dve.scalar_tensor_tensor(out=ahead, in0=place, scalar=float(j * P), in1=ahead, op0=ALU.is_ge, op1=ALU.add))
                do(dve.scalar_tensor_tensor(out=extras, in0=count, scalar=float(j * P), in1=extras, op0=ALU.is_gt, op1=ALU.add))
            do(dve.tensor_tensor_scan(upto, ones[:, 0:EXPERTS], extras, 0.0, ALU.mult, ALU.add))
            own.mark(dve.scalar_tensor_tensor(out=extras, in0=upto, scalar=EXPERTS - 1.0, in1=extras, op0=ALU.add, op1=ALU.subtract))
            own.mark(dve.scalar_tensor_tensor(out=place, in0=ahead, scalar=-float(P), in1=place, op0=ALU.mult, op1=ALU.add))
            own.settle()
            do(dve.tensor_tensor(extras, extras, iota_row[:, 0:EXPERTS], ALU.subtract))

            def over_tokens(ap):
                return ap.unsqueeze(1).to_broadcast([P, TT, EXPERTS])
            do(dve.tensor_tensor(beyond, beyond, over_tokens(extras), ALU.mult))
            do(dve.tensor_tensor(ahead, ahead, beyond, ALU.add))
            do(dve.tensor_tensor(ahead, ahead, over_tokens(iota_row[:, 0:EXPERTS]), ALU.add))
            for j, m in enumerate((first, second)):
                for src, out in ((ahead, tile_at), (place, place_at)):
                    do(dve.tensor_tensor(big, m, src, ALU.mult))
                    do(dve.tensor_reduce(out[:, j, :], big, AX_X, ALU.add))
            for j in range(2):
                for c in range(TT):
                    own.mark(dve.tensor_scalar(tile_hot[:, 4 * j + c, :], iota_row[:, 0:24], tile_at[:, j, c:c + 1], token_id[:, c:c + 1],
                                               ALU.is_equal, ALU.mult))
                    own.settle()
                    dve.tensor_scalar(one_hot[:, 4 * j + c, :], iota_row, place_at[:, j, c:c + 1], None,
                                      ALU.is_equal).then_inc(sem("one_hot_ready"), 1)
            own.mark(dve.scalar_tensor_tensor(out=slot_of[:], in0=tile_at, scalar=float(P), in1=place_at, op0=ALU.mult, op1=ALU.add))
            xe = one_extra
            do(dve.tensor_tensor(xe, upto.unsqueeze(1).to_broadcast([P, EXTRA, EXPERTS]),
                                 iota_row[:, 0:EXTRA].unsqueeze(2).to_broadcast([P, EXTRA, EXPERTS]), ALU.is_le))
            do(dve.tensor_reduce(extra_at[:, 0:EXTRA], xe, AX_X, ALU.add))
            own.mark(dve.tensor_copy(extra_of[:, 0:EXTRA], extra_at[:, 0:EXTRA]))
            own.mark(dve.tensor_copy(extra_of[:, 7:8], upto[:, EXPERTS - 1:EXPERTS]))
            own.settle()
            dve.wait_ge(sem("placed"), 1)
            dve.tensor_copy(token_of[:], psum[5][:, 0:24]).then_inc(sem("planned"), 1)
            for pre in ("e_", "x_"):
                dve.sem_inc(sem(pre + "hgT_ready"), 1)
                dve.sem_inc(sem(pre + "hid_ready"), 1)
            dve.sem_inc(sem("x_hg_turned"), 1)

            def take_tokens(T, u, pre, credit=0):
                dve.wait_ge(sem(pre + "hg_turned"), T + 1 + credit)
                for b in range(2):
                    gain = cols[:, C_G2 + 4 * b:C_G2 + 4 * b + 4].unsqueeze(2).to_broadcast([P, 4, P])
                    ins = dve.tensor_tensor(hgT[:, u, 4 * b:4 * b + 4, :], psum[2 + b][:].rearrange("p (k j) -> p k j", k=4), gain, ALU.mult)
                ins.then_inc(sem(pre + "hgT_ready"), 1)

            def hidden(T, pre):
                dve.wait_ge(sem(pre + "up_done"), T + 1)
                dve.wait_ge(sem(pre + "sg_ready"), T + 2)
                dve.tensor_tensor(hid, sg, psum[1][:], ALU.mult).then_inc(sem(pre + "hid_ready"), 1)
            take_tokens(0, 0, "e_")
            with dve.Fori(0, EXPERTS // 2) as i:
                for u in range(2):
                    hidden(2 * i + u, "e_")
                    take_tokens(2 * i + u + 1, 1 - u, "e_")
            n_extra = dve.value_load(extra_of[0:1, 7:8], min_val=0, max_val=EXTRA)
            with dve.Fori(0, EXTRA) as x:
                with dve.If(x < n_extra):
                    take_tokens(x, 0, "x_", credit=1)
                    hidden(x, "x_")
            for c in range(TT):
                dve.wait_ge(sem(f"rows{c % 2}_loaded"), 32 * (c // 2) + 32)
                for m, share in ((0, g1), (1, g2)):
                    if c + m:
                        dve.wait_ge(sem("rows_added"), 2 * c + m)
                    dve.scalar_tensor_tensor(out=x2[:, c, :], in0=pick[:, c % 2, m, :], scalar=share[:, c:c + 1], in1=x2[:, c, :],
                                             op0=ALU.mult, op1=ALU.add).then_inc(sem("rows_added"), 1)
            dve.wait_ge(sem("rows_added"), 2 * TT)
            mean_squares("ms_ready")
            dve.wait_ge(sem("rstd_ready"), 4)
            dve.wait_ge(sem("final_g_loaded"), 16)
            for c in range(TT):
                dve.scalar_tensor_tensor(out=x2[:, c, :], in0=x2[:, c, :], scalar=rstd[:, c:c + 1], in1=final_g,
                                         op0=ALU.mult, op1=ALU.mult).then_inc(sem("out_ready"), 1)


def heads(ap):
    return ap.rearrange("p (h d) -> p h d", d=HEAD)


def relu_tmp(relu, j):
    return relu[:, 0, j * 128:(j + 1) * 128].rearrange("p (t h) -> p t h", t=TT)


def tile_k(w, n=None):
    k, n = w.shape
    return np.ascontiguousarray(w.reshape(k // P, P, n).transpose(1, 0, 2).reshape(P, -1))


def layout(i):
    g = {k: np.asarray(v)[0] for k, v in i.items() if k not in ("x", "final_norm_g")}
    w_in = g["w_in"]
    sizes = [2048, 3072, 32, 1024, 1024, 1024, 384, 256, 64, 8, 1024, 1024, 1024]
    at = np.cumsum([0] + sizes)
    z, xbc, dt, sb_, sc_, sx_, cq, ckv, kix, wix, ga, gb, gc = (w_in[:, at[j]:at[j + 1]] for j in range(len(sizes)))

    def pair3(ws):
        return np.stack([np.stack([w[:, j * P:(j + 1) * P] for w in ws], 1).reshape(KT, P, 3, P).transpose(1, 0, 2, 3).reshape(P, -1)
                         for j in range(KT)])

    a = {}
    a["x"] = np.asarray(i["x"]).reshape(TT, P, D)
    a["w_kv"] = tile_k(w_in[:, at[7]:at[10]])
    a["w_q"] = tile_k(cq)
    a["w_dt"] = tile_k(dt)
    a["w_idx"] = tile_k(g["idx_w_q"].reshape(Q_LORA, -1))
    a["w_sc"] = pair3([sb_, sc_, sx_])
    uq = g["att_w_uq"].reshape(Q_LORA, -1)
    uk = g["att_w_uk"].reshape(4, 2, 2, HEAD, KV_LORA).transpose(0, 2, 3, 1, 4).reshape(4, P, -1)
    a["w_qk"] = np.stack([np.concatenate([tile_k(uq[:, j * 256:(j + 1) * 256]), uk[j]], 1) for j in range(4)])
    a["w_uv"] = g["att_w_uv"].reshape(4, HQ, RT, P, HEAD).transpose(0, 3, 1, 2, 4).reshape(4, P, -1)
    xs_, b_, c_ = xbc[:, :2048], xbc[:, 2048:2560], xbc[:, 2560:]
    a["w_ssm_x"] = np.stack([tile_k(xs_[:, 512 * q:512 * q + 512]) for q in range(GROUPS)])
    a["w_ssm_bc"] = np.stack([tile_k(np.concatenate([b_[:, P * q:P * q + P], c_[:, P * q:P * q + P]], 1)) for q in range(GROUPS)])
    a["w_z"] = np.stack([tile_k(z[:, 512 * q:512 * q + 512]) for q in range(GROUPS)])
    outs = np.concatenate([g["ssm_w_out"], g["sc_w_out"], g["att_w_out"]], 0)
    a["w_merge"] = np.stack([tile_k(outs[:, P * j:P * j + P]) for j in range(KT)])
    a["w_gates"] = pair3([ga, gb, gc])
    a["w_mix"] = np.stack([tile_k(g["mix_w_out"][:, 512 * j:512 * j + 512]) for j in range(2)])
    a["w_router"] = tile_k(np.concatenate([g["moe_w_group"], g["moe_w_expert"]], 1))
    for n in ("gate", "up"):
        a["w_" + n] = g["moe_w_" + n].reshape(EXPERTS, KT, P, F_EXP).transpose(0, 2, 1, 3).reshape(EXPERTS, P, -1)
    a["w_down"] = g["moe_w_down"].reshape(EXPERTS, FT, P, D).transpose(0, 2, 1, 3).reshape(EXPERTS, P, -1)
    a["final_g"] = np.asarray(i["final_norm_g"])[None]
    conv = np.concatenate([g["ssm_conv_w"], g["ssm_conv_b"][None]], 0)
    ct = conv.reshape(5, 24, P).transpose(2, 1, 0)
    order = [j for q in range(GROUPS) for j in (4 * q, 4 * q + 1, 4 * q + 2, 4 * q + 3, 16 + q, 20 + q)]

    def col(v):
        return v.reshape(-1, P).T
    a["cols"] = np.concatenate([
        col(g["norm1_g"]), col(g["att_q_norm_g"]), np.tile(g["idx_k_norm_g"], 2)[:, None],
        g["sc_conv_w"].reshape(SC_TAPS, KT, P).transpose(2, 1, 0).reshape(P, -1),
        ct[:, order, :].reshape(P, -1), col(g["ssm_norm_g"]), col(g["norm2_g"])], 1)
    a["rows"] = np.concatenate([g["att_kv_norm_g"], g["ssm_dt_bias"], g["ssm_a_log"], g["ssm_d"],
                                g["moe_b_group"], g["moe_b_expert"]])[None]
    assert a["cols"].shape == (P, NCOL) and a["rows"].shape == (1, NROW)
    return {k: np.ascontiguousarray(v) for k, v in a.items()}


def kernel(**inputs):
    import concourse.bacc as bacc
    from concourse.bass_utils import run_bass_kernel_spmd

    nc = bacc.Bacc("TRN2", target_bir_lowering=False, num_devices=1)
    arrays = {"in_" + k: v for k, v in layout(inputs).items()}
    t = {k[3:]: nc.dram_tensor(k, v.shape, mybir.dt.from_np(v.dtype), kind="ExternalInput").ap() for k, v in arrays.items()}
    t["out"] = nc.dram_tensor("out_dram", (TT, P, D), F32, kind="ExternalOutput").ap()
    build(nc, t)
    r = run_bass_kernel_spmd(nc, [arrays], core_ids=[0])
    return r.results[0]["out_dram"].reshape(1, S, D)
```

```python
from contextlib import ExitStack

import numpy as np

import concourse.bass as bass
from concourse import mybir

F32 = mybir.dt.float32
F32R = mybir.dt.float32r
U32 = mybir.dt.uint32
I32 = mybir.dt.int32
ALU = mybir.AluOpType
ACT = mybir.ActivationFunctionType
AX_X = mybir.AxisListType.X

P = 128
D = 1024
S = 512
KT = D // P
TT = S // P
EPS = 1e-6
D_INNER = 2048
SSM_HEADS = 32
HEAD = 64
GROUPS = 4
GH = SSM_HEADS // GROUPS
TAPS = 4
SC_TAPS = 3
Q_LORA = 384
QT = Q_LORA // P
KV_LORA = 256
RT = KV_LORA // P
D_IDX = 64
IDX_HEADS = 8
KVC = KV_LORA + D_IDX + IDX_HEADS
KVD = KVC + SSM_HEADS
IDX_SCALE = (IDX_HEADS * D_IDX) ** -0.5
ATT_SCALE = 64 ** -0.5
HQ = 4
TOPK = 128
RING = 8
LAG = 5
BIG = 1e30
UNSEEN = -1e38
TAKEN = -3e38
EXPERTS = 16
EG = 4
F_EXP = 512
FT = F_EXP // P
EXTRA = 7
TILES = EXPERTS + EXTRA

C_G1 = 0
C_QG = C_G1 + KT
C_KG = C_QG + QT
C_SC = C_KG + 1
C_CONV = C_SC + KT * SC_TAPS
C_NG = C_CONV + GROUPS * 6 * (TAPS + 1)
C_G2 = C_NG + D_INNER // P
NCOL = C_G2 + KT
R_KVG = 0
R_DTB = R_KVG + KV_LORA
R_ALOG = R_DTB + SSM_HEADS
R_D = R_ALOG + SSM_HEADS
R_RB = R_D + SSM_HEADS
NROW = R_RB + EG + EXPERTS


PAIR = [("y", 0), ("y", 1), ("y", 2), ("y", 3), ("z", 0), ("z", 1), ("s", 0), ("s", 1), ("z", 2), ("s", 2), ("s", 3),
        ("s", 4), ("s", 5), ("z", 3), ("s", 6), ("s", 7), ("n", 0), ("n", 1)]
SSM_UNITS = 10
SLOT = [0, 1, 2, 0, 1, 2, 0, 1, 2, 1]


def pair_at(g, kind, c, only=("y", "z", "s", "n")):
    if isinstance(g, int) and g == GROUPS and kind == "n":
        return pair_at(g, "y", 3, only) + 1 + c
    kinds = [k for k, _ in PAIR]
    return g * sum(k in only for k in kinds) + (sum(k in only for k in kinds[:PAIR.index((kind, c)) + 1]) - 4)


def pair_made(g, kind, c):
    return pair_at(g, kind, c, ("y", "s", "n"))


class Marks:

    def __init__(self, eng, sem):
        self.eng, self.sem, self.n, self.base = eng, sem, 0, 0

    def mark(self, ins):
        ins.then_inc(self.sem, 1)
        self.n += 1

    def settle(self):
        self.eng.wait_ge(self.sem, self.base + self.n)

    def loop(self, i, per):
        self.before, self.per = self.n, per
        self.base, self.n = i * per + self.n, 0

    def end(self, reps):
        assert self.n == self.per, (self.n, self.per)
        self.base, self.n = 0, self.before + reps * self.per


def build(nc, t):
    with ExitStack() as ctx:
        def sb(name, shape):
            return ctx.enter_context(nc.sbuf_tensor(name, shape, F32))

        sems = {}

        def sem(name):
            if name not in sems:
                sems[name] = ctx.enter_context(nc.semaphore(name))
            return sems[name]

        def over(first, *names):
            with ExitStack() as undo:
                return [undo.enter_context(nc.sbuf_tensor(name or f"under{at}", [P, n], F32R)) for at, (name, n) in enumerate(names, first)]
        unit01, _, unit23, split_a, split_b, split_cd, _, split_e = over(
            0, ("unit01", 4096), (None, 4096), ("unit23", 4096), ("split_a", 4096), ("split_b", 4096),
            ("split_cd", 8192), (None, 12288), ("split_e", 8192))
        _, sc_unit01, _, sc_unit2 = over(8, (None, 7 * 4096 + 5376), ("sc_unit01", 4096), (None, 8098), ("sc_unit2", 2048))
        hT = sb("hT", [P, KT, S])
        gatedT = sb("gatedT", [P, KT, S])
        oT = sb("oT", [P, KT, S])
        WA = sb("WA", [P, 4096])
        WB = sb("WB", [P, 4096])
        WC = sb("WC", [P, 4096])
        WD = sb("WD", [P, 4096])
        arena = sb("arena", [P, 21504])
        cols = sb("cols", [P, NCOL])
        rows = sb("rows", [P, NROW])
        ident = sb("ident", [P, P])
        tri_le = sb("tri_le", [P, P])
        tri_gt = sb("tri_gt", [P, P])
        ones = sb("ones", [P, P])
        small = sb("small", [P, 256])
        dt_sb = sb("dt_sb", [P, TT, SSM_HEADS])
        da_sb = sb("da_sb", [P, TT, SSM_HEADS])
        ex_sb = sb("ex_sb", [P, 3, TT, SSM_HEADS])
        psum = [ctx.enter_context(nc.psum_tensor(f"bank{b}", [P, 512], F32)) for b in range(8)]

        h2_dram = nc.dram_tensor("h2_dram", (S, D), F32, kind="Internal").ap()
        y_dram = nc.dram_tensor("y_dram", (TILES * P, D), F32, kind="Internal").ap()
        token_of = ctx.enter_context(nc.sbuf_tensor("token_of", [P, 24], U32))
        slot_of = ctx.enter_context(nc.sbuf_tensor("slot_of", [P, 2, TT], U32))
        extra_of = ctx.enter_context(nc.sbuf_tensor("extra_of", [P, 8], I32))
        place_now = ctx.enter_context(nc.sbuf_tensor("place_now", [P, 1], U32))
        iota_i = ctx.enter_context(nc.sbuf_tensor("iota_i", [P, P + TT], I32))

        def part(at, *shape):
            n = int(np.prod(shape))
            ap = arena[:, at:at + n]
            if len(shape) == 2:
                ap = ap.rearrange("p (a b) -> p a b", a=shape[0])
            if len(shape) == 3:
                ap = ap.rearrange("p (a b c) -> p a b c", a=shape[0], b=shape[1])
            return ap, at + n

        cqT, at = part(0, QT, S)
        kvn, at = part(at, TT, KV_LORA)
        kvnT, at = part(at, RT, S)
        kidxT, at = part(at, S)
        bias, at_att = part(at, P * (1 + 2 + 3 + 4))
        BIAS_AT = [0, P, 3 * P, 6 * P]
        assert at_att == 5376
        x_sb, at = part(at_att, TT, D)
        kvraw, at = part(at, TT, KVD)
        qraw, at = part(at, TT, Q_LORA)
        kdup, at = part(at, TT, 2 * D_IDX)
        qiT, at = part(at, 4, S)
        relu, at = part(at, 2, S)
        sc_u, at = part(at, S + SC_TAPS - 1)
        sc_v, at = part(at, S)
        sc_w, at = part(at, S)
        assert at == 5376 + 4096 + 8098
        at = at_att + TT * D
        probs, at = part(at, RING, S)
        PT, at = part(at, 2, TT, HQ * P)
        assert at <= 21504
        qT = WD[:, 0:1024].rearrange("p (j s) -> p j s", j=2)
        kT = WD[:, 1024:2048].rearrange("p (j s) -> p j s", j=2)
        v_sb = WD[:, 2048:3072].rearrange("p (c n) -> p c n", c=TT)
        SCORE_BANKS = (2, 3, 6, 7)
        HEADS_N = 10
        w_uq = WC[:, 0:768].rearrange("p (k n) -> p k n", k=QT)
        w_uk = WC[:, 768:1280].rearrange("p (r n) -> p r n", r=RT)
        w_uv = WC[:, 1280:1792].rearrange("p (r n) -> p r n", r=RT)
        ynT, at_local = part(0, D_INNER // P, S)
        xsT, at = part(at_local, 6, S)
        conv, at = part(at, 2, S)
        xdt, at = part(at, TT, S)
        xend, at = part(at, 2, S)
        decay, at = part(at, 2, 4, P)
        da_tri, at = part(at, 2, 4, P)
        mix_m, at = part(at, 4, 4, P)
        y, at = part(at, TT, S)
        assert at <= 21504
        sz = WD[:, 0:2048].rearrange("p (c n) -> p c n", c=TT)
        state = WD[:, 2048:2560]
        tmp = WD[:, 2560:3072]
        b_tok = WD[:, 3072:3584]
        cb = WD[:, 3584:4096].rearrange("p (c l) -> p c l", c=TT)
        ssm_land = [WC[:, 2048:3072], WC[:, 3072:4096]]
        ssm_units = [(b[:, at:at + 1024], b[:, at + d:at + d + 1024]) for b, at, d in
                     ((unit01, 0, 1024), (unit01, 2048, 1024), (split_cd, 0, 1024))]
        norm_by = xend[:, 1]
        norm_diag = conv[:, 1].rearrange("p (c t) -> p c t", c=TT)
        def parts(buf, at, kn):
            return buf[:, at:at + kn * S].rearrange("p (k s) -> p k s", k=kn)
        hH, hL = parts(split_a, 0, KT), parts(split_b, 0, KT)
        ynH, ynL = parts(split_cd, 0, 16), parts(split_e, 0, 16)
        gH, gL = parts(split_cd, 0, KT), parts(split_cd, 4096, KT)
        oH, oL = parts(split_e, 0, KT), parts(split_e, 4096, KT)
        land = [arena[:, at_local + j * 1024:at_local + (j + 1) * 1024] for j in range(3)]
        unitH, unitL = ([buf[:, a + j * 1024:a + j * 1024 + 1024] for buf in (unit01, unit23) for a in (0, 2048)] for j in range(2))
        mergedT = gatedT
        sig = arena[:, 20480:20992]
        x2, at_moe = part(at_local + 4096 + 3 * S + 2 * S, TT, D)
        w_mix = [arena[:, 4096 * j:4096 * (j + 1)].rearrange("p (k n) -> p k n", k=KT) for j in range(2)]
        h2, at = part(0, TT, D)
        h2T = hT
        f_flat, o_flat = (b[:].rearrange("p k s -> p (k s)") for b in (gatedT, oT))
        w_exp = [[w.rearrange("p (k n) -> p k n", k=k) for w, k in zip(ws, (KT, KT, FT))]
                 for ws in ((WA[:], WB[:], WC[:]), (f_flat, o_flat, arena[:, 4096:8192]))]
        gath, at = part(at_local, 2, D)
        hgT, at = part(at, 2, KT, P)
        sg, at = part(at, F_EXP)
        hid, at = part(at, F_EXP)
        hidT, at = part(at, FT, P)
        yt, at = part(at, D)
        assert at <= at_moe - TT * D
        pick = [arena[:, at + c % 2 * 2 * D:at + (c % 2 + 1) * 2 * D].rearrange("p (m d) -> p m d", m=2)
                for c, at in enumerate((at_local, at_local, 0, 0))]
        w_router = WD[:, 0:KT * (EG + EXPERTS)].rearrange("p (k n) -> p k n", k=KT)
        final_g = WD[:, 1024:1024 + D]
        NR = EG + EXPERTS
        rt = at_moe
        logits, rt = part(rt, TT, NR)
        rsc, rt = part(rt, 22, TT * EXPERTS)
        first, second, chosen, place, ahead, beyond = (rsc[:, j, :].rearrange("p (c e) -> p c e", c=TT) for j in (1, 2, 19, 20, 21, 8))
        count, extras, upto = (rsc[:, 18, 16 * j:16 * j + 16] for j in range(3))
        place_tile = rsc[:, 4, 0:16].rearrange("p (s m c) -> p s m c", s=2, m=2)
        place_at, tile_at = (place_tile[:, j] for j in range(2))
        logitsT = WD[0:NR, 3328:3328 + S]
        weight4 = rsc[:, 16, 32:36]
        before = arena[:, 20992:20992 + (TT + 1) * EXPERTS].rearrange("p (c e) -> p c e", c=TT + 1)
        extra_at = rsc[:, 4, 16:24]
        iota_row, rt = part(rt, P)
        one_extra, rt = part(rt, EXTRA, EXPERTS)
        token_id, rt = part(rt, TT)
        at_one = 2048
        one_hot = WD[:, at_one:at_one + 8 * P].rearrange("p (a j) -> p a j", a=8)
        tile_hot = WD[:, at_one + 8 * P:at_one + 8 * P + 8 * 24].rearrange("p (a j) -> p a j", a=8)
        assert rt <= 21504

        sc_in = oT[:].rearrange("p k s -> p (k s)")[:, 0:6 * S].rearrange("p (a b c) -> p a b c", a=2, b=3)
        sq = WD[:, 3072:4096]

        wa_kv = WA[:, 0:KT * KVD].rearrange("p (k n) -> p k n", k=KT)
        wb_q = WB[:, 0:KT * Q_LORA].rearrange("p (k n) -> p k n", k=KT)
        wd_idx = WD[:, 0:QT * 512].rearrange("p (k n) -> p k n", k=QT)
        sc_land = [WC[:, 1792:2816], WC[:, 2816:3840], WD[:, 2048:3072]]
        sc_high, sc_low = ([sc_unit01[:, a:a + 1024] for a in (j * 1024, 2048 + j * 1024)] + [sc_unit2[:, j * 1024:j * 1024 + 1024]] for j in range(2))
        SCU = 3 * KT
        MGU = SCU + SSM_UNITS * GROUPS
        SSM_LOADS = KT + SSM_UNITS // 2 * GROUPS

        ms = small[:, 0:4]
        rstd = small[:, 4:8]
        ms2 = small[:, 8:20]
        rstd2 = small[:, 20:32]
        m8 = small[:, 32:40]
        widx = small[:, 40:72].rearrange("p (t h) -> p t h", t=TT)
        powm = small[:, 72:84]
        pmax, nmax, psums, pinv = (small[:, 112 + RING * j:112 + RING * (j + 1)] for j in range(4))
        m16 = small[:, 100:104]
        r16 = small[:, 104:108]
        waited = small[:, 108:109]
        carried = small[:, 144:153]

        def flat(ap):
            return ap.rearrange("p k n -> p (k n)")

        block = ctx.enter_context(nc.Block())

        @block.sync
        def _(sp):
            for c in range(TT):
                sp.dma_start(x_sb[:, c, :], t["x"][c]).then_inc(sem(f"x{c}_loaded"), 16)
                if c == 0:
                    sp.dma_start(cols[:], t["cols"]).then_inc(sem("params_loaded"), 16)
            sp.dma_start(rows[:], t["rows"].broadcast_to([P, NROW])).then_inc(sem("params_loaded"), 16)
            sp.dma_start(WA[:, 0:KT * KVD], t["w_kv"]).then_inc(sem("w_kv_loaded"), 16)
            sp.dma_start(WB[:, 0:KT * Q_LORA], t["w_q"]).then_inc(sem("w_q_loaded"), 16)
            sp.dma_start(WD[:, 0:QT * 512], t["w_idx"]).then_inc(sem("w_idx_loaded"), 16)
            for u in range(3):
                sp.dma_start(sc_land[u], t["w_sc"][u]).then_inc(sem(f"unit{u}_loaded"), 16)
            def load_sc(T):
                for u in range(3):
                    sp.wait_ge(sem("unit_low"), 3 * T + (u - 2))
                    sp.dma_start(sc_land[u], t["w_sc"][3 * T + u]).then_inc(sem(f"unit{u}_loaded"), 16)
            load_sc(1)
            def load_heads(hg, first=False):
                if not first:
                    sp.wait_ge(sem("head_done"), hg * HEADS_N - 6)
                sp.dma_start(WC[:, 0:1280], t["w_qk"][hg]).then_inc(sem("w_qk_loaded"), 16)
                if not first:
                    sp.wait_ge(sem("head_done"), hg * HEADS_N - 4)
                sp.dma_start(WC[:, 1280:1792], t["w_uv"][hg]).then_inc(sem("w_uv_loaded"), 16)
            load_heads(0, first=True)
            with sp.Fori(2, KT) as T:
                load_sc(T)
            def load_ssm(g, u):
                sp.dma_start(ssm_land[u % 2], t["w_ssm"][SSM_UNITS * g + u]).then_inc(sem(f"unit{u % 2}_loaded"), 16)
            sp.wait_ge(sem("unit_low"), SCU)
            load_ssm(0, 0)
            load_ssm(0, 1)
            with sp.Fori(1, TT) as hg:
                load_heads(hg)
            for u in range(2, SSM_UNITS):
                sp.wait_ge(sem("unit_low"), SCU + u - 1)
                load_ssm(0, u)
            with sp.Fori(1, GROUPS) as g:
                for u in range(SSM_UNITS):
                    sp.wait_ge(sem("unit_low"), SSM_UNITS * g + (SCU + u - 1))
                    load_ssm(g, u)
            def load_unit(m, u):
                sp.dma_start(land[u], t["w_units"][m]).then_inc(sem(f"unit{u}_loaded"), 16)
            sp.wait_ge(sem("x_ready"), TT * GROUPS)
            for v in range(4):
                sp.wait_ge(sem("unit_low"), MGU + v - 1)
                load_unit(v, v % 2)
            with sp.Fori(1, KT) as n:
                for v in range(4):
                    sp.wait_ge(sem("unit_low"), n * 4 + (MGU + v - 1))
                    load_unit(4 * n + v, v % 2)
            for v in range(3):
                if v < 2:
                    sp.wait_ge(sem("unit_low"), MGU + 4 * KT - 1 + v)
                load_unit(4 * KT + v, v)
            sp.wait_ge(sem("split_low"), 32)
            def load_mix(n):
                sp.dma_start(arena[:, bass.ds(n * 1024, 1024)], t["w_mix"][n]).then_inc(sem("w_mix_loaded"), 16)
            with sp.Fori(1, KT) as n:
                for v in range(3):
                    sp.wait_ge(sem("unit_low"), n * 3 + (MGU + 4 * KT + v - 2))
                    load_unit(3 * n + (4 * KT + v), v)
                load_mix(n - 1)
            load_mix(KT - 1)
            sp.wait_ge(sem("unit_used"), MGU + 7 * KT)
            sp.dma_start(x2, t["x"].rearrange("t p d -> p t d")).then_inc(sem("x_loaded"), 16)
            sp.dma_start(WD[:, 0:KT * (EG + EXPERTS)], t["w_router"]).then_inc(sem("router_final_loaded"), 16)
            sp.dma_start(final_g, t["final_g"].broadcast_to([P, D])).then_inc(sem("router_final_loaded"), 16)
            sp.dma_start(WA[:], t["w_gate"][0]).then_inc(sem("w_gate0_loaded"), 16)
            sp.dma_start(WB[:], t["w_up"][0]).then_inc(sem("w_up0_loaded"), 16)
            sp.dma_start(WC[:], t["w_down"][0]).then_inc(sem("w_down0_loaded"), 16)
            sp.wait_ge(sem("mix_done"), 8)
            sp.dma_start(flat(w_exp[1][0]), t["w_gate"][1]).then_inc(sem("w_gate1_loaded"), 16)
            sp.dma_start(flat(w_exp[1][1]), t["w_up"][1]).then_inc(sem("w_up1_loaded"), 16)
            sp.dma_start(flat(w_exp[1][2]), t["w_down"][1]).then_inc(sem("w_down1_loaded"), 16)
            sp.wait_ge(sem("h2_ready"), TT)
            sp.dma_start(h2_dram.rearrange("(c p) d -> p c d", p=P), h2).then_inc(sem("h2_stored"), 16)
            for at_row, n in ((EXPERTS, TT), (EXPERTS + TT, EXTRA - TT)):
                sp.dma_start(y_dram[at_row * P:(at_row + n) * P, :].rearrange("(c p) d -> p c d", p=P), h2[:, 0:n, :]).then_inc(sem("rows_filled"), 16)
            sp.wait_ge(sem("rows_filled"), 32)
            sp.sem_inc(sem("e_y_stored"), 16)
            sp.sem_inc(sem("x_y_stored"), 16)

            def reload(T, u):
                sp.wait_ge(sem("e_gate_done"), T + 1)
                sp.dma_start(flat(w_exp[u][0]), t["w_gate"][T + 2]).then_inc(sem(f"w_gate{u}_loaded"), 16)
                sp.wait_ge(sem("e_up_done"), T + 1)
                sp.dma_start(flat(w_exp[u][1]), t["w_up"][T + 2]).then_inc(sem(f"w_up{u}_loaded"), 16)
                sp.wait_ge(sem("e_down_done"), 2 * T + 2)
                sp.dma_start(flat(w_exp[u][2]), t["w_down"][T + 2]).then_inc(sem(f"w_down{u}_loaded"), 16)

            def store_rows(T, slot, pre):
                sp.wait_ge(sem(pre + "y_taken"), 2 * T + 2 + 2)
                sp.dma_start(y_dram[bass.ds(slot * P, P), :], yt).then_inc(sem(pre + "y_stored"), 16)
            with sp.Fori(0, EXPERTS // 2 - 1) as i:
                for u in range(2):
                    reload(2 * i + u, u)
                    store_rows(2 * i + u, 2 * i + u, "e_")
            for T in (EXPERTS - 2, EXPERTS - 1):
                store_rows(T, T, "e_")
            sp.wait_ge(sem("planned"), 1)
            n_extra = sp.value_load(extra_of[0:1, 7:8], min_val=0, max_val=EXTRA)
            with sp.Fori(0, EXTRA) as x:
                with sp.If(x < n_extra):
                    e = sp.value_load(extra_of[0:1, bass.ds(x, 1)], min_val=0, max_val=EXPERTS - 1)
                    sp.wait_ge(sem("x_y_stored"), x * 16 + 16)
                    for w, b in zip(("w_gate", "w_up", "w_down"), w_exp[0]):
                        sp.dma_start(flat(b), t[w][bass.ds(e, 1)].rearrange("o p n -> p (o n)")).then_inc(sem("x_w_loaded"), 16)
                    store_rows(x, x + EXPERTS, "x_")
            sp.wait_ge(sem("e_y_stored"), EXPERTS * 16 + 16)
            sp.wait_ge(sem("x_y_stored"), n_extra * 16 + 16)
            sp.sem_inc(sem("rows_stored"), 1)
            for c in range(TT):
                sp.wait_ge(sem("out_ready"), c + 1)
                sp.dma_start(t["out"][c], x2[:, c, :]).then_inc(sem("out_stored"), 16)
            sp.wait_ge(sem("out_stored"), 16 * TT)

        @block.gpsimd
        def _(pool):
            def tri(ap, op, base, mult, step):
                pool.affine_select(out=ap, in_=ones[:], compare_op=op, fill=0.0, base=base,
                                   pattern=[[step, P]], channel_multiplier=mult).then_inc(sem("consts_ready"), 1)
            pool.memset(ones[:], 1.0).then_inc(sem("ones_ready"), 1)
            pool.iota(iota_i[:, 0:P], pattern=[[1, P]], base=0, channel_multiplier=0).then_inc(sem("iota_ready"), 1)
            pool.iota(iota_i[:, P:], pattern=[[P, TT]], base=0, channel_multiplier=1).then_inc(sem("iota_ready"), 1)
            pool.memset(powm, -0.5).then_inc(sem("ones_ready"), 1)
            pool.memset(sc_u, 0.0).then_inc(sem("ones_ready"), 1)
            pool.wait_ge(sem("ones_ready"), 3)
            tri(ident[:], ALU.is_equal, 0, 1, -1)
            tri(tri_le[:], ALU.is_ge, 0, -1, 1)
            tri(tri_gt[:], ALU.is_gt, 0, 1, -1)
            pool.memset(bias[:, 0:P], 0.0).then_inc(sem("bias_zero"), 1)
            pool.wait_ge(sem("bias_zero"), 1)
            pool.affine_select(out=bias[:, 0:P], in_=bias[:, 0:P], compare_op=ALU.is_ge, fill=-BIG, base=0,
                               pattern=[[-1, P]], channel_multiplier=1).then_inc(sem("consts_ready"), 1)
            for c in range(TT):
                pool.wait_ge(sem("ms_ready"), c + 1)
                pool.tensor_tensor(rstd[:, c:c + 1], ms[:, c:c + 1], powm[:, 0:1], ALU.pow).then_inc(sem("rstd_ready"), 1)
            for u in range(2):
                pool.sem_inc(sem(f"sc_gated{u}"), 1)

            def split_h(first, end, at=0):
                for k in range(first, end):
                    pool.wait_ge(sem("h_high"), at + k + 1)
                    pool.tensor_tensor(hL[:, k, :], hT[:, k, :], hH[:, k, :].bitcast(F32), ALU.subtract).then_inc(sem("h_low"), 1)

            def unit_low(U, low, high, src):
                pool.wait_ge(sem("unit_high"), U + 1)
                pool.tensor_tensor(low, src, high.bitcast(F32), ALU.subtract).then_inc(sem("unit_low"), 1)

            def sc_units(T):
                for u in range(3):
                    unit_low(3 * T + u, sc_low[u], sc_high[u], sc_land[u])
            sc_units(0)
            pool.wait_ge(sem("kq_projected"), 2 * TT)
            split_h(0, 3)
            pool.wait_ge(sem("ms_ready"), TT + 1)
            pool.tensor_tensor(rstd2, ms2, powm[:, 0:12], ALU.pow).then_inc(sem("rstd_ready"), 1)
            split_h(3, KT)
            sc_units(1)
            for b in range(1, TT):
                pool.wait_ge(sem("score_ready"), b)
                dg = bias[:, BIAS_AT[b] + b * P:BIAS_AT[b] + (b + 1) * P]
                pool.affine_select(out=dg, in_=dg, compare_op=ALU.is_ge, fill=UNSEEN, base=0,
                                   pattern=[[-1, P]], channel_multiplier=1).then_inc(sem("score_hidden"), 1)
            own = Marks(pool, sem("pool_sc"))
            def sc_tile(T, i, u):
                b, c, x = (sc_in[:, u, j, :] for j in range(3))
                w = [cols[:, bass.ds(C_SC + T * SC_TAPS + k, 1)].to_broadcast([P, S]) for k in range(SC_TAPS)]
                pool.wait_ge(sem(f"sc_in{u}"), i * 3 + 6)
                own.mark(pool.tensor_tensor(sc_u[:, SC_TAPS - 1:], c, x, ALU.mult))
                own.settle()
                own.mark(pool.tensor_tensor(sc_v, sc_u[:, 2:2 + S], w[2], ALU.mult))
                own.mark(pool.tensor_tensor(sc_w, sc_u[:, 1:1 + S], w[1], ALU.mult))
                own.settle()
                own.mark(pool.tensor_tensor(sc_v, sc_v, sc_w, ALU.add))
                own.settle()
                own.mark(pool.tensor_tensor(sc_w, sc_u[:, 0:S], w[0], ALU.mult))
                own.settle()
                own.mark(pool.tensor_tensor(sc_v, sc_v, sc_w, ALU.add))
                own.settle()
                pool.tensor_tensor(gatedT[:, bass.ds(T, 1), :].rearrange("p o s -> p (o s)"), sc_v, b, ALU.mult).then_inc(sem(f"sc_gated{u}"), 1)
                pool.wait_ge(sem(f"sc_gated{u}"), i + 2)
            sc_tile(0, 0, 0)
            with pool.Fori(0, KT // 2 - 1) as i:
                own.loop(i, 2 * 6)
                sc_units(2 * i + 2)
                sc_tile(2 * i + 1, i, 1)
                sc_units(2 * i + 3)
                sc_tile(2 * i + 2, i + 1, 0)
                own.end(KT // 2 - 1)
            sc_tile(KT - 1, KT // 2 - 1, 1)
            def ssm_unit(g, *us):
                for u in us:
                    high, low = ssm_units[SLOT[u]]
                    unit_low(SSM_UNITS * g + (SCU + u), low, high, ssm_land[u % 2])

            pool.wait_ge(sem("unit_used"), SCU)
            for u in range(2):
                pool.wait_ge(sem(f"unit{u}_loaded"), (KT + 1) * 16)
                pool.tensor_copy(ssm_units[u][0], ssm_land[u]).then_inc(sem("unit_high"), 1)
            ssm_unit(0, 0, 1)
            norm = Marks(pool, sem("norm_own"))
            pool.sem_inc(sem("y_scaled"), 4)

            def tile_y(g, j):
                return ynT[:, bass.ds(g * 4 + (j - 4), 1), :].rearrange("p o s -> p (o s)")

            def carry_wait(j):
                pool.tensor_tensor(carried[:, j:j + 1], powm[:, 0:1], powm[:, 0:1], ALU.add)

            def gate_y(g):
                for j in range(4):
                    pool.wait_ge(sem("pair_taken"), pair_at(g, "y", j) + 2)
                    pool.wait_ge(sem("z_ready"), g * 4 + (j - 3))
                    carry_wait(j)
                    pool.tensor_tensor(tile_y(g, j), tile_y(g, j), sz[:, j, :], ALU.mult).then_inc(sem("y_gated"), 1)

            def square_y(g, *js):
                for j in js:
                    pool.wait_ge(sem("y_gated"), g * 4 + (j + 1))
                    carry_wait(4 + j)
                    if j == 0:
                        norm.mark(pool.tensor_tensor(conv[:, 0], tile_y(g, j), tile_y(g, j), ALU.mult))
                    else:
                        norm.mark(pool.tensor_tensor(conv[:, 1], tile_y(g, j), tile_y(g, j), ALU.mult))
                        norm.settle()
                        ins = pool.tensor_tensor(conv[:, 0], conv[:, 0], conv[:, 1], ALU.add)
                        if j < 3:
                            norm.mark(ins)
                            norm.settle()
                        else:
                            ins.then_inc(sem("y_squared"), 1)

            def norm_y(g):
                pool.wait_ge(sem("pair_taken"), pair_at(g, "n", 0) + 2)
                norm.mark(pool.tensor_tensor(r16, m16, powm[:, 0:4], ALU.pow))
                norm.settle()
                pool.tensor_tensor(norm_diag, ident[:].unsqueeze(1).to_broadcast([P, TT, P]), r16.unsqueeze(2).to_broadcast([P, TT, P]),
                                   ALU.mult).then_inc(sem("diag_ready"), 1)

            def scale_y(g, by):
                pool.wait_ge(sem("pair_taken"), pair_at(g, "n", 1) + 2)
                carry_wait(8)
                for j in range(4):
                    pool.tensor_tensor(tile_y(g, j), tile_y(g, j), by, ALU.mult).then_inc(sem("y_scaled"), 1)

            def scan_group(g, first=False, last=False):
                def triangle(k):
                    if k < 2:
                        pool.wait_ge(sem("unit_used"), SSM_UNITS * g + (SCU + 1))
                    else:
                        pool.wait_ge(sem("pair_done"), pair_made(g, "s", k - 2))
                    da = da_sb[:, k // 2, bass.ds(g * GH + 4 * (k % 2), 4)].unsqueeze(2).to_broadcast([P, 4, P])
                    tri = tri_le[:].unsqueeze(1).to_broadcast([P, 4, P])
                    pool.tensor_tensor(da_tri[:, k % 2], tri, da, ALU.mult).then_inc(sem("tri_ready"), 1)

                def end_state(c):
                    pool.wait_ge(sem("xdt_ready"), g * TT + c + 1)
                    if c == 1 and not first:
                        pool.wait_ge(sem("y_scaled"), g * 4)
                    if c == 2:
                        pool.wait_ge(sem("state_done"), g * 3 + 1)
                    ex = ex_sb[:, 1, c, bass.ds(g * GH, GH)].unsqueeze(2).to_broadcast([P, GH, HEAD])
                    pool.tensor_tensor(heads(xend[:, c % 2]), heads(xdt[:, c]), ex, ALU.mult).then_inc(sem("xend_ready"), 1)
                if first:
                    ssm_unit(g, 2)
                triangle(0)
                triangle(1)
                ssm_unit(g, 3, 4, 5, 6, 7, 8)
                if not first:
                    norm.loop(g - 1, 7)
                    pool.wait_ge(sem("conv_ready"), g * 6 + 6 + 2)
                    gate_y(g)
                ssm_unit(g, 9)
                end_state(0)
                triangle(2)
                triangle(3)
                if not first:
                    square_y(g, 0, 1)
                end_state(1)
                triangle(4)
                triangle(5)
                if not first:
                    square_y(g, 2, 3)
                if last:
                    merge_unit(MGU, 0)
                else:
                    ssm_unit(g + 1, 0)
                end_state(2)
                triangle(6)
                triangle(7)
                if not first:
                    norm_y(g)
                if last:
                    merge_unit(MGU + 1, 1)
                else:
                    ssm_unit(g + 1, 1, 2)
                if not first:
                    scale_y(g, conv[:, 0] if last else norm_by)

            def merge_unit(U, u, place=None):
                unit_low(U, unitL[u], unitH[u], land[u % 2 if place is None else place])
            scan_group(0, first=True)
            with pool.Fori(1, GROUPS - 1) as g:
                scan_group(g)
                norm.end(GROUPS - 1)
            norm.n = 0
            scan_group(GROUPS - 1, last=True)
            norm.base, norm.n = 0, 7 * (GROUPS - 1)
            pool.wait_ge(sem("conv_ready"), 6 * GROUPS + 2)
            gate_y(GROUPS)
            pool.wait_ge(sem("y_scaled"), 4 * GROUPS)
            square_y(GROUPS, 0, 1, 2, 3)
            merge_unit(MGU + 2, 2)
            merge_unit(MGU + 3, 3)
            norm_y(GROUPS)
            scale_y(GROUPS, conv[:, 0])
            with pool.Fori(1, KT) as n:
                for v in range(4):
                    merge_unit(4 * n + (MGU + v), v)
            with pool.Fori(0, KT) as n:
                for v in range(3):
                    merge_unit(3 * n + (MGU + 4 * KT + v), v, place=v)
            pool.wait_ge(sem("ms_ready"), TT + 2)
            pool.tensor_tensor(rstd, ms, powm[:, 0:4], ALU.pow).then_inc(sem("rstd_ready"), 1)
            pool.wait_ge(sem("planned"), 1)
            pool.wait_ge(sem("h2_stored"), 16)
            for T in range(EXPERTS + 1):
                if T >= 2:
                    pool.wait_ge(sem("e_hg_turned"), T - 1)
                pool.indirect_dma_start(out=gath[:, T % 2, :], out_offset=None, in_=h2_dram,
                                        in_offset=bass.IndirectOffsetOnAxis(ap=token_of[:, T:T + 1], axis=0)
                                        ).then_inc(sem(f"e_hg{T % 2}_loaded"), 16)
            pool.wait_ge(sem("e_hg_turned"), EXPERTS + 1)
            pool.sem_inc(sem("place_ready"), 1)
            n_extra = pool.value_load(extra_of[0:1, 7:8], min_val=0, max_val=EXTRA)
            with pool.Fori(0, EXTRA) as x:
                with pool.If(x < n_extra):
                    pool.wait_ge(sem("x_hg_turned"), x + 1)
                    pool.tensor_tensor(r16, r16, r16, ALU.add)
                    pool.tensor_copy(place_now[:], token_of[:, bass.ds(x + EXPERTS, 1)]).then_inc(sem("place_ready"), 1)
                    pool.wait_ge(sem("place_ready"), x + 2)
                    pool.tensor_tensor(m16, m16, m16, ALU.add)
                    pool.indirect_dma_start(out=gath[:, 0, :], out_offset=None, in_=h2_dram,
                                            in_offset=bass.IndirectOffsetOnAxis(ap=place_now[:, 0:1], axis=0)
                                            ).then_inc(sem("x_hg0_loaded"), 16)
            pool.wait_ge(sem("rows_stored"), 1)
            pool.wait_ge(sem("e_hgT_ready"), EXPERTS + 2)
            for c in range(TT):
                for m in range(2):
                    pool.indirect_dma_start(out=pick[c][:, m, :], out_offset=None, in_=y_dram,
                                            in_offset=bass.IndirectOffsetOnAxis(ap=slot_of[:, m, c:c + 1], axis=0)
                                            ).then_inc(sem(f"rows{c}_loaded"), 16)
            for c in range(TT):
                pool.wait_ge(sem("ms_ready"), TT + 3 + c)
                pool.tensor_tensor(rstd[:, c:c + 1], ms[:, c:c + 1], powm[:, 0:1], ALU.pow).then_inc(sem("rstd_ready"), 1)

        @block.tensor
        def _(pe):
            pe.wait_ge(sem("consts_ready"), 3)
            def turn_x(c):
                pe.wait_ge(sem("xn_ready"), c + 1)
                for k in range(KT):
                    ins = pe.transpose(psum[2 * c + k // 4][:, k % 4 * P:(k % 4 + 1) * P], x_sb[:, c, k * P:(k + 1) * P], ident[:])
                    if k % 4 == 3:
                        ins.then_inc(sem("x_turned"), 1)

            def project(c, w, cn, bank):
                for k in range(KT):
                    ins = pe.matmul(psum[bank][:, 0:cn], hT[:, k, c * P:(c + 1) * P], w[:, k, :],
                                    start=k == 0, stop=k == KT - 1)
                ins.then_inc(sem("kq_projected"), 1)

            def project_kv(c):
                if c == 0:
                    pe.wait_ge(sem("w_kv_loaded"), 16)
                pe.wait_ge(sem("hT_ready"), 2 * c + 2)
                project(c, wa_kv, KVD, c)
            turn_x(0)
            turn_x(1)
            project_kv(0)
            turn_x(2)
            project_kv(1)
            turn_x(3)
            project_kv(2)
            project_kv(3)
            pe.wait_ge(sem("w_q_loaded"), 16)
            for c in range(TT):
                project(c, wb_q, Q_LORA, TT + c)

            def products(bank, weights, acts, first=True, last=True, ready=None):
                (wh, wl), (high, low) = weights, acts
                for k in range(KT):
                    if ready:
                        pe.wait_ge(sem(ready[0]), ready[1] + k + 1)
                    w = slice(k * P, (k + 1) * P)
                    pe.matmul(bank, wh[:, w], high[:, k, :], start=first and k == 0, stop=False)
                    pe.matmul(bank, wh[:, w], low[:, k, :], start=False, stop=False)
                    ins = pe.matmul(bank, wl[:, w], high[:, k, :], start=False, stop=last and k == KT - 1)
                ins.then_inc(sem("unit_used"), 1)

            def sc_tile(T, i, u, ready=None):
                for j in range(3):
                    pe.wait_ge(sem("unit_low"), 3 * T + j + 1)
                    pe.wait_ge(sem(f"sc_in{u}"), i * 3 + j + 1)
                    products(psum[3 * u + j][:], (sc_high[j], sc_low[j]), (hH, hL), ready=ready)
            pe.wait_ge(sem("kv_taken"), TT)
            sc_tile(0, 0, 0, ready=("h_low", 0))
            pe.wait_ge(sem("latents_scaled"), 3)
            pe.wait_ge(sem("q_taken"), TT)
            for j in range(QT + RT + 1):
                b = 4 + j % 4
                if j >= 4:
                    pe.wait_ge(sem("latents_taken"), j - 3)
                for c in range(TT):
                    src = (qraw[:, c, j * P:(j + 1) * P] if j < QT else
                           kvn[:, c, (j - QT) * P:(j - QT + 1) * P] if j < QT + RT else kdup[:, c, :])
                    ins = pe.transpose(psum[b][:, c * P:(c + 1) * P], src, ident[:])
                ins.then_inc(sem("latents_turned"), 1)
            pe.wait_ge(sem("da_ready"), 1)
            for c in range(TT):
                for j, m in enumerate((tri_le, tri_gt, ones)):
                    ins = pe.matmul(psum[3][:, (j * TT + c) * SSM_HEADS:(j * TT + c + 1) * SSM_HEADS], m[:], da_sb[:, c, :],
                                    start=True, stop=True)
            ins.then_inc(sem("sums_ready"), 1)
            pe.wait_ge(sem("latents_taken"), QT + RT + 1)
            pe.wait_ge(sem("w_idx_loaded"), 16)
            for j in range(IDX_HEADS // 2):
                for k in range(QT):
                    ins = pe.matmul(psum[4 + j][:], wd_idx[:, k, j * P:(j + 1) * P], cqT[:, k, :], start=k == 0, stop=k == QT - 1)
                ins.then_inc(sem("qi_projected"), 1)
            pe.wait_ge(sem("qi_ready"), IDX_HEADS // 2)
            n = 0
            for b in range(1, TT):
                for h in range(IDX_HEADS):
                    if n >= 2:
                        pe.wait_ge(sem("dots_taken"), n - 1)
                    half = slice(64 * (h % 2), 64 * (h % 2) + 64)
                    pe.matmul(psum[6 + n % 2][:, 0:(b + 1) * P], qiT[half, h // 2, b * P:(b + 1) * P],
                              kidxT[half, 0:(b + 1) * P], start=True, stop=True).then_inc(sem("dots_ready"), 1)
                    n += 1
            pe.wait_ge(sem("sums_taken"), 1)
            with pe.Fori(0, KT // 2 - 1) as i:
                sc_tile(2 * i + 1, i, 1)
                sc_tile(2 * i + 2, i + 1, 0)
            sc_tile(KT - 1, KT // 2 - 1, 1)
            for u in range(2):
                pe.wait_ge(sem(f"sc_in{u}"), 3 + 3 * KT // 2)
            with pe.Fori(0, TT) as hg:
                def head(k):
                    pe.wait_ge(sem("head_taken"), hg * HEADS_N + k + 1)
                    return psum[k % 2]

                def half(h):
                    return slice(64 * (h % 2), 64 * (h % 2) + 64)

                def score(s):
                    b, h = s // HQ, s % HQ
                    pe.wait_ge(sem("logits_taken"), hg * 16 + s + 1)
                    pe.matmul(psum[SCORE_BANKS[s % 4]][:, 0:(b + 1) * P], qT[half(h), h // 2, b * P:(b + 1) * P],
                              kT[half(h), h // 2, 0:(b + 1) * P], start=True, stop=True).then_inc(sem("logits_done"), 1)

                def out_heads(b):
                    pe.wait_ge(sem("turned_taken"), hg * 16 + 4 * b + 4 + 2)
                    bank = head(6 + b)
                    for h in range(HQ):
                        for kb in range(b + 1):
                            ins = pe.matmul(bank[half(h), (h // 2) * P:(h // 2 + 1) * P], v_sb[:, kb, h * HEAD:(h + 1) * HEAD],
                                            PT[:, b % 2, kb, h * P:(h + 1) * P], start=kb == 0, stop=kb == b)
                    ins.then_inc(sem("head_done"), 1)

                pe.wait_ge(sem("w_qk_loaded"), hg * 16 + 16)
                for j in range(2):
                    bank = head(j)
                    for k in range(QT):
                        ins = pe.matmul(bank[:], w_uq[:, k, j * P:(j + 1) * P], cqT[:, k, :], start=k == 0, stop=k == QT - 1)
                    ins.then_inc(sem("head_done"), 1)
                for j in range(2):
                    bank = head(2 + j)
                    for r in range(RT):
                        ins = pe.matmul(bank[:], w_uk[:, r, j * P:(j + 1) * P], kvnT[:, r, :], start=r == 0, stop=r == RT - 1)
                    ins.then_inc(sem("head_done"), 1)
                pe.wait_ge(sem("w_uv_loaded"), hg * 16 + 16)
                for j in range(2):
                    bank = head(4 + j)
                    for c in range(2):
                        for r in range(RT):
                            ins = pe.matmul(bank[:, c * HQ * HEAD:(c + 1) * HQ * HEAD], kvnT[:, r, (2 * j + c) * P:(2 * j + c + 1) * P],
                                            w_uv[:, r, :], start=r == 0, stop=r == RT - 1)
                    ins.then_inc(sem("head_done"), 1)
                pe.wait_ge(sem("head_taken"), hg * HEADS_N + 4 + 2)
                for s in range(LAG):
                    score(s)
                for s in range(16):
                    b = s // HQ
                    if s + LAG < 16:
                        score(s + LAG)
                    pe.wait_ge(sem("probs_ready"), hg * 16 + s + 1)
                    pe.wait_ge(sem("turned_taken"), hg * 16 + s + 1)
                    for kb in range(b + 1):
                        ins = pe.transpose(psum[4 + s % 2][:, kb * P:(kb + 1) * P], probs[:, s % RING, kb * P:(kb + 1) * P], ident[:])
                    ins.then_inc(sem("turned"), 1)
                    if s % 4 == 1 and s > 4:
                        out_heads(s // 4 - 1)
                out_heads(TT - 1)
            pe.wait_ge(sem("head_taken"), HEADS_N * TT + 2)
            pe.wait_ge(sem("logits_taken"), 16 * TT + 4)
            def ssm_unit(g, u, bank):
                pe.wait_ge(sem("unit_low"), SSM_UNITS * g + (SCU + u + 1))
                products(bank, ssm_units[SLOT[u]], (hH, hL))

            def project_group(g):
                for j in range(6):
                    if j < 4:
                        pe.wait_ge(sem("diag_taken"), g * 4 + j + 1)
                    elif j == 4:
                        pe.wait_ge(sem("btok_ready"), g + 1)
                        pe.wait_ge(sem("off_taken"), g * 3 + 1)
                    else:
                        pe.wait_ge(sem("cb_ready"), g + 1)
                    ssm_unit(g, j, psum[j][:])

            def pair(g, kind, c):
                pe.wait_ge(sem("pair_taken"), pair_at(g, kind, c))
                return psum[6 + PAIR.index((kind, c)) % 2]

            def norm_sums(g):
                pe.wait_ge(sem("y_squared"), g)
                bank = pair(g, "n", 0)
                for c in range(TT):
                    ins = pe.matmul(bank[:, c:c + 1], conv[:, 0, c * P:(c + 1) * P], ones[:, 0:1], start=True, stop=True)
                ins.then_inc(sem("pair_done"), 1)

            def norm_spread(g):
                pe.wait_ge(sem("diag_ready"), g)
                pe.matmul(pair(g, "n", 1)[:], ones[:], conv[:, 1], start=True, stop=True).then_inc(sem("pair_done"), 1)

            def turn_y(g):
                pe.wait_ge(sem("diag_taken"), g * 4 + 4)
                pe.wait_ge(sem("yn_ready"), g * 3 + 1)
                for j in range(4):
                    bank = pair(g, "y", j)
                    for c in range(TT):
                        ins = pe.transpose(bank[:, c * P:(c + 1) * P], y[:, c, j * P:(j + 1) * P], ident[:])
                    ins.then_inc(sem("pair_done"), 1)

            def scan_group(g, first=False):
                def gate_z(j):
                    ssm_unit(g, 6 + j, pair(g, "z", j)[:])

                def sums(k):
                    pe.wait_ge(sem("tri_ready"), g * 8 + k + 1)
                    pe.matmul(pair(g, "s", k)[:], tri_gt[:], da_tri[:, k % 2].rearrange("p h l -> p (h l)"),
                              start=True, stop=True).then_inc(sem("pair_done"), 1)
                gate_z(0)
                gate_z(1)
                pe.wait_ge(sem("conv_ready"), g * 6 + 6 + 2)
                for c in range(TT):
                    for j in range(4):
                        ins = pe.transpose(psum[c][:, j * P:(j + 1) * P], xsT[:, j, c * P:(c + 1) * P], ident[:])
                    ins.then_inc(sem("x_ready"), 1)
                for c in range(TT):
                    ins = pe.transpose(psum[4][:, c * P:(c + 1) * P], xsT[:, 4, c * P:(c + 1) * P], ident[:])
                ins.then_inc(sem("b_turned"), 1)
                for c in range(TT):
                    ins = pe.matmul(psum[5][:, c * P:(c + 1) * P], xsT[:, 4, c * P:(c + 1) * P], xsT[:, 5, c * P:(c + 1) * P],
                                    start=True, stop=True)
                ins.then_inc(sem("cb_done"), 1)
                sums(0)
                sums(1)
                for c in range(TT):
                    if c in (0, 2):
                        gate_z(2 + c // 2)
                    if c < TT - 1:
                        sums(2 * c + 2)
                        sums(2 * c + 3)
                        if c == 2 and not first:
                            norm_sums(g)
                        pe.wait_ge(sem("xend_ready"), g * 3 + c + 1)
                        if c == 0:
                            pe.wait_ge(sem("btok_ready"), g + 2)
                            pe.wait_ge(sem("cb_ready"), g + 2)
                    if c > 0:
                        pe.wait_ge(sem("state_ready"), g * 3 + c)
                        pe.wait_ge(sem("off_taken"), g * 3 + c)
                        pe.matmul(psum[4][:], xsT[:, 5, c * P:(c + 1) * P], state, start=True, stop=True).then_inc(sem("off_done"), 1)
                    if c < TT - 1:
                        pe.matmul(psum[5][:], b_tok[:, c * P:(c + 1) * P], xend[:, c % 2], start=True, stop=True).then_inc(sem("state_done"), 1)
                    pe.wait_ge(sem("m_ready"), g * 8 + 2 * c + 2 + 2)
                    pe.wait_ge(sem("xdt_ready"), g * 4 + c + 1)
                    for h in range(GH):
                        ins = pe.matmul(psum[c][:, h * HEAD:(h + 1) * HEAD], mix_m[:, (2 * c + h // 4) % 4, h % 4, :],
                                        xdt[:, c, h * HEAD:(h + 1) * HEAD], start=True, stop=True)
                    ins.then_inc(sem("diag_done"), 1)
                if not first:
                    norm_spread(g)
            project_group(0)
            scan_group(0, first=True)
            with pe.Fori(1, GROUPS) as g:
                project_group(g)
                turn_y(g)
                scan_group(g)
            units = list(zip(unitH, unitL))


            def gate(q, m, u):
                if q is not None:
                    pe.wait_ge(sem("gate_taken"), q)
                pe.wait_ge(sem("unit_low"), m + 1)
                products(psum[0][:], units[u], (hH, hL))

            def branch(q, m, u, acts, ready, kt=1):
                if q is not None:
                    pe.wait_ge(sem("merged"), q)
                for j in range(kt):
                    pe.wait_ge(sem("unit_low"), m + (j + 1))
                    products(psum[1][:], units[u + j], [a[:, j * KT:(j + 1) * KT] for a in acts],
                             first=j == 0, last=j == kt - 1, ready=("split_low", ready + j * KT))
            turn_y(GROUPS)
            pe.wait_ge(sem("diag_taken"), 4 * GROUPS + 2)
            gate(None, MGU, 0)
            branch(None, MGU + 1, 1, (oH, oL), 0)
            norm_sums(GROUPS)
            gate(1, MGU + 2, 2)
            norm_spread(GROUPS)
            branch(1, MGU + 3, 3, (gH, gL), KT)
            with pe.Fori(1, KT) as n:
                gate(2 * n, 4 * n + MGU, 0)
                branch(2 * n, 4 * n + (MGU + 1), 1, (oH, oL), 0)
                gate(2 * n + 1, 4 * n + (MGU + 2), 2)
                branch(2 * n + 1, 4 * n + (MGU + 3), 3, (gH, gL), KT)
            with pe.Fori(0, KT) as n:
                gate(n + 2 * KT, 3 * n + (MGU + 4 * KT), 0)
                branch(n + 2 * KT, 3 * n + (MGU + 4 * KT + 1), 1, (ynH, ynL), 2 * KT, kt=2)
            pe.wait_ge(sem("w_mix_loaded"), KT * 16)
            pe.wait_ge(sem("pair_taken"), pair_at(GROUPS, "n", 1) + 2)
            pe.wait_ge(sem("merged"), 3 * KT)
            for b in range(8):
                c, half = b // 2, b % 2
                for k in range(KT):
                    ins = pe.matmul(psum[b][:], mergedT[:, k, c * P:(c + 1) * P], w_mix[half][:, k, :], start=k == 0, stop=k == KT - 1)
                ins.then_inc(sem("mix_done"), 1)
            pe.wait_ge(sem("h2_ready"), TT)
            for k in range(KT):
                for c in range(TT):
                    ins = pe.transpose(psum[k][:, c * P:(c + 1) * P], h2[:, c, k * P:(k + 1) * P], ident[:])
                ins.then_inc(sem("h2_turned"), 1)
            pe.wait_ge(sem("h2T_ready"), KT)
            pe.wait_ge(sem("router_final_loaded"), 32)
            for k in range(KT):
                ins = pe.matmul(psum[0][0:NR, :], w_router[:, k, :], h2T[:, k, :], start=k == 0, stop=k == KT - 1)
            ins.then_inc(sem("routed"), 1)
            pe.wait_ge(sem("routed_taken"), 1)
            for c in range(TT):
                ins = pe.transpose(psum[7][:, c * NR:(c + 1) * NR], logitsT[:, c * P:(c + 1) * P], ident[0:NR, 0:NR])
            ins.then_inc(sem("routed"), 1)
            pe.wait_ge(sem("chosen"), 1)
            pe.matmul(psum[4][:, 0:TT * EXPERTS], tri_le[:], chosen.rearrange("p c e -> p (c e)"), start=True, stop=False)
            pe.matmul(psum[4][:, 0:TT * EXPERTS], ones[:], before[:, 0:TT].rearrange("p c e -> p (c e)"), start=False, stop=True)
            pe.matmul(psum[4][:, TT * EXPERTS:(TT + 1) * EXPERTS], ones[:], before[:, TT], start=True, stop=True).then_inc(sem("counted"), 1)
            pe.wait_ge(sem("one_hot_ready"), 1)
            for a in range(8):
                ins = pe.matmul(psum[5][:, 0:24], one_hot[:, a, :], tile_hot[:, a, :], start=a == 0, stop=a == 7)
            ins.then_inc(sem("placed"), 1)

            def turn_tokens(T, u, loaded, pre):
                pe.wait_ge(sem(f"{pre}hg{u}_loaded"), loaded)
                pe.wait_ge(sem(pre + "hgT_ready"), T + 1)
                for k in range(KT):
                    ins = pe.transpose(psum[2 + k // 4][:, k % 4 * P:(k % 4 + 1) * P], gath[:, u, k * P:(k + 1) * P], ident[:])
                ins.then_inc(sem(pre + "hg_turned"), 1)

            def expert_tile(T, u, pre, loads, between):
                pe.wait_ge(sem(pre + "hgT_ready"), T + 2)
                for j, name in enumerate(("gate", "up")):
                    pe.wait_ge(sem(loads[j][0]), loads[j][1])
                    pe.wait_ge(sem(pre + ("sg_ready", "hid_ready")[j]), T + 1)
                    for k in range(KT):
                        ins = pe.matmul(psum[j][:], hgT[:, u, k, :], w_exp[u][j][:, k, :], start=k == 0, stop=k == KT - 1)
                    ins.then_inc(sem(f"{pre}{name}_done"), 1)
                between()
                pe.wait_ge(sem(pre + "hid_ready"), T + 2)
                pe.wait_ge(sem(pre + "hidT_ready"), T + 1)
                for f in range(FT):
                    ins = pe.transpose(psum[4][:, f * P:(f + 1) * P], hid[:, f * P:(f + 1) * P], ident[:])
                ins.then_inc(sem(pre + "hid_turned"), 1)
                pe.wait_ge(sem(pre + "hidT_ready"), T + 2)
                pe.wait_ge(sem(loads[2][0]), loads[2][1])
                for half in range(2):
                    pe.wait_ge(sem(pre + "y_taken"), 2 * T + half + 1)
                    for f in range(FT):
                        ins = pe.matmul(psum[5 + half][:], hidT[:, f, :], w_exp[u][2][:, f, half * 512:(half + 1) * 512],
                                        start=f == 0, stop=f == FT - 1)
                    ins.then_inc(sem(pre + "down_done"), 1)
            pe.wait_ge(sem("planned"), 1)
            turn_tokens(0, 0, 16, "e_")
            with pe.Fori(0, EXPERTS // 2) as i:
                for u in range(2):
                    T = 2 * i + u
                    expert_tile(T, u, "e_", [(f"w_{w}{u}_loaded", i * 16 + 16) for w in ("gate", "up", "down")],
                                lambda: turn_tokens(T + 1, 1 - u, i * 16 + 16 + 16 * u, "e_"))
            pe.wait_ge(sem("e_hgT_ready"), EXPERTS + 2)
            pe.wait_ge(sem("e_y_taken"), 2 * EXPERTS + 2)
            n_extra = pe.value_load(extra_of[0:1, 7:8], min_val=0, max_val=EXTRA)
            with pe.Fori(0, EXTRA) as x:
                with pe.If(x < n_extra):
                    turn_tokens(x, 0, x * 16 + 16, "x_")
                    expert_tile(x, 0, "x_", [("x_w_loaded", x * 48 + 48)] * 3, lambda: None)

        @block.scalar
        def _(act):
            act.wait_ge(sem("params_loaded"), 32)
            for c in range(TT):
                act.wait_ge(sem("kq_projected"), c + 1)
                act.activation(kvraw[:, c, :], psum[c][:, 0:KVD], ACT.Copy).then_inc(sem("kv_taken"), 1)
            def split_h():
                for k in range(KT):
                    act.activation(hH[:, k, :], hT[:, k, :], ACT.Copy).then_inc(sem("h_high"), 1)

            def unit_high(loads, u, high, src):
                act.wait_ge(sem(f"unit{u}_loaded"), loads * 16)
                act.activation(high, src, ACT.Copy).then_inc(sem("unit_high"), 1)
            for u in range(3):
                unit_high(1, u, sc_high[u], sc_land[u])
            split_h()
            for c in range(TT):
                act.wait_ge(sem("kq_projected"), TT + c + 1)
                act.activation(qraw[:, c, :], psum[4 + c][:, 0:Q_LORA], ACT.Copy).then_inc(sem("q_taken"), 1)
            act.wait_ge(sem("dtabs_ready"), 1)
            act.activation(da_sb[:], da_sb[:], ACT.Exp, scale=-1.0).then_inc(sem("dtexp_ready"), 1)
            act.activation(rows[:, R_ALOG:R_ALOG + SSM_HEADS], rows[:, R_ALOG:R_ALOG + SSM_HEADS], ACT.Exp).then_inc(sem("dtexp_ready"), 1)
            for u in range(2):
                act.sem_inc(sem(f"sc_in{u}"), 3)

            def sc_tile(T, i, u, more=True):
                for j in range(3):
                    act.wait_ge(sem("unit_used"), 3 * T + j + 1)
                    if more:
                        unit_high(T + 2, j, sc_high[j], sc_land[j])
                    if j == 0:
                        act.wait_ge(sem(f"sc_gated{u}"), i + 1)
                    act.activation(sc_in[:, u, j, :], psum[3 * u + j][:], ACT.Copy).then_inc(sem(f"sc_in{u}"), 1)
            sc_tile(0, 0, 0)
            for j in range(QT + RT + 1):
                act.wait_ge(sem("latents_turned"), j + 1)
                src = psum[4 + j % 4][:]
                if j < QT:
                    ins = act.activation(cqT[:, j, :], src, ACT.Copy, scale=cols[:, C_QG + j:C_QG + j + 1])
                elif j < QT + RT:
                    ins = act.activation(kvnT[:, j - QT, :], src, ACT.Copy)
                else:
                    ins = act.activation(kidxT, src, ACT.Copy, scale=cols[:, C_KG:C_KG + 1])
                ins.then_inc(sem("latents_taken"), 1)
            act.wait_ge(sem("sums_ready"), 1)
            act.activation(ex_sb[:].rearrange("p a c h -> p (a c h)"), psum[3][:, 0:3 * TT * SSM_HEADS], ACT.Exp).then_inc(sem("sums_taken"), 1)
            for j in range(IDX_HEADS // 2):
                act.wait_ge(sem("qi_projected"), j + 1)
                act.activation(qiT[:, j, :], psum[4 + j][:], ACT.Copy).then_inc(sem("qi_ready"), 1)
            n = 0
            for b in range(1, TT):
                for h in range(IDX_HEADS):
                    act.wait_ge(sem("dots_ready"), n + 1)
                    if n >= 2:
                        act.wait_ge(sem("score_added"), n - 1)
                    act.activation(relu[:, n % 2, 0:(b + 1) * P], psum[6 + n % 2][:, 0:(b + 1) * P], ACT.Relu).then_inc(sem("dots_taken"), 1)
                    n += 1
            with act.Fori(0, KT // 2 - 1) as i:
                sc_tile(2 * i + 1, i, 1)
                sc_tile(2 * i + 2, i + 1, 0)
            sc_tile(KT - 1, KT // 2 - 1, 1, more=False)
            act.wait_ge(sem("bias_ready"), TT - 1)
            act.sem_inc(sem("head_taken"), 2)
            act.sem_inc(sem("turned_taken"), 2)
            with act.Fori(0, TT) as hg:
                def take_head(k):
                    act.wait_ge(sem("head_done"), hg * HEADS_N + k + 1)
                    if k < 2:
                        ins = act.activation(qT[:, k, :], psum[k][:], ACT.Copy)
                    elif k < 4:
                        ins = act.activation(kT[:, k - 2, :], psum[k % 2][:], ACT.Copy)
                    elif k < 6:
                        ins = act.activation(v_sb[:, 2 * (k - 4):2 * (k - 4) + 2, :],
                                             psum[k % 2][:].rearrange("p (c n) -> p c n", c=2), ACT.Copy)
                    else:
                        b = k - 6
                        ins = act.activation(oT[:, bass.ds(hg * 2, 2), b * P:(b + 1) * P],
                                             psum[k % 2][:, 0:2 * P].rearrange("p (j q) -> p j q", j=2), ACT.Copy)
                    ins.then_inc(sem("head_taken"), 1)

                def take_turned(s):
                    b, h = s // HQ, s % HQ
                    act.wait_ge(sem("turned"), hg * 16 + s + 1)
                    act.activation(PT[:, b % 2, 0:b + 1, h * P:(h + 1) * P],
                                   psum[4 + s % 2][:, 0:(b + 1) * P].rearrange("p (k q) -> p k q", k=b + 1), ACT.Copy
                                   ).then_inc(sem("turned_taken"), 1)
                for k in range(6):
                    take_head(k)
                for s in range(19):
                    if s < 16:
                        act.wait_ge(sem("max_ready"), hg * 16 + s + 1)
                        pr = probs[:, s % RING, 0:(s // HQ + 1) * P]
                        act.activation(pr, pr, ACT.Exp, bias=nmax[:, s % RING:s % RING + 1], scale=ATT_SCALE,
                                       accum_out=psums[:, s % RING:s % RING + 1]).then_inc(sem("exp_done"), 1)
                    if s == 3:
                        for u in range(2):
                            act.wait_ge(sem(f"sc_gated{u}"), KT // 2 + 1)
                    if s >= 3:
                        take_turned(s - 3)
                    if s % 4 == 1 and s > 8:
                        take_head(6 + s // 4 - 2)
                take_head(9)
            act.sem_inc(sem("btok_ready"), 1)
            act.sem_inc(sem("y_gated"), 4)
            act.sem_inc(sem("pair_taken"), 2)
            act.sem_inc(sem("conv_ready"), 2)

            def ssm_unit(g, u):
                unit_high(g * (SSM_UNITS // 2) + (KT + u // 2 + 1), u % 2, ssm_units[SLOT[u]][0], ssm_land[u % 2])

            def merge_high(loads, u, place, used=None):
                if used is not None:
                    act.wait_ge(sem("unit_used"), used)
                unit_high(loads + (SSM_LOADS if place < 2 else KT), place, unitH[u], land[place])

            def silu_z(g):
                act.wait_ge(sem("pair_taken"), pair_at(g, "y", 0) - 1 + 2)
                for j in range(4):
                    act.activation(sz[:, j, :], sz[:, j, :], ACT.Silu).then_inc(sem("z_ready"), 1)

            def take_conv(g, first=False):
                for j in range(6):
                    if j == 3 and not first:
                        silu_z(g)
                    act.wait_ge(sem("unit_used"), SSM_UNITS * g + (SCU + j + 1))
                    ssm_unit(g, 3 + j)
                    if j == 5 and not first:
                        take_pair(g, 0, 4)
                    act.wait_ge(sem("conv_out"), g * 6 + j + 1)
                    act.activation(xsT[:, j, :], conv[:, j % 2], ACT.Silu,
                                   bias=cols[:, bass.ds(C_CONV + TAPS + g * 30 + j * 5, 1)]).then_inc(sem("conv_ready"), 1)

            def take_pair(g, first, end, by=norm_by):
                for kind, c in PAIR[first:end]:
                    bank = psum[6 + PAIR.index((kind, c)) % 2][:]
                    if kind == "z":
                        act.wait_ge(sem("unit_used"), SSM_UNITS * g + (SCU + 6 + c + 1))
                    else:
                        act.wait_ge(sem("pair_done"), pair_made(g, kind, c))
                    if kind == "y":
                        ins = act.activation(ynT[:, bass.ds(g * 4 - 4 + c, 1), :].rearrange("p o s -> p (o s)"), bank, ACT.Copy)
                    elif kind == "z":
                        act.wait_ge(sem("y_gated"), g * 4 - 4 + c + 1 + 4)
                        ins = act.activation(sz[:, c, :], bank, ACT.Copy)
                    elif kind == "s":
                        act.wait_ge(sem("m_ready"), g * 8 + c + 1)
                        ins = act.activation(decay[:, c % 2].rearrange("p h l -> p (h l)"), bank, ACT.Exp)
                    elif c == 0:
                        ins = act.activation(m16, bank[:, 0:TT], ACT.Copy, scale=1.0 / 512, bias=EPS)
                    else:
                        ins = act.activation(by, bank, ACT.Copy)
                    ins.then_inc(sem("pair_taken"), 1)

            def take_scan(g, first=False, last=False):
                take_pair(g, 4, 6)
                ssm_unit(g, 9)
                if last:
                    merge_high(1, 0, 0)
                else:
                    ssm_unit(g + 1, 0)
                act.wait_ge(sem("b_turned"), g + 1)
                act.activation(b_tok, psum[4][:], ACT.Copy).then_inc(sem("btok_ready"), 1)
                take_pair(g, 6, 14)
                if last:
                    merge_high(1, 1, 1)
                else:
                    ssm_unit(g + 1, 1)
                    ssm_unit(g + 1, 2)
                take_pair(g, 14, 16)
                if first:
                    act.wait_ge(sem("pair_taken"), pair_at(0, "s", 7) + 2)
                    act.sem_inc(sem("pair_done"), 2)
                    act.sem_inc(sem("pair_taken"), 2)
                else:
                    take_pair(g, 16, 18, by=conv[:, 0] if last else norm_by)
            act.wait_ge(sem("unit_low"), SCU + 2)
            ssm_unit(0, 2)
            take_conv(0, first=True)
            take_scan(0, first=True)
            with act.Fori(1, GROUPS - 1) as g:
                take_conv(g)
                take_scan(g)
            take_conv(GROUPS - 1)
            take_scan(GROUPS - 1, last=True)
            def high_parts(dst, src, kn, gain=None):
                for k in range(kn):
                    scale = 1.0 if gain is None else cols[:, gain + k:gain + k + 1]
                    act.activation(dst[:, k, :], src[:, k, :], ACT.Copy, scale=scale).then_inc(sem("split_high"), 1)

            def gate(q, used, first=False):
                act.wait_ge(sem("unit_used"), used)
                if not first:
                    act.wait_ge(sem("merged"), q)
                act.activation(sig, psum[0][:], ACT.Sigmoid).then_inc(sem("gate_taken"), 1)
            silu_z(GROUPS)
            take_pair(GROUPS, 0, 4)
            high_parts(oH, oT, KT)
            gate(0, MGU + 1, first=True)
            act.wait_ge(sem("split_low"), KT)
            merge_high(2, 2, 0)
            merge_high(2, 3, 1)
            high_parts(gH, gatedT, KT)
            take_pair(GROUPS, 16, 17)
            for v in (0, 1):
                merge_high(3, v, v, MGU + v + 1)
            gate(1, MGU + 3)
            take_pair(GROUPS, 17, 18, by=conv[:, 0])
            for v in (2, 3):
                merge_high(4, v, v - 2, MGU + v + 1)
            with act.Fori(1, KT - 1) as n:
                for j in range(2):
                    gate(2 * n + j, 4 * n + (MGU + 2 * j + 1))
                    for v in (2 * j, 2 * j + 1):
                        merge_high(2 * n + (j + 3), v, v % 2, 4 * n + (MGU + v + 1))
            gate(2 * KT - 2, MGU + 4 * KT - 3)
            for v in range(2):
                merge_high(2 * KT + 1, v, v, MGU + 4 * KT - 3 + v)
            gate(2 * KT - 1, MGU + 4 * KT - 1)
            merge_high(1, 2, 2, MGU + 4 * KT - 1)
            act.wait_ge(sem("unit_used"), MGU + 4 * KT)
            act.wait_ge(sem("y_scaled"), 4 * GROUPS + 4)
            high_parts(ynH, ynT, 2 * KT, gain=C_NG)
            with act.Fori(0, KT - 1) as n:
                gate(n + 2 * KT, 3 * n + (MGU + 4 * KT + 1))
                for v in range(3):
                    merge_high(n + (2 * KT + 2 if v < 2 else 2), v, v, 3 * n + (MGU + 4 * KT + v + 1))
            gate(3 * KT - 1, MGU + 7 * KT - 2)
            for k in range(KT):
                act.wait_ge(sem("h2_turned"), k + 1)
                act.activation(h2T[:, k, :], psum[k][:], ACT.Copy, scale=cols[:, C_G2 + k:C_G2 + k + 1]).then_inc(sem("h2T_ready"), 1)
            act.wait_ge(sem("routed"), 1)
            act.activation(logitsT, psum[0][0:NR, :], ACT.Copy).then_inc(sem("routed_taken"), 1)
            act.wait_ge(sem("rt_in"), 1)
            act.activation(rsc[:, 2, 0:16], rsc[:, 1, 0:16], ACT.Exp).then_inc(sem("rt_exp"), 1)
            act.wait_ge(sem("rt_in"), 2)
            act.activation(rsc[:, 10, 0:4], rsc[:, 10, 0:4], ACT.Exp).then_inc(sem("rt_exp"), 1)
            def expert_tile(T, pre):
                act.wait_ge(sem(pre + "gate_done"), T + 1)
                act.wait_ge(sem(pre + "hid_ready"), T + 1)
                act.activation(sg, psum[0][:], ACT.Silu).then_inc(sem(pre + "sg_ready"), 1)
                act.wait_ge(sem(pre + "hid_turned"), T + 1)
                act.activation(hidT.rearrange("p f j -> p (f j)"), psum[4][:], ACT.Copy).then_inc(sem(pre + "hidT_ready"), 1)
                for half in range(2):
                    act.wait_ge(sem(pre + "down_done"), 2 * T + half + 1)
                    if half == 0:
                        act.wait_ge(sem(pre + "y_stored"), T * 16 + 16)
                    act.activation(yt[:, half * 512:(half + 1) * 512], psum[5 + half][:], ACT.Copy).then_inc(sem(pre + "y_taken"), 1)
            act.wait_ge(sem("planned"), 1)
            for pre in ("e_", "x_"):
                act.sem_inc(sem(pre + "sg_ready"), 1)
                act.sem_inc(sem(pre + "hidT_ready"), 1)
                act.sem_inc(sem(pre + "y_taken"), 2)
            with act.Fori(0, EXPERTS) as T:
                expert_tile(T, "e_")
            act.wait_ge(sem("e_y_stored"), EXPERTS * 16 + 16)
            n_extra = act.value_load(extra_of[0:1, 7:8], min_val=0, max_val=EXTRA)
            with act.Fori(0, EXTRA) as x:
                with act.If(x < n_extra):
                    expert_tile(x, "x_")
            for c in range(TT):
                act.wait_ge(sem("rows_added"), c + 1)
                act.activation(sq, x2[:, c, :], ACT.Square, accum_out=ms[:, c:c + 1]).then_inc(sem("x_squared"), 1)
                act.wait_ge(sem("x_squared"), c + 1)

        @block.vector
        def _(dve):
            own = Marks(dve, sem("dve_own"))
            def gain_h(c):
                for j in range(2):
                    dve.wait_ge(sem("x_turned"), 2 * c + j + 1)
                    g1cols = cols[:, C_G1 + 4 * j:C_G1 + 4 * j + 4].unsqueeze(2).to_broadcast([P, 4, P])
                    dve.tensor_tensor(hT[:, 4 * j:4 * j + 4, c * P:(c + 1) * P], psum[2 * c + j][:].rearrange("p (k t) -> p k t", k=4),
                                      g1cols, ALU.mult).then_inc(sem("hT_ready"), 1)
            for c in range(TT):
                dve.wait_ge(sem(f"x{c}_loaded"), 16)
                own.mark(dve.tensor_tensor_reduce(sq, x_sb[:, c, :], x_sb[:, c, :], 1.0, 0.0, ALU.mult, ALU.add, ms[:, c:c + 1]))
                own.settle()
                dve.tensor_scalar(ms[:, c:c + 1], ms[:, c:c + 1], 1.0 / D, EPS, ALU.mult, ALU.add).then_inc(sem("ms_ready"), 1)
                if c == 1:
                    dve.wait_ge(sem("params_loaded"), 32)
                if c > 0:
                    gain_h(c - 1)
                dve.wait_ge(sem("rstd_ready"), c + 1)
                dve.tensor_scalar(x_sb[:, c, :], x_sb[:, c, :], rstd[:, c:c + 1], None, ALU.mult).then_inc(sem("xn_ready"), 1)
            gain_h(TT - 1)
            dve.wait_ge(sem("kv_taken"), TT)
            dve.wait_ge(sem("params_loaded"), 32)
            for c in range(TT):
                a = kvraw[:, c, 0:KV_LORA]
                own.mark(dve.tensor_tensor_reduce(sq[:, 0:KV_LORA], a, a, 1.0, 0.0, ALU.mult, ALU.add, ms2[:, 4 + c:5 + c]))
                a = kvraw[:, c, KV_LORA:KV_LORA + D_IDX]
                own.mark(dve.tensor_tensor_reduce(sq[:, 256:256 + D_IDX], a, a, 1.0, 0.0, ALU.mult, ALU.add, ms2[:, 8 + c:9 + c]))
                own.settle()
            dve.wait_ge(sem("q_taken"), TT)
            for c in range(TT):
                own.mark(dve.tensor_tensor_reduce(sq[:, 0:Q_LORA], qraw[:, c, :], qraw[:, c, :], 1.0, 0.0, ALU.mult, ALU.add, ms2[:, c:c + 1]))
                own.settle()
            own.mark(dve.tensor_scalar(ms2[:, 0:4], ms2[:, 0:4], 1.0 / Q_LORA, EPS, ALU.mult, ALU.add))
            own.mark(dve.tensor_scalar(ms2[:, 4:8], ms2[:, 4:8], 1.0 / KV_LORA, EPS, ALU.mult, ALU.add))
            dve.tensor_scalar(ms2[:, 8:12], ms2[:, 8:12], 1.0 / D_IDX, EPS, ALU.mult, ALU.add).then_inc(sem("ms_ready"), 1)
            own.settle()
            dtb = rows[:, R_DTB:R_DTB + SSM_HEADS]
            own.mark(dve.tensor_tensor(dt_sb[:], kvraw[:, :, KVC:KVD],
                                       dtb.unsqueeze(1).to_broadcast([P, TT, SSM_HEADS]), ALU.add))
            own.settle()
            own.mark(dve.tensor_scalar(da_sb[:], dt_sb[:], -1.0, None, ALU.mult))
            own.settle()
            dve.tensor_tensor(da_sb[:], da_sb[:], dt_sb[:], ALU.max).then_inc(sem("dtabs_ready"), 1)
            dve.wait_ge(sem("rstd_ready"), TT + 1)
            for c in range(TT):
                own.mark(dve.tensor_scalar(qraw[:, c, :], qraw[:, c, :], rstd2[:, c:c + 1], None, ALU.mult))
                own.mark(dve.scalar_tensor_tensor(out=kvn[:, c, :], in0=kvraw[:, c, 0:KV_LORA], scalar=rstd2[:, 4 + c:5 + c],
                                                  in1=rows[:, R_KVG:R_KVG + KV_LORA], op0=ALU.mult, op1=ALU.mult))
                for u in range(2):
                    own.mark(dve.tensor_scalar(kdup[:, c, u * D_IDX:(u + 1) * D_IDX], kvraw[:, c, KV_LORA:KV_LORA + D_IDX],
                                               rstd2[:, 8 + c:9 + c], None, ALU.mult))
            own.settle()
            dve.tensor_scalar(widx, kvraw[:, :, KV_LORA + D_IDX:KVC], IDX_SCALE, None, ALU.mult).then_inc(sem("latents_scaled"), 3)
            dve.wait_ge(sem("dtexp_ready"), 2)
            lu, ls, lp = da_sb[:], relu_tmp(relu, 0), relu_tmp(relu, 1)
            ls2 = relu_tmp(relu, 2)
            own.mark(dve.tensor_scalar(ls, lu, 2.0, None, ALU.add))
            own.settle()
            own.mark(dve.reciprocal(ls, ls))
            own.settle()
            own.mark(dve.tensor_tensor(ls, lu, ls, ALU.mult))
            own.settle()
            own.mark(dve.tensor_tensor(ls2, ls, ls, ALU.mult))
            own.settle()
            own.mark(dve.tensor_scalar(lp, ls2, 1.0 / 15, 1.0 / 13, ALU.mult, ALU.add))
            own.settle()
            for d in (11, 9, 7, 5, 3, 1):
                own.mark(dve.tensor_tensor(lp, lp, ls2, ALU.mult))
                own.settle()
                own.mark(dve.tensor_scalar(lp, lp, 1.0 / d, None, ALU.add))
                own.settle()
            own.mark(dve.scalar_tensor_tensor(out=lp, in0=lp, scalar=2.0, in1=ls, op0=ALU.mult, op1=ALU.mult))
            own.settle()
            own.mark(dve.scalar_tensor_tensor(out=dt_sb[:], in0=dt_sb[:], scalar=0.0, in1=lp, op0=ALU.max, op1=ALU.add))
            own.settle()
            ea = rows[:, R_ALOG:R_ALOG + SSM_HEADS].unsqueeze(1).to_broadcast([P, TT, SSM_HEADS])
            dve.scalar_tensor_tensor(out=da_sb[:], in0=dt_sb[:], scalar=-1.0, in1=ea, op0=ALU.mult, op1=ALU.mult).then_inc(sem("da_ready"), 1)
            n = 0
            for b in range(1, TT):
                sc = bias[:, BIAS_AT[b]:BIAS_AT[b] + (b + 1) * P]
                for h in range(IDX_HEADS):
                    dve.wait_ge(sem("dots_taken"), n + 1)
                    r = relu[:, n % 2, 0:(b + 1) * P]
                    if h == 0:
                        ins = dve.tensor_scalar(sc, r, widx[:, b, h:h + 1], None, ALU.mult)
                    else:
                        dve.wait_ge(sem("score_added"), n)
                        ins = dve.scalar_tensor_tensor(out=sc, in0=r, scalar=widx[:, b, h:h + 1], in1=sc, op0=ALU.mult, op1=ALU.add)
                    ins.then_inc(sem("score_added"), 1)
                    n += 1
                dve.wait_ge(sem("score_added"), n)
                dve.engine_nop().then_inc(sem("score_ready"), 1)
            for b in range(1, TT):
                sc = bias[:, BIAS_AT[b]:BIAS_AT[b] + (b + 1) * P]
                dve.wait_ge(sem("score_hidden"), b)
                for r in range(TOPK // 8):
                    own.mark(dve.max(m8, sc))
                    own.settle()
                    own.mark(dve.match_replace(sc, m8, sc, TAKEN))
                    own.settle()
                dve.tensor_scalar(sc, sc, 0.5 * (UNSEEN + TAKEN), -BIG, ALU.is_gt, ALU.mult).then_inc(sem("bias_ready"), 1)
            dve.wait_ge(sem("consts_ready"), 4)
            dve.sem_inc(sem("logits_taken"), 4)
            with dve.Fori(0, TT) as hg:
                def largest(s):
                    b = s // HQ
                    n = (b + 1) * P
                    dve.wait_ge(sem("logits_done"), hg * 16 + s + 1)
                    dve.memset(waited, 0.0)
                    dve.tensor_tensor_reduce(probs[:, s % RING, 0:n], psum[SCORE_BANKS[s % 4]][:, 0:n], bias[:, BIAS_AT[b]:BIAS_AT[b] + n],
                                             1.0, TAKEN, ALU.add, ALU.max, pmax[:, s % RING:s % RING + 1]).then_inc(sem("logits_taken"), 1)
                    dve.wait_ge(sem("logits_taken"), hg * 16 + s + 1 + 4)
                    dve.tensor_scalar(nmax[:, s % RING:s % RING + 1], pmax[:, s % RING:s % RING + 1], -ATT_SCALE, None, ALU.mult).then_inc(sem("max_ready"), 1)

                def divide(s):
                    n = (s // HQ + 1) * P
                    dve.wait_ge(sem("exp_done"), hg * 16 + s + 1)
                    dve.reciprocal(pinv[:, s % RING:s % RING + 1], psums[:, s % RING:s % RING + 1]).then_inc(sem("pinv_ready"), 1)
                    dve.wait_ge(sem("pinv_ready"), hg * 16 + s + 1)
                    pr = probs[:, s % RING, 0:n]
                    dve.tensor_scalar(pr, pr, pinv[:, s % RING:s % RING + 1], None, ALU.mult).then_inc(sem("probs_ready"), 1)

                for s in range(18):
                    if s < 16:
                        largest(s)
                    if s >= 2:
                        divide(s - 2)
            dve.wait_ge(sem("head_done"), HEADS_N * TT)
            dve.sem_inc(sem("cb_ready"), 1)
            dve.sem_inc(sem("m_ready"), 2)
            dve.sem_inc(sem("off_taken"), 1)
            dve.sem_inc(sem("yn_ready"), 1)
            dve.sem_inc(sem("diag_taken"), 4)
            with dve.Fori(0, GROUPS) as g:
                own.loop(i=g, per=6 * 3 + 2)
                for j in range(6):
                    w = [cols[:, bass.ds(C_CONV + k + g * 30 + j * 5, 1)] for k in range(TAPS)]
                    a, src = conv[:, j % 2], psum[j][:]
                    dve.wait_ge(sem("unit_used"), SSM_UNITS * g + (SCU + j + 1))
                    dve.wait_ge(sem("conv_ready"), g * 6 + j + 1)
                    own.mark(dve.tensor_scalar(a, src, w[3], None, ALU.mult))
                    for d in (1, 2, 3):
                        own.settle()
                        ins = dve.scalar_tensor_tensor(out=a[:, d:], in0=src[:, 0:S - d], scalar=w[3 - d], in1=a[:, d:], op0=ALU.mult, op1=ALU.add)
                        if d < 3:
                            own.mark(ins)
                    ins.then_inc(sem("conv_out"), 1)
                hs = bass.ds(g * GH, GH)
                dskip = rows[:, bass.ds(R_D + g * GH, GH)].unsqueeze(2).to_broadcast([P, GH, HEAD])
                dve.wait_ge(sem("x_ready"), g * 4 + 4)
                for c in range(TT):
                    dve.tensor_tensor(heads(y[:, c]), heads(psum[c][:]), dskip, ALU.mult)
                    dve.tensor_tensor(heads(xdt[:, c]), heads(psum[c][:]), dt_sb[:, c, hs].unsqueeze(2).to_broadcast([P, GH, HEAD]),
                                      ALU.mult).then_inc(sem("xdt_ready"), 1)
                dve.wait_ge(sem("cb_done"), g + 1)
                dve.tensor_tensor(cb, psum[5][:].rearrange("p (c l) -> p c l", c=TT), tri_le[:].unsqueeze(1).to_broadcast([P, TT, P]),
                                  ALU.mult).then_inc(sem("cb_ready"), 1)
                dve.wait_ge(sem("cb_ready"), g + 2)
                dve.wait_ge(sem("xdt_ready"), g * 4 + 4)
                for c in range(TT):
                    for k in (2 * c, 2 * c + 1):
                        dve.wait_ge(sem("pair_taken"), pair_at(g, "s", k) + 2)
                        dve.tensor_tensor(mix_m[:, k % 4], decay[:, k % 2], cb[:, c, :].unsqueeze(1).to_broadcast([P, 4, P]),
                                          ALU.mult).then_inc(sem("m_ready"), 1)
                    if c < TT - 1:
                        dve.wait_ge(sem("state_done"), g * 3 + c + 1)
                        if c == 0:
                            dve.tensor_copy(state, psum[5][:]).then_inc(sem("state_ready"), 1)
                        else:
                            dve.wait_ge(sem("off_done"), g * 3 + c)
                            cd = ex_sb[:, 2, c, hs].unsqueeze(2).to_broadcast([P, GH, HEAD])
                            own.mark(dve.tensor_tensor(heads(state), heads(state), cd, ALU.mult))
                            own.settle()
                            dve.tensor_tensor(state, state, psum[5][:], ALU.add).then_inc(sem("state_ready"), 1)
                    dve.wait_ge(sem("diag_done"), g * 4 + c + 1)
                    dve.tensor_tensor(y[:, c], y[:, c], psum[c][:], ALU.add).then_inc(sem("diag_taken"), 1)
                    if c > 0:
                        dve.wait_ge(sem("off_done"), g * 3 + c)
                        dve.wait_ge(sem("yn_ready"), g * 3 + c)
                        ec = ex_sb[:, 0, c, hs].unsqueeze(2).to_broadcast([P, GH, HEAD])
                        dve.tensor_tensor(heads(tmp), heads(psum[4][:]), ec, ALU.mult).then_inc(sem("off_taken"), 1)
                        dve.wait_ge(sem("off_taken"), g * 3 + c + 1)
                        dve.wait_ge(sem("diag_taken"), g * 4 + c + 1 + 4)
                        dve.tensor_tensor(y[:, c], y[:, c], tmp, ALU.add).then_inc(sem("yn_ready"), 1)
                own.end(GROUPS)
            def low_parts(dst, high, src, kn, at_split, gain=None):
                for k in range(kn):
                    dve.wait_ge(sem("split_high"), at_split + k + 1)
                    if gain is None:
                        ins = dve.tensor_tensor(dst[:, k, :], src[:, k, :], high[:, k, :].bitcast(F32), ALU.subtract)
                    else:
                        ins = dve.scalar_tensor_tensor(out=dst[:, k, :], in0=src[:, k, :], scalar=cols[:, gain + k:gain + k + 1],
                                                       in1=high[:, k, :].bitcast(F32), op0=ALU.mult, op1=ALU.subtract)
                    ins.then_inc(sem("split_low"), 1)

            def merge(q, n, used, first=False):
                m = mergedT[:, bass.ds(n, 1), :].rearrange("p o s -> p (o s)")
                dve.wait_ge(sem("unit_used"), used)
                dve.wait_ge(sem("gate_taken"), q + 1)
                dve.memset(waited, 0.0)
                if first:
                    dve.tensor_tensor(m, psum[1][:], sig, ALU.mult).then_inc(sem("merged"), 1)
                else:
                    own.mark(dve.tensor_tensor(sig, psum[1][:], sig, ALU.mult))
                    own.settle()
                    dve.wait_ge(sem("merged"), q)
                    dve.tensor_tensor(m, m, sig, ALU.add).then_inc(sem("merged"), 1)
            low_parts(oL, oH, oT, KT, 0)
            dve.wait_ge(sem("y_gated"), 4 * GROUPS + 4)
            low_parts(gL, gH, gatedT, KT, KT)
            dve.wait_ge(sem("split_low"), 2 * KT)
            with dve.Fori(0, KT) as n:
                own.loop(n, 1)
                merge(2 * n, n, 4 * n + (MGU + 2), first=True)
                merge(2 * n + 1, n, 4 * n + (MGU + 4))
                own.end(KT)
            low_parts(ynL, ynH, ynT, 2 * KT, 2 * KT, gain=C_NG)
            with dve.Fori(0, KT) as n:
                own.loop(n, 1)
                merge(n + 2 * KT, n, 3 * n + (MGU + 4 * KT + 3))
                own.end(KT)
            dve.wait_ge(sem("x_loaded"), 16)
            own.mark(dve.tensor_scalar(weight4, iota_i[:, 0:4], -1.0, 4.0, ALU.mult, ALU.add))
            own.mark(dve.memset(before[:, 0], 0.0))
            for b in range(8):
                c, half = b // 2, b % 2
                dve.wait_ge(sem("mix_done"), b + 1)
                a = x2[:, c, half * 512:(half + 1) * 512]
                own.mark(dve.tensor_tensor(a, a, psum[b][:], ALU.add))
                if half:
                    own.settle()
                    own.mark(dve.tensor_tensor_reduce(sq, x2[:, c, :], x2[:, c, :], 1.0, 0.0, ALU.mult, ALU.add, ms[:, c:c + 1]))
            own.settle()
            dve.tensor_scalar(ms, ms, 1.0 / D, EPS, ALU.mult, ALU.add).then_inc(sem("ms_ready"), 1)
            dve.wait_ge(sem("rstd_ready"), TT + 2)
            for c in range(TT):
                dve.tensor_scalar(h2[:, c, :], x2[:, c, :], rstd[:, c:c + 1], None, ALU.mult).then_inc(sem("h2_ready"), 1)
            def do(ins):
                own.mark(ins)
                own.settle()

            def b4(ap, inner):
                return ap.unsqueeze(len(ap.shape)).to_broadcast(list(ap.shape) + [inner])

            def first_of(out, val, largest, tmp4):
                do(dve.tensor_tensor(tmp4, val, b4(largest, 4), ALU.is_equal))
                do(dve.tensor_tensor(tmp4, tmp4, weight4.unsqueeze(1).to_broadcast([P, TT, 4]), ALU.mult))
                do(dve.tensor_reduce(r1, tmp4, AX_X, ALU.max))
                do(dve.tensor_tensor(out, tmp4, b4(r1, 4), ALU.is_equal))

            def r4(j):
                return rsc[:, j, 0:TT * 4].rearrange("p (c g) -> p c g", c=TT)
            r1, gmax, l1, l2, pg, g1, g2 = (rsc[:, 11 + j, 0:TT] for j in range(7))
            ohg, t4, ing, oh1, oh2, gx, t4b = (r4(j) for j in (3, 4, 5, 6, 7, 1, 8))
            big16 = rsc[:, 18, :].rearrange("p (c j g) -> p c j g", c=TT, j=4)
            dve.wait_ge(sem("routed"), 2)
            dve.tensor_tensor(logits, psum[7][:, 0:TT * NR].rearrange("p (c n) -> p c n", c=TT),
                              rows[:, R_RB:R_RB + NR].unsqueeze(1).to_broadcast([P, TT, NR]), ALU.add).then_inc(sem("logits_out"), 1)
            dve.wait_ge(sem("logits_out"), 1)
            glog = logits[:, :, 0:EG]
            do(dve.tensor_reduce(gmax, glog, AX_X, ALU.max))
            dve.tensor_tensor(gx, glog, b4(gmax, 4), ALU.subtract).then_inc(sem("rt_in"), 1)
            first_of(ohg, glog, gmax, t4)
            do(dve.tensor_tensor(big16, logits[:, :, EG:].rearrange("p c (g j) -> p c j g", j=4),
                                 ohg.unsqueeze(2).to_broadcast([P, TT, 4, 4]), ALU.mult))
            do(dve.tensor_reduce(ing, big16, AX_X, ALU.add))
            do(dve.tensor_reduce(l1, ing, AX_X, ALU.max))
            first_of(oh1, ing, l1, t4)
            do(dve.scalar_tensor_tensor(out=t4b, in0=oh1, scalar=-BIG, in1=ing, op0=ALU.mult, op1=ALU.add))
            do(dve.tensor_reduce(l2, t4b, AX_X, ALU.max))
            first_of(oh2, t4b, l2, t4)
            dve.tensor_tensor(rsc[:, 10, 0:TT], l2, l1, ALU.subtract).then_inc(sem("rt_in"), 1)
            dve.wait_ge(sem("rt_exp"), 2)
            do(dve.tensor_reduce(pg, r4(2), AX_X, ALU.add))
            do(dve.tensor_scalar(g1, rsc[:, 10, 0:TT], 1.0, None, ALU.add))
            do(dve.tensor_tensor(g1, g1, pg, ALU.mult))
            do(dve.reciprocal(g1, g1))
            do(dve.tensor_tensor(g2, g1, rsc[:, 10, 0:TT], ALU.mult))
            for m, oh in ((first, oh1), (second, oh2)):
                own.mark(dve.tensor_tensor(m.rearrange("p c (g j) -> p c g j", j=4), oh.unsqueeze(2).to_broadcast([P, TT, 4, 4]),
                                           b4(ohg, 4), ALU.mult))
            own.settle()
            do(dve.tensor_tensor(chosen, first, second, ALU.add))
            for c in range(TT):
                ins = dve.tensor_tensor(before[:, c + 1], before[:, c], chosen[:, c], ALU.add)
                if c < TT - 1:
                    do(ins)
            ins.then_inc(sem("chosen"), 1)
            dve.wait_ge(sem("iota_ready"), 2)
            own.mark(dve.tensor_copy(iota_row, iota_i[:, 0:P]))
            own.mark(dve.tensor_copy(token_id, iota_i[:, P:]))
            own.settle()
            dve.wait_ge(sem("counted"), 1)
            own.mark(dve.tensor_scalar(place, psum[4][:, 0:TT * EXPERTS].rearrange("p (c e) -> p c e", c=TT), -1.0, None, ALU.add))
            do(dve.tensor_copy(count, psum[4][:, TT * EXPERTS:(TT + 1) * EXPERTS]))
            own.mark(dve.tensor_scalar(ahead, place, float(P), None, ALU.is_ge))
            do(dve.tensor_scalar(extras, count, float(P), None, ALU.is_gt))
            own.mark(dve.tensor_scalar(beyond, ahead, 1.0, None, ALU.mult))
            for j in (2, 3):
                own.mark(dve.scalar_tensor_tensor(out=ahead, in0=place, scalar=float(j * P), in1=ahead, op0=ALU.is_ge, op1=ALU.add))
                do(dve.scalar_tensor_tensor(out=extras, in0=count, scalar=float(j * P), in1=extras, op0=ALU.is_gt, op1=ALU.add))
            do(dve.tensor_tensor_scan(upto, ones[:, 0:EXPERTS], extras, 0.0, ALU.mult, ALU.add))
            own.mark(dve.scalar_tensor_tensor(out=extras, in0=upto, scalar=EXPERTS - 1.0, in1=extras, op0=ALU.add, op1=ALU.subtract))
            own.mark(dve.scalar_tensor_tensor(out=place, in0=ahead, scalar=-float(P), in1=place, op0=ALU.mult, op1=ALU.add))
            own.settle()
            do(dve.tensor_tensor(extras, extras, iota_row[:, 0:EXPERTS], ALU.subtract))

            def over_tokens(ap):
                return ap.unsqueeze(1).to_broadcast([P, TT, EXPERTS])
            do(dve.tensor_tensor(beyond, beyond, over_tokens(extras), ALU.mult))
            do(dve.tensor_tensor(ahead, ahead, beyond, ALU.add))
            do(dve.tensor_tensor(ahead, ahead, over_tokens(iota_row[:, 0:EXPERTS]), ALU.add))
            for j, m in enumerate((first, second)):
                both = rsc[:, 8:10].rearrange("p s (c e) -> p s c e", c=TT)
                do(dve.tensor_tensor(both, m.unsqueeze(1).to_broadcast([P, 2, TT, EXPERTS]),
                                     rsc[:, 20:22].rearrange("p s (c e) -> p s c e", c=TT), ALU.mult))
                do(dve.tensor_reduce(place_tile[:, :, j, :], both, AX_X, ALU.add))
            a8 = [v.rearrange("p m c -> p (m c)") for v in (place_at, tile_at)]
            own.mark(dve.tensor_tensor(tile_hot, iota_row[:, 0:24].unsqueeze(1).to_broadcast([P, 8, 24]),
                                       a8[1].unsqueeze(2).to_broadcast([P, 8, 24]), ALU.is_equal))
            own.settle()
            for j in range(2):
                own.mark(dve.tensor_tensor(tile_hot[:, 4 * j:4 * j + 4, :], tile_hot[:, 4 * j:4 * j + 4, :],
                                           token_id.unsqueeze(2).to_broadcast([P, TT, 24]), ALU.mult))
            own.settle()
            dve.tensor_tensor(one_hot, iota_row.unsqueeze(1).to_broadcast([P, 8, P]), a8[0].unsqueeze(2).to_broadcast([P, 8, P]),
                              ALU.is_equal).then_inc(sem("one_hot_ready"), 1)
            own.mark(dve.scalar_tensor_tensor(out=slot_of[:], in0=tile_at, scalar=float(P), in1=place_at, op0=ALU.mult, op1=ALU.add))
            xe = one_extra
            do(dve.tensor_tensor(xe, upto.unsqueeze(1).to_broadcast([P, EXTRA, EXPERTS]),
                                 iota_row[:, 0:EXTRA].unsqueeze(2).to_broadcast([P, EXTRA, EXPERTS]), ALU.is_le))
            do(dve.tensor_reduce(extra_at[:, 0:EXTRA], xe, AX_X, ALU.add))
            own.mark(dve.tensor_copy(extra_of[:, 0:EXTRA], extra_at[:, 0:EXTRA]))
            own.mark(dve.tensor_copy(extra_of[:, 7:8], upto[:, EXPERTS - 1:EXPERTS]))
            own.settle()
            dve.wait_ge(sem("placed"), 1)
            dve.tensor_copy(token_of[:], psum[5][:, 0:24]).then_inc(sem("planned"), 1)
            for pre in ("e_", "x_"):
                dve.sem_inc(sem(pre + "hgT_ready"), 1)
                dve.sem_inc(sem(pre + "hid_ready"), 1)
            dve.sem_inc(sem("x_hg_turned"), 1)

            def take_tokens(T, u, pre, credit=0):
                dve.wait_ge(sem(pre + "hg_turned"), T + 1 + credit)
                for b in range(2):
                    gain = cols[:, C_G2 + 4 * b:C_G2 + 4 * b + 4].unsqueeze(2).to_broadcast([P, 4, P])
                    ins = dve.tensor_tensor(hgT[:, u, 4 * b:4 * b + 4, :], psum[2 + b][:].rearrange("p (k j) -> p k j", k=4), gain, ALU.mult)
                ins.then_inc(sem(pre + "hgT_ready"), 1)

            def hidden(T, pre):
                dve.wait_ge(sem(pre + "up_done"), T + 1)
                dve.wait_ge(sem(pre + "sg_ready"), T + 2)
                dve.tensor_tensor(hid, sg, psum[1][:], ALU.mult).then_inc(sem(pre + "hid_ready"), 1)
            take_tokens(0, 0, "e_")
            with dve.Fori(0, EXPERTS // 2) as i:
                for u in range(2):
                    hidden(2 * i + u, "e_")
                    take_tokens(2 * i + u + 1, 1 - u, "e_")
            n_extra = dve.value_load(extra_of[0:1, 7:8], min_val=0, max_val=EXTRA)
            with dve.Fori(0, EXTRA) as x:
                with dve.If(x < n_extra):
                    take_tokens(x, 0, "x_", credit=1)
                    hidden(x, "x_")
            def last_norm(c):
                dve.wait_ge(sem("rstd_ready"), TT + 3 + c)
                dve.scalar_tensor_tensor(out=x2[:, c, :], in0=x2[:, c, :], scalar=rstd[:, c:c + 1], in1=final_g,
                                         op0=ALU.mult, op1=ALU.mult).then_inc(sem("out_ready"), 1)

            def mean_square(c):
                dve.wait_ge(sem("x_squared"), c + 1)
                dve.tensor_scalar(ms[:, c:c + 1], ms[:, c:c + 1], 1.0 / D, EPS, ALU.mult, ALU.add).then_inc(sem("ms_ready"), 1)
            dve.wait_ge(sem("router_final_loaded"), 32)
            for c in range(TT):
                dve.wait_ge(sem(f"rows{c}_loaded"), 32)
                own.mark(dve.scalar_tensor_tensor(out=x2[:, c, :], in0=pick[c][:, 0, :], scalar=g1[:, c:c + 1], in1=x2[:, c, :],
                                                  op0=ALU.mult, op1=ALU.add))
                own.settle()
                dve.scalar_tensor_tensor(out=x2[:, c, :], in0=pick[c][:, 1, :], scalar=g2[:, c:c + 1], in1=x2[:, c, :],
                                         op0=ALU.mult, op1=ALU.add).then_inc(sem("rows_added"), 1)
                if c > 0:
                    mean_square(c - 1)
                if c > 1:
                    last_norm(c - 2)
            mean_square(TT - 1)
            last_norm(TT - 2)
            last_norm(TT - 1)


def heads(ap):
    return ap.rearrange("p (h d) -> p h d", d=HEAD)


def relu_tmp(relu, j):
    return relu[:, 0, j * 128:(j + 1) * 128].rearrange("p (t h) -> p t h", t=TT)


def tile_k(w, n=None):
    k, n = w.shape
    return np.ascontiguousarray(w.reshape(k // P, P, n).transpose(1, 0, 2).reshape(P, -1))


def layout(i):
    g = {k: np.asarray(v)[0] for k, v in i.items() if k not in ("x", "final_norm_g")}
    w_in = g["w_in"]
    sizes = [2048, 3072, 32, 1024, 1024, 1024, 384, 256, 64, 8, 1024, 1024, 1024]
    at = np.cumsum([0] + sizes)
    z, xbc, dt, sb_, sc_, sx_, cq, ckv, kix, wix, ga, gb, gc = (w_in[:, at[j]:at[j + 1]] for j in range(len(sizes)))

    def unit(w, row, n):
        return tile_k(w[row * D:row * D + D, n * P:(n + 1) * P])

    a = {}
    a["x"] = np.asarray(i["x"]).reshape(TT, P, D)
    a["w_kv"] = tile_k(np.concatenate([w_in[:, at[7]:at[10]], dt], 1))
    a["w_q"] = tile_k(cq)
    a["w_idx"] = tile_k(g["idx_w_q"].reshape(Q_LORA, -1))
    a["w_sc"] = np.stack([unit(w, 0, n) for n in range(KT) for w in (sb_, sc_, sx_)])
    uq = g["att_w_uq"].reshape(Q_LORA, -1)
    uk = g["att_w_uk"].reshape(4, 4 * HEAD, KV_LORA).transpose(0, 2, 1)
    a["w_qk"] = np.stack([np.concatenate([tile_k(uq[:, j * 256:(j + 1) * 256]), tile_k(uk[j])], 1) for j in range(4)])
    a["w_uv"] = g["att_w_uv"].reshape(4, HQ, RT, P, HEAD).transpose(0, 3, 2, 1, 4).reshape(4, P, -1)
    xs_, b_, c_ = xbc[:, :2048], xbc[:, 2048:2560], xbc[:, 2560:]
    a["w_ssm"] = np.stack([u for q in range(GROUPS) for u in [unit(xs_, 0, 4 * q + j) for j in range(4)] +
                           [unit(b_, 0, q), unit(c_, 0, q)] + [unit(z, 0, 4 * q + j) for j in range(4)]])
    outs = np.concatenate([g["ssm_w_out"], g["sc_w_out"], g["att_w_out"]], 0)
    a["w_units"] = np.stack([u for n in range(KT) for u in (unit(gc, 0, n), unit(outs, 3, n), unit(gb, 0, n), unit(outs, 2, n))] +
                            [u for n in range(KT) for u in (unit(ga, 0, n), unit(outs, 0, n), unit(outs, 1, n))])
    a["w_mix"] = np.concatenate([tile_k(g["mix_w_out"][:, 512 * j:512 * j + 512]).reshape(P, 4, 1024).transpose(1, 0, 2) for j in range(2)])
    a["w_router"] = tile_k(np.concatenate([g["moe_w_group"], g["moe_w_expert"]], 1))
    for n in ("gate", "up"):
        a["w_" + n] = g["moe_w_" + n].reshape(EXPERTS, KT, P, F_EXP).transpose(0, 2, 1, 3).reshape(EXPERTS, P, -1)
    a["w_down"] = g["moe_w_down"].reshape(EXPERTS, FT, P, D).transpose(0, 2, 1, 3).reshape(EXPERTS, P, -1)
    a["final_g"] = np.asarray(i["final_norm_g"])[None]
    conv = np.concatenate([g["ssm_conv_w"], g["ssm_conv_b"][None]], 0)
    ct = conv.reshape(5, 24, P).transpose(2, 1, 0)
    order = [j for q in range(GROUPS) for j in (4 * q, 4 * q + 1, 4 * q + 2, 4 * q + 3, 16 + q, 20 + q)]

    def col(v):
        return v.reshape(-1, P).T
    a["cols"] = np.concatenate([
        col(g["norm1_g"]), col(g["att_q_norm_g"]), np.tile(g["idx_k_norm_g"], 2)[:, None],
        g["sc_conv_w"].reshape(SC_TAPS, KT, P).transpose(2, 1, 0).reshape(P, -1),
        ct[:, order, :].reshape(P, -1), col(g["ssm_norm_g"]), col(g["norm2_g"])], 1)
    a["rows"] = np.concatenate([g["att_kv_norm_g"], g["ssm_dt_bias"], g["ssm_a_log"], g["ssm_d"],
                                g["moe_b_group"], g["moe_b_expert"]])[None]
    assert a["cols"].shape == (P, NCOL) and a["rows"].shape == (1, NROW)
    return {k: np.ascontiguousarray(v) for k, v in a.items()}


def kernel(**inputs):
    import concourse.bacc as bacc
    from concourse.bass_utils import run_bass_kernel_spmd

    nc = bacc.Bacc("TRN2", target_bir_lowering=False, num_devices=1)
    arrays = {"in_" + k: v for k, v in layout(inputs).items()}
    t = {k[3:]: nc.dram_tensor(k, v.shape, mybir.dt.from_np(v.dtype), kind="ExternalInput").ap() for k, v in arrays.items()}
    t["out"] = nc.dram_tensor("out_dram", (TT, P, D), F32, kind="ExternalOutput").ap()
    build(nc, t)
    r = run_bass_kernel_spmd(nc, [arrays], core_ids=[0])
    return r.results[0]["out_dram"].reshape(1, S, D)
```
